# Optimizing a Trainium2 kernel written in Bass

```python
import jax, jax.numpy as jnp
from jax import lax
import numpy as np

D_MODEL = 1024
BATCH = 1
SEQ = 512
DEPTH = 1
DEC_BATCH = 8
DEC_SEQ = 8
PAST_LEN = 4096
PAGE_SIZE = 128

HEAD_DIM = 64
N_RET_HEADS = 8
N_ATT_HEADS = 8
RET_WIDTH = N_RET_HEADS * HEAD_DIM
ATT_WIDTH = N_ATT_HEADS * HEAD_DIM
MIX_WIDTH = RET_WIDTH + ATT_WIDTH
IN_COLS = 4 * RET_WIDTH + 3 * ATT_WIDTH
RET_CHUNK = 128
DIL_PATTERNS = ((128, 1), (512, 4), (2048, 16))
WIN_MAX = 2048
ATT_BLOCK = 128
N_MEM = 256
N_MEM_HEADS = 4
MEM_HEAD_DIM = D_MODEL // N_MEM_HEADS
N_GROUPS = 4
N_EXP_PER_GROUP = 8
N_EXPERTS = N_GROUPS * N_EXP_PER_GROUP
TOP_K_IN_GROUP = 2
D_EXPERT = 256
MOE_TOKEN_BLOCK = 2048
EPS = 1e-6
F32 = jnp.float32

kernel_name = 'hymba_retention_dilated_hmoe_step'

def rmsnorm(x, g):
    x32 = x.astype(F32)
    y = x32 * lax.rsqrt(jnp.mean(x32 * x32, axis=-1, keepdims=True) + EPS)
    return (y * g.astype(F32)).astype(x.dtype)

def retention_log_decay():
    gamma = 1.0 - 2.0 ** (-5.0 - jnp.arange(N_RET_HEADS, dtype=F32))
    return jnp.log(gamma)

def alibi_slopes():
    return 2.0 ** (-8.0 * jnp.arange(1, N_ATT_HEADS + 1, dtype=F32) / N_ATT_HEADS)

def project_mixers(h, w_in, g_q_att, g_k_att):
    B, L, _ = h.shape
    z = h @ w_in
    cuts = [RET_WIDTH, 2 * RET_WIDTH, 3 * RET_WIDTH, 4 * RET_WIDTH,
            4 * RET_WIDTH + ATT_WIDTH, 4 * RET_WIDTH + 2 * ATT_WIDTH]
    q_r, k_r, v_r, g_r, q_a, k_a, v_a = jnp.split(z, cuts, axis=-1)
    heads = lambda t: t.reshape(B, L, -1, HEAD_DIM)
    return (heads(q_r), heads(k_r), heads(v_r), g_r,
            rmsnorm(heads(q_a), g_q_att), rmsnorm(heads(k_a), g_k_att), heads(v_a))

def retention(q, k, v, s0):
    B, L, H, Dh = q.shape
    C = RET_CHUNK if L % RET_CHUNK == 0 else L
    n = L // C
    lg = retention_log_decay()
    qc = q.astype(F32).reshape(B, n, C, H, Dh)
    kc = (k.astype(F32) * (Dh ** -0.5)).reshape(B, n, C, H, Dh)
    vc = v.astype(F32).reshape(B, n, C, H, Dh)
    i = jnp.arange(C, dtype=F32)
    rel = i[:, None] - i[None, :]
    dmat = jnp.where(rel >= 0, jnp.exp(lg[:, None, None] * jnp.maximum(rel, 0.0)), 0.0)
    s = jnp.einsum('bnihd,bnjhd->bnhij', qc, kc) * dmat
    o_in = jnp.einsum('bnhij,bnjhe->bnihe', s, vc)
    w_k = jnp.exp(lg[:, None] * (C - 1.0 - i)[None, :])
    kv = jnp.einsum('bnjhd,bnjhe,hj->nbhde', kc, vc, w_k)
    g_chunk = jnp.exp(lg * C)[None, :, None, None]

    def step(state, kv_c):
        return g_chunk * state + kv_c, state

    s_fin, s_prev = lax.scan(step, s0.astype(F32), kv)
    w_q = jnp.exp(lg[None, :] * (i + 1.0)[:, None])
    o_x = jnp.einsum('bnihd,nbhde->bnihe', qc, s_prev) * w_q[None, None, :, :, None]
    return (o_in + o_x).reshape(B, L, H, Dh), s_fin

def head_groupnorm(o, g):
    B, L, H, Dh = o.shape
    c = o - jnp.mean(o, axis=-1, keepdims=True)
    y = c * lax.rsqrt(jnp.mean(c * c, axis=-1, keepdims=True) + EPS)
    return y.reshape(B, L, H * Dh) * g.astype(F32)

def dilated_attn_strided(q, k, v, window, dil):
    B, S, H, Dh = q.shape
    n_off = window // dil
    L = S // dil
    nb = -(-L // ATT_BLOCK)
    Lp = nb * ATT_BLOCK

    def split(t):
        t = jnp.moveaxis(t.reshape(B, L, dil, H, Dh), 2, 1)
        t = jnp.pad(t, ((0, 0), (0, 0), (0, Lp - L), (0, 0), (0, 0)))
        return t.reshape(B, dil, nb, ATT_BLOCK, H, Dh)

    def with_prev(t):
        prev = jnp.concatenate([jnp.zeros_like(t[:, :, :1]), t[:, :, :-1]], axis=2)
        return jnp.concatenate([prev, t], axis=3)

    qb = split(q)
    kk = with_prev(split(k))
    vv = with_prev(split(v))
    i = jnp.arange(ATT_BLOCK)
    j = jnp.arange(2 * ATT_BLOCK)
    rel = ATT_BLOCK + i[:, None] - j[None, :]
    kpos = jnp.arange(nb)[:, None] * ATT_BLOCK - ATT_BLOCK + j[None, :]
    valid = (rel >= 0) & (rel <= n_off) & (kpos[:, None, :] >= 0)
    s = jnp.einsum('bgnihd,bgnjhd->bgnhij', qb, kk).astype(F32) * (Dh ** -0.5)
    s = s - alibi_slopes()[:, None, None] * (rel * dil).astype(F32)
    s = jnp.where(valid[:, None], s, -jnp.inf)
    m = jnp.max(s, axis=-1)
    p = jnp.exp(s - m[..., None])
    l = jnp.sum(p, axis=-1)
    o = jnp.einsum('bgnhij,bgnjhd->bgnihd', p, vv.astype(F32)) / jnp.swapaxes(l, 3, 4)[..., None]

    def unsplit(t):
        t = t.reshape((B, dil, Lp) + t.shape[4:])[:, :, :L]
        return jnp.moveaxis(t, 1, 2).reshape((B, S) + t.shape[3:])

    return unsplit(o), unsplit(jnp.swapaxes(m, 3, 4)), unsplit(jnp.swapaxes(l, 3, 4))

def dilated_attn_gather(q, k_ext, v_ext, window, dil):
    B, L, H, Dh = q.shape
    P = k_ext.shape[1] - L
    n = jnp.arange(window // dil + 1)
    idx = P + jnp.arange(L)[:, None] - dil * n[None, :]
    valid = idx >= 0
    idx = jnp.maximum(idx, 0)
    kg = k_ext[:, idx]
    vg = v_ext[:, idx]
    s = jnp.einsum('bihd,binhd->bhin', q, kg).astype(F32) * (Dh ** -0.5)
    s = s - alibi_slopes()[:, None, None] * (dil * n).astype(F32)
    s = jnp.where(valid, s, -jnp.inf)
    m = jnp.max(s, axis=-1)
    p = jnp.exp(s - m[..., None])
    l = jnp.sum(p, axis=-1)
    o = jnp.einsum('bhin,binhd->bihd', p, vg.astype(F32)) / jnp.swapaxes(l, 1, 2)[..., None]
    return o, jnp.swapaxes(m, 1, 2), jnp.swapaxes(l, 1, 2)

def combine_dilation_groups(outs):
    o_all = jnp.stack([o for o, _, _ in outs])
    m_all = jnp.stack([m for _, m, _ in outs])
    l_all = jnp.stack([l for _, _, l in outs])
    w = l_all * jnp.exp(m_all - jnp.max(m_all, axis=0, keepdims=True))
    return jnp.sum(w[..., None] * o_all, axis=0) / jnp.sum(w, axis=0)[..., None]

def mixer_output(o_r, g_r, o_a, g_ret_out, w_o, dtype):
    B, L = o_r.shape[:2]
    r = head_groupnorm(o_r, g_ret_out) * jax.nn.silu(g_r.astype(F32))
    a = o_a.reshape(B, L, ATT_WIDTH)
    return jnp.concatenate([r, a], axis=-1).astype(dtype) @ w_o

def memory_kv(mem, g_mem, w_mk, w_mv, g_k_mem):
    B, M, _ = mem.shape
    h = rmsnorm(mem, g_mem)
    k = rmsnorm((h @ w_mk).reshape(B, M, N_MEM_HEADS, MEM_HEAD_DIM), g_k_mem)
    v = (h @ w_mv).reshape(B, M, N_MEM_HEADS, MEM_HEAD_DIM)
    return k, v

def memory_attend(h, mk, mv, w_mq, g_q_mem, w_mo):
    B, L, _ = h.shape
    q = rmsnorm((h @ w_mq).reshape(B, L, N_MEM_HEADS, MEM_HEAD_DIM), g_q_mem)
    s = jnp.einsum('blhd,bmhd->bhlm', q, mk).astype(F32) * (MEM_HEAD_DIM ** -0.5)
    p = jax.nn.softmax(s, axis=-1)
    o = jnp.einsum('bhlm,bmhd->blhd', p, mv.astype(F32)).reshape(B, L, D_MODEL)
    return o.astype(h.dtype) @ w_mo

def hier_moe(h, w_rg, b_rg, w_re, b_re, w_eg, w_eu, w_ed):
    B, L, D = h.shape
    T = B * L
    blk = min(MOE_TOKEN_BLOCK, T)
    nblk = -(-T // blk)
    t_all = jnp.pad(h.reshape(T, D), ((0, nblk * blk - T), (0, 0))).reshape(nblk, blk, D)

    def one_block(t):
        lg = (t @ w_rg).astype(F32) + b_rg.astype(F32)
        pg = jax.nn.softmax(lg, axis=-1)
        oh_g = jax.nn.one_hot(jnp.argmax(lg, axis=-1), N_GROUPS, dtype=F32)
        p_top = jnp.sum(pg * oh_g, axis=-1)
        le = jnp.einsum('td,gde->tge', t, w_re).astype(F32) + b_re.astype(F32)
        le_sel = jnp.einsum('tge,tg->te', le, oh_g)
        top_v, top_i = lax.top_k(le_sel, TOP_K_IN_GROUP)
        w2 = jax.nn.softmax(top_v, axis=-1) * p_top[:, None]
        in_group = jnp.sum(jax.nn.one_hot(top_i, N_EXP_PER_GROUP, dtype=F32) * w2[..., None], axis=1)
        gate = (oh_g[:, :, None] * in_group[:, None, :]).reshape(-1, N_EXPERTS)
        hid = jax.nn.silu(jnp.einsum('td,edf->tef', t, w_eg)) * jnp.einsum('td,edf->tef', t, w_eu)
        return jnp.einsum('tef,efd->td', hid * gate[..., None].astype(hid.dtype), w_ed)

    y = lax.map(one_block, t_all).reshape(nblk * blk, D)[:T]
    return y.reshape(B, L, D).astype(h.dtype)

def setup_inputs(seed: int = 0) -> dict:
    key = jax.random.key(seed)
    k = jax.random.split(key, 32)
    nrm = lambda i, shape, scale: jax.random.normal(k[i], shape, F32) * scale
    gain = lambda i, shape: 1.0 + 0.05 * jax.random.normal(k[i], shape, F32)
    w_buf = min(WIN_MAX, PAST_LEN)
    Dm = D_MODEL
    return {
        'x_prompt': nrm(0, (BATCH, SEQ, Dm), 1.0),
        'x_sample': nrm(1, (DEC_BATCH, DEC_SEQ, Dm), 1.0),
        'mem_prompt': nrm(2, (BATCH, N_MEM, Dm), 1.0),
        'state_ret': nrm(3, (DEPTH, DEC_BATCH, N_RET_HEADS, HEAD_DIM, HEAD_DIM), 0.5),
        'cache_win_k': nrm(4, (DEPTH, DEC_BATCH, w_buf, N_ATT_HEADS, HEAD_DIM), 1.0),
        'cache_win_v': nrm(5, (DEPTH, DEC_BATCH, w_buf, N_ATT_HEADS, HEAD_DIM), 1.0),
        'cache_mem_k': nrm(6, (DEPTH, DEC_BATCH, N_MEM, N_MEM_HEADS, MEM_HEAD_DIM), 1.0),
        'cache_mem_v': nrm(7, (DEPTH, DEC_BATCH, N_MEM, N_MEM_HEADS, MEM_HEAD_DIM), 1.0),
        'g_mix': gain(8, (DEPTH, Dm)),
        'w_in': nrm(9, (DEPTH, Dm, IN_COLS), Dm ** -0.5),
        'g_ret_out': gain(10, (DEPTH, RET_WIDTH)),
        'g_q_att': gain(11, (DEPTH, HEAD_DIM)),
        'g_k_att': gain(12, (DEPTH, HEAD_DIM)),
        'w_o': nrm(13, (DEPTH, MIX_WIDTH, Dm), MIX_WIDTH ** -0.5),
        'g_cross': gain(14, (DEPTH, Dm)),
        'g_mem': gain(15, (DEPTH, Dm)),
        'w_mq': nrm(16, (DEPTH, Dm, Dm), Dm ** -0.5),
        'w_mk': nrm(17, (DEPTH, Dm, Dm), Dm ** -0.5),
        'w_mv': nrm(18, (DEPTH, Dm, Dm), Dm ** -0.5),
        'g_q_mem': gain(19, (DEPTH, MEM_HEAD_DIM)),
        'g_k_mem': gain(20, (DEPTH, MEM_HEAD_DIM)),
        'w_mo': nrm(21, (DEPTH, Dm, Dm), Dm ** -0.5),
        'g_moe': gain(22, (DEPTH, Dm)),
        'w_router_group': nrm(23, (DEPTH, Dm, N_GROUPS), Dm ** -0.5),
        'b_router_group': nrm(24, (DEPTH, N_GROUPS), 0.01),
        'w_router_expert': nrm(25, (DEPTH, N_GROUPS, Dm, N_EXP_PER_GROUP), Dm ** -0.5),
        'b_router_expert': nrm(26, (DEPTH, N_GROUPS, N_EXP_PER_GROUP), 0.01),
        'w_exp_gate': nrm(27, (DEPTH, N_EXPERTS, Dm, D_EXPERT), Dm ** -0.5),
        'w_exp_up': nrm(28, (DEPTH, N_EXPERTS, Dm, D_EXPERT), Dm ** -0.5),
        'w_exp_down': nrm(29, (DEPTH, N_EXPERTS, D_EXPERT, Dm), D_EXPERT ** -0.5),
    }

def reference(x_prompt, x_sample, mem_prompt, state_ret, cache_win_k, cache_win_v,
              cache_mem_k, cache_mem_v, g_mix, w_in, g_ret_out, g_q_att, g_k_att, w_o,
              g_cross, g_mem, w_mq, w_mk, w_mv, g_q_mem, g_k_mem, w_mo, g_moe,
              w_router_group, b_router_group, w_router_expert, b_router_expert,
              w_exp_gate, w_exp_up, w_exp_down):
    yp, ys = x_prompt, x_sample
    S = x_prompt.shape[1]
    w_keep = min(WIN_MAX, S)
    p_ret, p_wk, p_wv, p_mk, p_mv, s_ret, s_wk, s_wv = [], [], [], [], [], [], [], []
    for l in range(DEPTH):
        q_r, k_r, v_r, g_r, q_a, k_a, v_a = project_mixers(rmsnorm(yp, g_mix[l]), w_in[l], g_q_att[l], g_k_att[l])
        s0 = jnp.zeros((yp.shape[0], N_RET_HEADS, HEAD_DIM, HEAD_DIM), F32)
        o_r, r_fin = retention(q_r, k_r, v_r, s0)
        o_a = combine_dilation_groups([dilated_attn_strided(q_a, k_a, v_a, w, d) for (w, d) in DIL_PATTERNS])
        yp = yp + mixer_output(o_r, g_r, o_a, g_ret_out[l], w_o[l], yp.dtype)
        mk, mv = memory_kv(mem_prompt, g_mem[l], w_mk[l], w_mv[l], g_k_mem[l])
        yp = yp + memory_attend(rmsnorm(yp, g_cross[l]), mk, mv, w_mq[l], g_q_mem[l], w_mo[l])
        yp = yp + hier_moe(rmsnorm(yp, g_moe[l]), w_router_group[l], b_router_group[l],
                           w_router_expert[l], b_router_expert[l], w_exp_gate[l], w_exp_up[l], w_exp_down[l])
        p_ret.append(r_fin)
        p_wk.append(k_a[:, S - w_keep:])
        p_wv.append(v_a[:, S - w_keep:])
        p_mk.append(mk)
        p_mv.append(mv)
        q_r, k_r, v_r, g_r, q_a, k_a, v_a = project_mixers(rmsnorm(ys, g_mix[l]), w_in[l], g_q_att[l], g_k_att[l])
        o_r, r_fin = retention(q_r, k_r, v_r, state_ret[l])
        k_ext = jnp.concatenate([cache_win_k[l].astype(k_a.dtype), k_a], axis=1)
        v_ext = jnp.concatenate([cache_win_v[l].astype(v_a.dtype), v_a], axis=1)
        o_a = combine_dilation_groups([dilated_attn_gather(q_a, k_ext, v_ext, w, d) for (w, d) in DIL_PATTERNS])
        ys = ys + mixer_output(o_r, g_r, o_a, g_ret_out[l], w_o[l], ys.dtype)
        ys = ys + memory_attend(rmsnorm(ys, g_cross[l]), cache_mem_k[l], cache_mem_v[l], w_mq[l], g_q_mem[l], w_mo[l])
        ys = ys + hier_moe(rmsnorm(ys, g_moe[l]), w_router_group[l], b_router_group[l],
                           w_router_expert[l], b_router_expert[l], w_exp_gate[l], w_exp_up[l], w_exp_down[l])
        s_ret.append(r_fin.astype(state_ret.dtype))
        s_wk.append(k_a)
        s_wv.append(v_a)
    return (yp, ys, jnp.stack(p_ret), jnp.stack(p_wk), jnp.stack(p_wv), jnp.stack(p_mk), jnp.stack(p_mv),
            jnp.stack(s_ret), jnp.stack(s_wk), jnp.stack(s_wv))


_drawn_inputs = setup_inputs


def setup_inputs(seed=0):
    import zlib

    import numpy as np

    out = dict(_drawn_inputs(seed))
    spreads = {}
    factors = {'g_q_att': 3.363,
     'g_cross': 3.306,
     'g_q_mem': 3.314,
     'b_router_group': 4.875,
     'b_router_expert': 4.251}
    for name, (base, spread) in spreads.items():
        noise = np.random.default_rng([zlib.crc32(name.encode()), seed]).standard_normal(out[name].shape)
        drawn = base * np.exp(spread * noise) if base else spread * noise
        out[name] = __import__('jax').numpy.asarray(drawn.astype(out[name].dtype))
    for name, factor in factors.items():
        out[name] = (out[name] * factor).astype(out[name].dtype)
    return out
```

```python
from contextlib import ExitStack

import numpy as np

import concourse.bass as bass
from concourse import mybir

F32 = mybir.dt.float32
F32R = mybir.dt.float32r
I32 = mybir.dt.int32
U32 = mybir.dt.uint32
ALU = mybir.AluOpType
ACT = mybir.ActivationFunctionType
AX = mybir.AxisListType

P = 128
D = 1024
C8 = D // P
SEQ = 512
NB, LS = 8, 8
NS = NB * LS
T = SEQ + NS
TP = SEQ + P
NT = 5
H, HD = 8, 64
NP = H // 2
RW = H * HD
PAST, WBUF = 4096, 2048
PATTERNS = ((128, 1), (512, 4), (2048, 16))
NEAR = 512
FAR = (WBUF - NEAR) // 16 * LS
KC = (FAR + NEAR) // P
FC = FAR // P
WK = KC * P + NS
MEM, MH, MD = 256, 4, 256
NG, EPG, NE, FE = 4, 8, 32, 256
SLOT = 64
OV = 18
NPAIR, NOVP = NE // 2, OV // 2
NPT = NPAIR + NOVP
EPS = 1e-6
NEG = -1e30


def rows(t):
    return P if t < NT - 1 else NS


def tcol(t):
    return slice(t * P, t * P + rows(t))


class Chain:

    def __init__(self, eng, sem, start=0):
        self.eng, self.sem, self.n = eng, sem, start

    def __call__(self, ins):
        self.n += 1
        ins.then_inc(self.sem, 1)
        self.eng.wait_ge(self.sem, self.n)


class Plan:

    X, HT, HTH, Z, W, WH, SMALL, END = 0, 5120, 10240, 15360, 33280, 41472, 49664, 53200

    def __init__(self, nc, ctx):
        self.nc, self.ctx = nc, ctx
        self.base = 16512
        self.open = []
        self.small = self.SMALL
        self.bank = [ctx.enter_context(nc.psum_tensor(f"bank{i}", [P, 512], F32)) for i in range(8)]
        self.x = self.at("x", self.X, [NT, D])
        self.ht = self.at("ht", self.HT, [C8, TP])

    def at(self, name, word, shape, dt=F32):
        n = int(np.prod(shape))
        assert word + n <= self.END, (name, word, n)
        return self.nc.alloc_sbuf_tensor_at(name, [P, *shape], dt, offset=self.base + 4 * word)

    def keep(self, name, shape, dt=F32):
        t = self.at(name, self.small, shape, dt)
        self.small += (int(np.prod(shape)) + 7) // 8 * 8
        return t

    def sem(self, name):
        self.open.append(self.nc.alloc_semaphore(name=name))
        return self.open[-1]

    def free_sems(self):
        self.nc.clear_and_free_semaphores(self.open)
        self.nc.all_engine_barrier()
        self.open = []


def over(ap, n):
    k = len(ap.shape)
    return ap.unsqueeze(k).to_broadcast([*ap.shape, n])


def across(ap, at, n):
    s = list(ap.shape)
    return ap.unsqueeze(at).to_broadcast(s[:at] + [n] + s[at:])


def dense(nc, m, name, src, blocks, tiles, gain, store, hooks={}, xtiles=None, extra=None):
    nt = len(tiles)
    hth = m.at(f"{name}_hth", m.HTH, [C8, TP], F32R)
    htl = m.at(f"{name}_htl", m.HT, [C8, TP], F32R)
    w = [m.at(f"{name}_w{i}", m.W + 4096 * i, [C8, 512]) for i in range(2)]
    wl = [m.at(f"{name}_wl{i}", m.W + 4096 * i, [C8, 512], F32R) for i in range(2)]
    wh = [m.at(f"{name}_wh{i}", m.WH + 4096 * i, [C8, 512], F32R) for i in range(2)]
    s = lambda n: m.sem(f"{name}_{n}")
    loaded = [s("w_loaded0"), s("w_loaded1")]
    sq_done, var_done, rstd_done, xs_done = s("sq_done"), s("var_done"), s("rstd_done"), s("xs_done")
    turned, ht_done, hth_done, htl_done = s("turned"), s("ht_done"), s("hth_done"), s("htl_done")
    padded = s("padded")
    wh_done, wl_done, mm_done, stored = s("wh_done"), s("wl_done"), s("mm_done"), s("stored")
    nb = len(blocks)
    wcols = nt * P

    with nc.Block() as block:
        @block.sync
        def _(sp):
            for b in range(nb):
                if b >= 2:
                    sp.wait_ge(mm_done, (b - 1) * nt)
                sp.dma_start(w[b % 2][:], blocks[b]).then_inc(loaded[b % 2], 16)

        @block.gpsimd
        def _(pool):
            if src is not None:
                for n, t in enumerate(tiles):
                    r = xtiles[n]
                    pool.wait_ge(sq_done, n + 1)
                    pool.tensor_scalar(m.stat[:r, 8 + n:9 + n], m.stat[:r, n:n + 1], 1.0 / D, EPS,
                                       ALU.mult, ALU.add).then_inc(var_done, 1)
                    pool.wait_ge(var_done, n + 1)
                    pool.tensor_tensor(m.stat[:r, 16 + n:17 + n], m.stat[:r, 8 + n:9 + n],
                                       m.neghalf[:r, 0:1], ALU.pow).then_inc(rstd_done, 1)
            if "gpsimd" in hooks:
                hooks["gpsimd"](pool)

        def split_ht_hi(act):
            if src is not None:
                act.wait_ge(ht_done, 2 * nt)
            elif nt == NT:
                act.wait_ge(padded, 1)
            act.activation(hth[:, :, :wcols], m.ht[:, :, :wcols], ACT.Copy).then_inc(hth_done, 1)

        @block.scalar
        def _(act):
            def split_w(b):
                act.wait_ge(loaded[b % 2], 16 * (b // 2 + 1))
                if b >= 2:
                    act.wait_ge(mm_done, (b - 1) * nt)
                act.activation(wh[b % 2][:], w[b % 2][:], ACT.Copy).then_inc(wh_done, 1)

            if src is not None:
                for n, t in enumerate(tiles):
                    r = xtiles[n]
                    if n >= 2:
                        act.wait_ge(turned, 2 * (n - 1))
                    act.activation(m.junk[n % 2][:r, :], src[:r, n, :], ACT.Square,
                                   accum_out=m.stat[:r, n:n + 1]).then_inc(sq_done, 1)
                    act.wait_ge(rstd_done, n + 1)
                    act.activation(m.junk[n % 2][:r, :], src[:r, n, :], ACT.Copy,
                                   scale=m.stat[:r, 16 + n:17 + n]).then_inc(xs_done, 1)
            split_ht_hi(act)
            split_w(0)
            for b in range(nb):
                if b + 1 < nb:
                    split_w(b + 1)
                for n, t in enumerate(tiles):
                    k = b * nt + n
                    act.wait_ge(mm_done, k + 1)
                    store(act, m.bank[k % 2], b, n).then_inc(stored, 1)
                    if "scalar" in hooks:
                        hooks["scalar"](act, b, n, stored, k)

        @block.vector
        def _(dve):
            if nt == NT:
                dve.memset(m.ht[:, :, T:TP], 0.0).then_inc(padded, 1)
                dve.wait_ge(padded, 1)
            if src is not None:
                for n, t in enumerate(tiles):
                    r = xtiles[n]
                    for j in range(2):
                        dve.wait_ge(turned, 2 * n + j + 1)
                        dve.tensor_tensor(m.ht[:, 4 * j:4 * j + 4, t * P:t * P + r],
                                          m.bank[4 + j][:].rearrange("p (c n) -> p c n", c=4)[:, :, :r],
                                          over(gain[:, 4 * j:4 * j + 4], r), ALU.mult).then_inc(ht_done, 1)
            if extra is not None:
                extra["vector"](dve, ht_done)
            dve.wait_ge(hth_done, 1)
            dve.tensor_tensor(htl[:, :, :wcols], m.ht[:, :, :wcols], hth[:, :, :wcols].bitcast(F32),
                              ALU.subtract).then_inc(htl_done, 1)

            def split_w(b):
                dve.wait_ge(wh_done, b + 1)
                dve.tensor_tensor(wl[b % 2][:], w[b % 2][:], wh[b % 2][:].bitcast(F32),
                                  ALU.subtract).then_inc(wl_done, 1)

            split_w(0)
            for b in range(nb):
                if b + 1 < nb:
                    split_w(b + 1)
                if "vector" in hooks:
                    for n in range(nt):
                        hooks["vector"](dve, b, n, stored, b * nt + n)

        @block.tensor
        def _(pe):
            if src is not None:
                for n, t in enumerate(tiles):
                    r = xtiles[n]
                    pe.wait_ge(xs_done, n + 1)
                    for j in range(2):
                        if n:
                            pe.wait_ge(ht_done, 2 * n - 1 + j)
                        for c in range(4):
                            last = pe.transpose(m.bank[4 + j][:, c * P:c * P + r],
                                                m.junk[n % 2][:r, :].rearrange("n (p c) -> n c p", c=C8)[:, 4 * j + c, :],
                                                m.ident[:r, :r])
                        last.then_inc(turned, 1)
            pe.wait_ge(hth_done, 1)
            pe.wait_ge(htl_done, 1)
            if extra is not None:
                extra["tensor"](pe)
            for b in range(nb):
                pe.wait_ge(wh_done, b + 1)
                pe.wait_ge(wl_done, b + 1)
                for n, t in enumerate(tiles):
                    k = b * nt + n
                    if k >= 2:
                        pe.wait_ge(stored, k - 1)
                    for c in range(C8):
                        hi, lo = hth[:, c, t * P:(t + 1) * P], htl[:, c, t * P:(t + 1) * P]
                        pe.matmul(m.bank[k % 2][:], hi, wh[b % 2][:, c, :], start=(c == 0), stop=False)
                        pe.matmul(m.bank[k % 2][:], hi, wl[b % 2][:, c, :], start=False, stop=False)
                        last = pe.matmul(m.bank[k % 2][:], lo, wh[b % 2][:, c, :], start=False,
                                         stop=(c == C8 - 1))
                    last.then_inc(mm_done, 1)


def load_constants(nc, m, a):
    with nc.Block() as block:
        loads = m.sem("constants_loaded")
        rows_in = m.sem("rows_loaded")
        zeroed = m.sem("zeroed")

        @block.sync
        def _(sp):
            xp = a["x_prompt"].rearrange("a (t p) d -> p (a t) d", p=P)
            for t in range(NT - 1):
                sp.dma_start(m.x[:, t, :], xp[:, t, :]).then_inc(rows_in, 16)
            sp.dma_start(m.x[:NS, NT - 1, :], a["x_sample"].rearrange("b i d -> (b i) d")).then_inc(rows_in, 16)
            sp.wait_ge(rows_in, 16 * NT)

        @block.scalar
        def _(act):
            n = 0
            for dst, src in m.constant_loads:
                act.dma_start(dst, src).then_inc(loads, 16)
                n += 16
            act.wait_ge(loads, n)

        @block.vector
        def _(dve):
            dve.memset(m.neghalf[:], -0.5).then_inc(zeroed, 1)


def project_in(nc, m, a):
    order = [4, 5, 3, 0, 1, 2, 6]
    w = a["w_in"].rearrange("a (p c) n -> p (a c) n", p=P)
    blocks = [w[:, :, 512 * j:512 * j + 512] for j in order]
    squared, reduced, rstd = m.sem("qk_squared"), m.sem("qk_reduced"), m.sem("qk_rstd")
    exped, gated, chain_s = m.sem("gate_exped"), m.sem("gate_gated"), m.sem("in_dve_chain")
    varied = m.sem("qk_varied")
    sq = [m.scr[:, 0:512], m.scr[:, 512:1024]]

    def store(act, bank, b, t):
        return act.activation(m.z[b][:rows(t), t, :], bank[:rows(t), :], ACT.Copy)

    def scalar(act, b, t, stored, k):
        r = rows(t)
        if b < 2:
            if k >= 2:
                act.wait_ge(reduced, k - 1)
            act.wait_ge(stored, k + 1)
            act.activation(sq[k % 2][:r, :], m.z[b][:r, t, :], ACT.Square).then_inc(squared, 1)
        elif b == 2:
            if k - 2 < 2 * NT:
                act.wait_ge(reduced, 2 * NT)
            else:
                act.wait_ge(gated, k - 2 * NT - 1)
            act.wait_ge(stored, k + 1)
            act.activation(sq[k % 2][:r, :], m.z[2][:r, t, :], ACT.Exp, scale=-1.0).then_inc(exped, 1)

    chain = []

    def vector(dve, b, t, stored, k):
        if not chain:
            chain.append(Chain(dve, chain_s))
        link, r = chain[0], rows(t)
        heads = lambda ap: ap.rearrange("p (h d) -> p h d", h=H)
        z = m.z[b][:r, t, :]
        if b < 2:
            dve.wait_ge(squared, k + 1)
            dve.tensor_reduce(m.qms[:r, 8 * k:8 * k + 8], heads(sq[k % 2][:r, :]), AX.X, ALU.add).then_inc(reduced, 1)
            dve.wait_ge(rstd, k + 1)
            link(dve.tensor_tensor(heads(z), heads(z), over(m.qrs[:r, 8 * k:8 * k + 8], HD), ALU.mult))
            link(dve.tensor_tensor(heads(z), heads(z), across(m.g_qk[b][:r, :], 1, H), ALU.mult))
        elif b == 2:
            e = sq[k % 2][:r, :]
            dve.wait_ge(exped, k - 2 * NT + 1)
            link(dve.tensor_scalar(e, e, 1.0, None, ALU.add))
            link(dve.reciprocal(e, e))
            link(dve.tensor_tensor(e, e, m.g_ret[:r, :], ALU.mult))
            dve.tensor_tensor(z, z, e, ALU.mult).then_inc(gated, 1)
            dve.wait_ge(gated, k - 2 * NT + 1)

    def gpsimd(pool):
        for k in range(2 * NT):
            r = rows(k % NT)
            c = slice(8 * k, 8 * k + 8)
            pool.wait_ge(reduced, k + 1)
            pool.tensor_scalar(m.qrs[:r, c], m.qms[:r, c], 1.0 / HD, EPS, ALU.mult, ALU.add).then_inc(varied, 1)
            pool.wait_ge(varied, k + 1)
            pool.tensor_tensor(m.qrs[:r, c], m.qrs[:r, c], m.neghalf[:r, 0:8], ALU.pow).then_inc(rstd, 1)

    dense(nc, m, "in", m.x, blocks, range(NT), m.g_mix, store,
          {"scalar": scalar, "vector": vector, "gpsimd": gpsimd}, [rows(t) for t in range(NT)])


def mix_prompt(nc, m, a):
    QA, KA, GR, QR, KR, VR, VA = range(7)
    tr = [m.at(n, m.W + i * NP * T, [NP, T]) for i, n in enumerate(("qr_t", "kr_t", "qa_t", "ka_t"))]
    qr_t, kr_t, qa_t, ka_t = tr
    m.qa_t, m.ka_t = qa_t, ka_t
    w0 = m.W + 4 * NP * T
    tab = m.at("tab", w0, [H, 512])
    dm = m.at("dm", w0 + 4096, [H, P])
    sb = [m.at(f"scored{i}", w0 + 5120 + 512 * i, [512]) for i in range(2)]
    pt = [m.at(f"probs_t{i}", w0 + 6144 + 512 * i, [512]) for i in range(2)]
    h0 = m.HTH
    pb = [m.at(f"probs{i}", h0 + 512 * i, [512]) for i in range(2)]
    sd = m.at("decayed", h0 + 1024, [H, P])
    qw = m.at("q_weighted", h0 + 2048, [NP, P])
    kw = m.at("k_weighted", h0 + 2560, [RW])
    cc = m.at("centred", h0 + 3072, [RW])
    sq = m.at("centred_sq", h0 + 3584, [RW])
    ot = [m.at(f"out_rows{i}", h0 + 4096 + 512 * i, [RW]) for i in range(2)]
    s0 = m.at("state_in", m.Z, [NP, NB * HD])
    vx = [m.at(f"v_spread{i}", m.Z + 2560 * i + 2048, [NB * HD]) for i in range(2)]
    s1 = m.at("state_out", m.Z + 2560, [NP, NB * HD])
    z3 = m.Z + QR * 2560
    dms = m.at("dms", z3, [H, NS])
    qws = m.at("qs_weighted", z3 + 512, [NP, NS])
    ots = m.at("os_t", z3 + 768, [NP, NS])
    wq, wqs = m.scr[:, 0:512], m.scr[:, 512:768]
    st = m.state
    z = m.z
    S = m.sem
    tabs_in, dms_in, state_in = S("tabs_in"), S("dms_in"), S("state_in")
    tr_done, tev = S("tr_done"), [S("tr_stored_even"), S("tr_stored_odd")]
    sc_done, sd_done, qw_done, kw_done = S("ret_scored"), S("ret_decayed"), S("q_weighted"), S("k_weighted")
    o_done, kv_done, st_done, gn_c = S("ret_out"), S("kv_out"), S("state_done"), S("gn_centred")
    gn_sq, gn_red, gn_var, gn_rstd = S("gn_squared"), S("gn_reduced"), S("gn_varied"), S("gn_rstd")
    out_ready, out_turned, out_stored = S("out_ready"), S("out_turned"), S("out_stored")
    vx_done, kvs_done, ots_done, os_done = S("v_spread"), S("kvs_out"), S("os_t_stored"), S("os_turned")
    osT_done = S("os_t_done")
    s1_done = S("state_out_done")
    as_done, sb_done, mx_done, ex_done = S("att_scored"), S("att_biased"), S("att_max"), S("att_exped")
    pt_done, pt_ev, pv_done = S("probs_turned"), S("probs_t_stored"), S("pv_done")
    stores = S("mix_stores")
    ch = S("mix_dve_chain")
    hv = lambda ap, h=H: ap.rearrange("p (h d) -> p h d", h=h)
    AT = [(qb, h) for qb in range(SEQ // P) for h in range(H)]

    with nc.Block() as block:
        @block.sync
        def _(sp):
            n = 0
            sp.dma_start(tab[:], a["c_tab"]).then_inc(tabs_in, 16)
            sp.dma_start(dm[:], a["c_dm"]).then_inc(tabs_in, 16)
            sp.dma_start(wq, a["c_wq"]).then_inc(tabs_in, 16)
            sp.dma_start(wqs, a["c_wqs"]).then_inc(tabs_in, 16)
            for src, dst_p, dst_s in ((KA, "o_wkp", "o_wks"), (VA, "o_wvp", "o_wvs")):
                sp.dma_start(a[dst_p].rearrange("a b (t p) h d -> p (a b t) (h d)", p=P),
                             z[src][:, 0:NT - 1, :]).then_inc(stores, 16)
                sp.dma_start(a[dst_s].rearrange("a b i h d -> (a b i) (h d)"), z[src][:NS, NT - 1, :]).then_inc(stores, 16)
                n += 32
            sp.wait_ge(stores, n)
            sp.wait_ge(tev[0], 10)
            sp.wait_ge(tev[1], 10)
            sp.dma_start(dms[:NS], a["c_dms"]).then_inc(dms_in, 16)
            src = a["state_ret"].rearrange("a b (q e) d f -> e q d (a b) f", e=2)
            for e in range(2):
                for q in range(NP):
                    sp.dma_start(s0[64 * e:64 * e + 64, q, :].rearrange("d (b f) -> d b f", b=NB),
                                 src[e, q]).then_inc(state_in, 16)
            sp.wait_ge(st_done, SEQ // P)
            dst = a["o_rp"].rearrange("a b (q e) d f -> e d (a b q) f", e=2)
            for e in range(2):
                sp.dma_start(dst[e], st[64 * e:64 * e + 64]).then_inc(stores, 16)
                n += 16
            sp.wait_ge(s1_done, NP)
            dst = a["o_rs"].rearrange("a b (q e) d f -> e q d (a b) f", e=2)
            for e in range(2):
                for q in range(NP):
                    sp.dma_start(dst[e, q], s1[64 * e:64 * e + 64, q, :].rearrange("d (b f) -> d b f", b=NB)
                                 ).then_inc(stores, 16)
                    n += 16
            sp.wait_ge(stores, n)

        @block.tensor
        def _(pe):
            for k in range(20):
                j, t = divmod(k, NT)
                r = rows(t)
                if k >= 2:
                    pe.wait_ge(tev[k % 2], k // 2)
                for p in range(NP):
                    last = pe.transpose(m.bank[k % 2][:, p * P:p * P + r],
                                        z[(QR, KR, QA, KA)[j]][:r, t, p * P:(p + 1) * P], m.ident[:r, :r])
                last.then_inc(tr_done, 1)
            pe.wait_ge(tev[0], 10)
            pe.wait_ge(tev[1], 10)

            def turn_out(i, r):
                pe.wait_ge(out_ready, i + 1)
                if i:
                    pe.wait_ge(out_stored, i)
                for c in range(4):
                    last = pe.transpose(m.bank[6][:, c * P:c * P + r], ot[i % 2][:r, c * P:(c + 1) * P],
                                        m.ident[:r, :r])
                last.then_inc(out_turned, 1)

            def half(ap, h):
                return ap[64 * (h % 2):64 * (h % 2) + 64]

            for n in range(SEQ // P):
                tc = slice(n * P, (n + 1) * P)
                for j in range(2):
                    if n:
                        pe.wait_ge(sd_done, 2 * n - 1 + j)
                    for h in range(j, H, 2):
                        last = pe.matmul(m.bank[2 + j][:, (h // 2) * P:(h // 2 + 1) * P],
                                         half(kr_t, h)[:, h // 2, tc], half(qr_t, h)[:, h // 2, tc],
                                         start=True, stop=True)
                    last.then_inc(sc_done, 1)
                pe.wait_ge(kw_done, n + 1)
                if n:
                    pe.wait_ge(st_done, n)
                    pe.wait_ge(gn_c, n)
                for h in range(H):
                    last = pe.matmul(half(m.bank[5], h)[:, (h // 2) * HD:(h // 2 + 1) * HD],
                                     kw[:, h * HD:(h + 1) * HD], z[VR][:, n, h * HD:(h + 1) * HD],
                                     start=True, stop=True)
                last.then_inc(kv_done, 1)
                pe.wait_ge(sd_done, 2 * n + 2)
                if n:
                    pe.wait_ge(qw_done, n)
                for h in range(H):
                    o = m.bank[(4, 7)[h % 2]][:, (h // 2) * HD:(h // 2 + 1) * HD]
                    last = pe.matmul(o, sd[:, h, :], z[VR][:, n, h * HD:(h + 1) * HD], start=True, stop=(n == 0))
                    if n:
                        last = pe.matmul(o, half(qw, h)[:, h // 2, :], half(st, h)[:, h // 2, :], start=False, stop=True)
                last.then_inc(o_done, 1)
                if n:
                    turn_out(n - 1, P)
            turn_out(3, P)

            sc = slice(SEQ, T)
            for h in range(H):
                last = pe.matmul(m.bank[2 + h % 2][:NS, (h // 2) * NS:(h // 2 + 1) * NS], half(kr_t, h)[:, h // 2, sc],
                                 half(qr_t, h)[:, h // 2, sc], start=True, stop=True)
            last.then_inc(sc_done, 1)
            pe.wait_ge(sd_done, 2 * 4 + 2)
            pe.wait_ge(qw_done, 4)
            pe.wait_ge(state_in, 16 * H)
            pe.wait_ge(gn_c, 4)
            for h in range(H):
                o = half(m.bank[4], h)[:, (h // 2) * NS:(h // 2 + 1) * NS]
                pe.matmul(o, z[VR][:NS, NT - 1, h * HD:(h + 1) * HD], sd[:NS, h, :NS], start=True, stop=True)
                o = half(m.bank[h % 2], h)[:, (h // 2) * NS:(h // 2 + 1) * NS]
                for b in range(NB):
                    last = pe.matmul(o[:, LS * b:LS * b + LS], half(s0, h)[:, h // 2, b * HD:(b + 1) * HD],
                                     half(qws, h)[:, h // 2, LS * b:LS * b + LS], start=True, stop=True)
            last.then_inc(osT_done, 1)
            pe.wait_ge(kw_done, 5)
            for h in range(H):
                q = h // 2
                if q >= 2 and h % 2 == 0:
                    pe.wait_ge(s1_done, q - 1)
                pe.wait_ge(vx_done, h + 1)
                last = pe.matmul(half(m.bank[(5, 7)[q % 2]], h)[:, :], kw[:NS, h * HD:(h + 1) * HD], vx[h % 2][:NS, :],
                                 start=True, stop=True)
                last.then_inc(kvs_done, 1)
            pe.wait_ge(ots_done, 3)
            for q in range(NP):
                last = pe.transpose(m.bank[3][:NS, q * P:(q + 1) * P], ots[:, q, :], m.ident[:, :])
            last.then_inc(os_done, 1)

            def scores(k):
                qb, h = AT[k]
                n = (qb + 1) * P
                if k >= 2:
                    pe.wait_ge(sb_done, k - 1)
                pe.matmul(m.bank[k % 2][:, :n], half(qa_t, h)[:, h // 2, qb * P:(qb + 1) * P],
                          half(ka_t, h)[:, h // 2, :n], start=True, stop=True).then_inc(as_done, 1)

            def probs_v(k):
                qb, h = AT[k]
                pe.wait_ge(pt_ev, k + 1)
                if h == 0 and qb >= 2:
                    pe.wait_ge(out_ready, qb + 4)
                if k == 0:
                    pe.wait_ge(gn_c, 5)
                    pe.wait_ge(ots_done, 3)
                for j in range(qb + 1):
                    last = pe.matmul(m.bank[4 + qb % 2][:, h * HD:(h + 1) * HD], pt[k % 2][:, j * P:(j + 1) * P],
                                     z[VA][:, j, h * HD:(h + 1) * HD], start=(j == 0), stop=(j == qb))
                last.then_inc(pv_done, 1)

            scores(0)
            for k, (qb, h) in enumerate(AT):
                if k + 1 < len(AT):
                    scores(k + 1)
                if k:
                    probs_v(k - 1)
                pe.wait_ge(ex_done, k + 1)
                if k >= 2:
                    pe.wait_ge(pt_ev, k - 1)
                if k == 0:
                    pe.wait_ge(sd_done, 10)
                    pe.wait_ge(gn_c, 5)
                for j in range(qb + 1):
                    last = pe.transpose(m.bank[2 + k % 2][:, j * P:(j + 1) * P], pb[k % 2][:, j * P:(j + 1) * P], m.ident[:, :])
                last.then_inc(pt_done, 1)
                if k == 4:
                    turn_out(4, NS)
                if h == 4 and qb:
                    turn_out(4 + qb, P)
            probs_v(len(AT) - 1)
            turn_out(8, P)

        @block.scalar
        def _(act):
            def store_turned(k):
                t = k % NT
                act.wait_ge(tr_done, k + 1)
                act.activation(tr[k // NT][:, :, tcol(t)],
                               m.bank[k % 2][:].rearrange("p (c n) -> p c n", c=4)[:, :, :rows(t)], ACT.Copy).then_inc(tev[1], 1)

            def store_out(i, t, off):
                act.wait_ge(out_turned, i + 1)
                act.activation(m.ht[:, off:off + 4, tcol(t)],
                               m.bank[6][:].rearrange("p (c n) -> p c n", c=4)[:, :, :rows(t)], ACT.Copy).then_inc(out_stored, 1)

            def square(i, r):
                act.wait_ge(gn_c, i + 1)
                if i:
                    act.wait_ge(gn_red, i)
                act.activation(sq[:r, :], cc[:r, :], ACT.Square).then_inc(gn_sq, 1)

            for k in range(1, 20, 2):
                store_turned(k)
            for n in range(4):
                square(n, P)
                store_out(n, n, 0)
            act.wait_ge(osT_done, 1)
            act.activation(ots[:], m.bank[4][:, :NP * NS].rearrange("p (q n) -> p q n", q=NP), ACT.Copy).then_inc(ots_done, 1)
            square(4, NS)

            def exps(k):
                n = (AT[k][0] + 1) * P
                act.wait_ge(mx_done, k + 1)
                if k >= 2:
                    act.wait_ge(pt_done, k - 1)
                act.activation(pb[k % 2][:, :n], sb[k % 2][:, :n], ACT.Exp, bias=m.amx[:, k:k + 1],
                               accum_out=m.asum[:, k:k + 1]).then_inc(ex_done, 1)

            for k, (qb, h) in enumerate(AT):
                exps(k)
                if k:
                    i, n = k - 1, (AT[k - 1][0] + 1) * P
                    act.wait_ge(pt_done, i + 1)
                    if i >= 2:
                        act.wait_ge(pv_done, i - 1)
                    act.activation(pt[i % 2][:, :n], m.bank[2 + i % 2][:, :n], ACT.Copy).then_inc(pt_ev, 1)
                if k == 5:
                    store_out(4, 4, 0)
                if h == 5 and qb:
                    store_out(4 + qb, qb - 1, 4)
            i = len(AT) - 1
            act.wait_ge(pt_done, i + 1)
            act.wait_ge(pv_done, i - 1)
            act.activation(pt[i % 2][:], m.bank[2 + i % 2][:], ACT.Copy).then_inc(pt_ev, 1)
            store_out(8, 3, 4)

        @block.gpsimd
        def _(pool):
            pool.wait_ge(tabs_in, 64)
            pool.wait_ge(tev[0], 10)
            pool.wait_ge(tev[1], 10)

            def norm(i, r):
                pool.wait_ge(gn_red, i + 1)
                pool.tensor_scalar(m.gnr[:r, :], m.gnv[:r, :], 1.0 / HD, EPS, ALU.mult, ALU.add).then_inc(gn_var, 1)
                pool.wait_ge(gn_var, i + 1)
                pool.tensor_tensor(m.gnr[:r, :], m.gnr[:r, :], m.neghalf[:r, 0:8], ALU.pow).then_inc(gn_rstd, 1)

            for n in range(4):
                if n:
                    pool.wait_ge(kv_done, n)
                pool.tensor_tensor(hv(kw[:]), hv(z[KR][:, n, :]), over(m.wk[:, :], HD), ALU.mult).then_inc(kw_done, 1)
                if n:
                    pool.wait_ge(o_done, n)
                    pool.tensor_tensor(qw[:], qr_t[:, :, n * P:(n + 1) * P], hv(wq, NP), ALU.mult).then_inc(qw_done, 1)
                norm(n, P)
            pool.wait_ge(kv_done, 4)
            pool.wait_ge(dms_in, 16)
            pool.tensor_tensor(qws[:], qr_t[:, :, SEQ:T], hv(wqs, NP), ALU.mult).then_inc(qw_done, 1)
            pool.tensor_tensor(hv(kw[:NS]), hv(z[KR][:NS, NT - 1, :]), over(m.wks[:NS, :], HD), ALU.mult).then_inc(kw_done, 1)
            for h in range(H):
                if h >= 2:
                    pool.wait_ge(kvs_done, h - 1)
                pool.tensor_tensor(hv(vx[h % 2][:NS]), across(z[VR][:NS, NT - 1, h * HD:(h + 1) * HD], 1, NB),
                                   over(m.bmask[:NS, :], HD), ALU.mult).then_inc(vx_done, 1)
            norm(4, NS)

        @block.vector
        def _(dve):
            link = Chain(dve, ch)
            for k in range(0, 20, 2):
                t = k % NT
                dve.wait_ge(tr_done, k + 1)
                dve.tensor_copy(tr[k // NT][:, :, tcol(t)],
                                m.bank[k % 2][:].rearrange("p (c n) -> p c n", c=4)[:, :, :rows(t)]).then_inc(tev[0], 1)
            dve.wait_ge(tabs_in, 64)

            def group_norm(i, t, o):
                r = rows(t)
                for e in range(2):
                    link(dve.tensor_reduce(m.gnm[:r, e::2], o[e], AX.X, ALU.add))
                link(dve.tensor_scalar(m.gnm[:r, :], m.gnm[:r, :], -1.0 / HD, None, ALU.mult))
                link(dve.tensor_tensor(hv(cc[:r])[:, 0::2], o[0], over(m.gnm[:r, 0::2], HD), ALU.add))
                dve.tensor_tensor(hv(cc[:r])[:, 1::2], o[1], over(m.gnm[:r, 1::2], HD), ALU.add).then_inc(gn_c, 1)
                dve.wait_ge(gn_sq, i + 1)
                dve.tensor_reduce(m.gnv[:r, :], hv(sq[:r]), AX.X, ALU.add).then_inc(gn_red, 1)
                dve.wait_ge(gn_rstd, i + 1)
                link(dve.tensor_tensor(hv(cc[:r]), hv(cc[:r]), over(m.gnr[:r, :], HD), ALU.mult))
                if i >= 2:
                    dve.wait_ge(out_turned, i - 1)
                dve.tensor_tensor(ot[i % 2][:r], cc[:r], z[GR][:r, t, :], ALU.mult).then_inc(out_ready, 1)

            for n in range(4):
                for j in range(2):
                    dve.wait_ge(sc_done, 2 * n + j + 1)
                    if n:
                        dve.wait_ge(o_done, n)
                    dve.tensor_tensor(sd[:, j::2, :], hv(m.bank[2 + j][:], 4), dm[:, j::2, :],
                                      ALU.mult).then_inc(sd_done, 1)
                dve.wait_ge(kv_done, n + 1)
                dve.wait_ge(o_done, n + 1)
                kv = hv(m.bank[5][:, :NP * HD], NP)
                if n == 0:
                    dve.tensor_copy(st[:], kv).then_inc(st_done, 1)
                else:
                    link(dve.tensor_tensor(st[:], st[:], over(m.decay_chunk[:, :], HD), ALU.mult))
                    dve.tensor_tensor(st[:], st[:], kv, ALU.add).then_inc(st_done, 1)
                group_norm(n, n, [hv(m.bank[k][:, :NP * HD], NP) for k in (4, 7)])
            dve.wait_ge(dms_in, 16)
            dve.wait_ge(sc_done, 9)
            dve.wait_ge(o_done, 4)
            for j in range(2):
                dve.tensor_tensor(sd[:NS, j::2, :NS], hv(m.bank[2 + j][:NS, :NP * NS], NP), dms[:NS, j::2, :],
                                  ALU.mult).then_inc(sd_done, 1)
            dve.wait_ge(ots_done, 1)
            for e in range(2):
                dve.tensor_tensor(ots[64 * e:64 * e + 64], ots[64 * e:64 * e + 64],
                                  m.bank[e][64 * e:64 * e + 64, :NP * NS].rearrange("p (q n) -> p q n", q=NP),
                                  ALU.add).then_inc(ots_done, 1)
            dve.wait_ge(state_in, 16 * H)
            for q in range(NP):
                dve.wait_ge(kvs_done, 2 * q + 2)
                link(dve.tensor_scalar(s1[:, q, :], s0[:, q, :], m.decay_steps[:, q:q + 1], None, ALU.mult))
                dve.tensor_tensor(s1[:, q, :], s1[:, q, :], m.bank[(5, 7)[q % 2]][:], ALU.add).then_inc(s1_done, 1)
            dve.wait_ge(os_done, 1)
            os_ = m.bank[3][:NS].rearrange("p (q e d) -> p e q d", e=2, d=HD)
            group_norm(4, 4, [os_[:, 0], os_[:, 1]])

            def out_rows(qb):
                i = 5 + qb
                dve.wait_ge(pv_done, 8 * qb + 8)
                link(dve.reciprocal(m.asum[:, 8 * qb:8 * qb + 8], m.asum[:, 8 * qb:8 * qb + 8]))
                dve.wait_ge(out_turned, i - 1)
                dve.tensor_tensor(hv(ot[i % 2][:]), hv(m.bank[4 + qb % 2][:]), over(m.asum[:, 8 * qb:8 * qb + 8], HD),
                                  ALU.mult).then_inc(out_ready, 1)

            for k, (qb, h) in enumerate(AT):
                n = (qb + 1) * P
                dve.wait_ge(as_done, k + 1)
                if k >= 2:
                    dve.wait_ge(ex_done, k - 1)
                dve.scalar_tensor_tensor(sb[k % 2][:, :n], m.bank[k % 2][:, :n], HD ** -0.5, tab[:, h, 512 - n:],
                                         ALU.mult, ALU.add).then_inc(sb_done, 1)
                dve.wait_ge(sb_done, k + 1)
                dve.tensor_reduce(m.amx[:, k:k + 1], sb[k % 2][:, :n], AX.X, ALU.max, negate=True).then_inc(mx_done, 1)
                if h == 2 and qb:
                    out_rows(qb - 1)
            out_rows(3)


def mix_windows(nc, m, a):
    qa_t, ka_t = m.qa_t, m.ka_t
    kv = [m.at(f"{n}_half{i}", m.Z + 2560 * j, [KC // 2, RW])
          for j, (n, i) in enumerate((("k", 0), ("k", 1), ("v", 0), ("v", 1)))]
    k_half, v_half = kv[:2], kv[2:]
    kt = m.at("window_k_t", m.Z + 4 * 2560, [NP, KC * P])
    btab = m.at("window_tab", m.W, [KC * P + 2 * NS - LS])
    pb = m.at("window_probs", m.W + 1408, [WK])
    pt = m.at("window_probs_t", m.W + 2752, [KC + 1, P])
    sb = m.at("window_scored", m.HTH, [WK])
    qb_all = m.at("q_blocks", m.HTH + 1344, [NB, NP, 32])
    qb = m.at("q_block", m.HTH + 2368, [NP, 32])
    va = m.z[6]
    ow = m.at("window_out", m.HTH + 3600, [P])
    ow_done, ot_done = m.sem("window_out_normed"), m.sem("window_out_turned")
    zero = m.at("zero_rows", m.HTH + 2560, [D])
    S = m.sem
    zero_done, zero_out = S("zero_rows_done"), S("zero_rows_out")
    tab_in, qz, qb_done = S("window_tab_in"), S("q_blocks_zeroed"), S("q_block_done")
    kin, vin = [S("k_half0_in"), S("k_half1_in")], [S("v_half0_in"), S("v_half1_in")]
    kt_done, kt_ev = S("window_k_turned"), [S("k_t_stored_even"), S("k_t_stored_odd")]
    ws_done, sb_done, mx_done, ex_done = (S("window_scored"), S("window_biased"), S("window_max"), S("window_exped"))
    rl = S("window_recip")
    pt_done, pt_ev, pv_done, o_ev = S("window_p_turned"), S("window_p_stored"), S("window_pv"), S("window_out")
    ck, cv = a["cache_win_k"], a["cache_win_v"]
    HC = KC // 2
    far = [c.rearrange("a b (c g r) h d -> (a b) g r c (h d)", g=16, r=16) for c in (ck, cv)]
    near = [c[:, :, WBUF - NEAR:].rearrange("a b (p c) h d -> (a b) p c (h d)", p=P) for c in (ck, cv)]
    out4 = lambda e: m.ht[64 * e:64 * e + 64, 4:8, :]

    with nc.Block() as block:
        @block.sync
        def _(sp):
            sp.dma_start(btab[:], a["c_btab"]).then_inc(tab_in, 16)

            def far_rows(dst, src, b, c0, n, sem):
                for c in range(n):
                    sp.dma_start(dst[:, c, :], src[b, :, 0:LS, c0 + c, :].rearrange("a g r n -> (a g) r n")
                                 ).then_inc(sem, 16)

            def load(b, is_v):
                half, sems = (v_half, vin) if is_v else (k_half, kin)
                i = bass.ds(b, 1)
                far_rows(half[0], far[is_v], i, 0, HC, sems[0])
                return half, sems, i

            def second(half, sems, i, is_v):
                far_rows(half[1], far[is_v], i, HC, FC - HC, sems[1])
                sp.dma_start(half[1][:, FC - HC:, :], near[is_v][i].rearrange("a p c n -> (a p) c n")).then_inc(sems[1], 16)

            def keys(n):
                sp.wait_ge(kt_done, n * KC - KC + HC + 1)
                half, sems, i = load(n, 0)
                sp.wait_ge(kt_done, n * KC + 1)
                second(half, sems, i, 0)

            def values(n):
                sp.wait_ge(pv_done, n + 1)
                second(*load(n, 1), 1)

            second(*load(0, 0), 0)
            second(*load(0, 1), 1)
            keys(1)
            with sp.Fori(0, NB - 2) as i:
                keys(i + 2)
                values(i + 1)
            values(NB - 1)

        @block.vector
        def _(dve):
            for sem in (sb_done, kt_ev[0], o_ev):
                dve.sem_inc(sem, 1)
            dve.memset(zero[:], 0.0).then_inc(zero_done, 1)
            dve.memset(qb_all[:], 0.0).then_inc(qz, 1)
            dve.wait_ge(qz, 1)
            for e in range(2):
                for q in range(NP):
                    dve.tensor_copy(qb_all[64 * e:64 * e + 64, :, q, 8 * e:8 * e + 8],
                                    qa_t[64 * e:64 * e + 64, q, SEQ:T].rearrange("p (b i) -> p b i", b=NB)).then_inc(qz, 1)
            dve.wait_ge(qz, 1 + 2 * NP)
            dve.wait_ge(tab_in, 16)

            def keys(n):
                for c in range(0, KC, 2):
                    dve.wait_ge(kt_done, n * KC + c + 2)
                    if c == 0:
                        dve.wait_ge(ws_done, n * 3 + 1)
                    dve.tensor_copy(kt[:, :, c * P:(c + 1) * P], m.bank[0][:].rearrange("p (q n) -> p q n", q=NP)
                                    ).then_inc(kt_ev[0], 1)
                dve.tensor_copy(qb[:], qb_all[:, bass.ds(n, 1)].rearrange("p a q n -> p (a q) n")).then_inc(qb_done, 1)

            def biased(n):
                dve.wait_ge(ex_done, n + 1)
                for j, lo in enumerate((0, 512)):
                    dve.wait_ge(ws_done, n * 3 + j + 2)
                    dve.scalar_tensor_tensor(sb[:, lo:lo + 512], m.bank[2 + j][:], HD ** -0.5, btab[:, lo:lo + 512],
                                             ALU.mult, ALU.add).then_inc(sb_done, 1)
                k = KC * P - 1024
                dve.wait_ge(ws_done, n * 3 + 4)
                dve.scalar_tensor_tensor(sb[:, 1024:KC * P], m.bank[4][:, :k], HD ** -0.5, btab[:, 1024:KC * P],
                                         ALU.mult, ALU.add).then_inc(sb_done, 1)
                dve.scalar_tensor_tensor(sb[:, KC * P:], m.bank[4][:, k:k + NS], HD ** -0.5,
                                         btab[:, bass.ds((n * -1 + (NB - 1)) * LS + KC * P, NS)],
                                         ALU.mult, ALU.add).then_inc(sb_done, 1)
                dve.wait_ge(sb_done, n * 4 + 5)
                dve.tensor_reduce(m.wmx[:, 0:1], sb[:], AX.X, ALU.max, negate=True).then_inc(mx_done, 1)

            def outputs(n):
                dve.wait_ge(pt_done, n * 3 + 3)
                dve.wait_ge(pv_done, n + 1)
                dve.tensor_copy(pt[:, 4:8, :], m.bank[6][:].rearrange("p (c n) -> p c n", c=4)).then_inc(pt_ev, 1)
                dve.wait_ge(ex_done, n + 2)
                dve.reciprocal(m.wmx[:, 2:3], m.wmx[:, 1:2]).then_inc(rl, 1)
                dve.wait_ge(rl, n + 1)
                dve.wait_ge(pv_done, n + 2)
                dve.tensor_scalar(ow[:], m.bank[1][:, 0:P], m.wmx[:, 2:3], None, ALU.mult).then_inc(ow_done, 1)
                dve.wait_ge(ot_done, n + 1)
                for e in range(2):
                    dve.tensor_copy(out4(e)[:, :, bass.ds(n * LS + SEQ, LS)],
                                    m.bank[1][64 * e:64 * e + 64, P:2 * P].rearrange("p (q n) -> p q n", q=NP)[:, :, 8 * e:8 * e + 8]
                                    ).then_inc(o_ev, 1)

            keys(0)
            with dve.Fori(0, NB - 1) as i:
                biased(i)
                keys(i + 1)
                outputs(i)
            biased(NB - 1)
            outputs(NB - 1)

        @block.scalar
        def _(act):
            for sem in (kt_ev[1], pt_ev, ex_done):
                act.sem_inc(sem, 1)
            act.wait_ge(zero_done, 1)
            for n in range(NPAIR, NPT):
                act.dma_start(m.slots_dram[n * P:(n + 1) * P, :], zero[:]).then_inc(zero_out, 16)

            def keys(n):
                for c in range(1, KC, 2):
                    act.wait_ge(kt_done, n * KC + c + 2)
                    if c == 1:
                        act.wait_ge(ws_done, n * 3 + 1)
                    act.activation(kt[:, :, c * P:(c + 1) * P], m.bank[7][:].rearrange("p (q n) -> p q n", q=NP),
                                   ACT.Copy).then_inc(kt_ev[1], 1)

            def exps(n):
                act.wait_ge(mx_done, n + 1)
                act.wait_ge(pt_done, n * 3 + 1)
                act.activation(pb[:], sb[:], ACT.Exp, bias=m.wmx[:, 0:1], accum_out=m.wmx[:, 1:2]).then_inc(ex_done, 1)

            def turned(n):
                act.wait_ge(pt_done, n * 3 + 2)
                act.wait_ge(pv_done, n + 1)
                act.activation(pt[:, 0:4, :], m.bank[5][:].rearrange("p (c n) -> p c n", c=4), ACT.Copy).then_inc(pt_ev, 1)
                act.wait_ge(pt_done, n * 3 + 4)
                act.activation(pt[:, 8:10, :], m.bank[2][:, 0:256].rearrange("p (c n) -> p c n", c=2), ACT.Copy).then_inc(pt_ev, 1)
                act.activation(pt[:NS, 10, :], m.bank[2][:NS, 256:384], ACT.Copy).then_inc(pt_ev, 1)

            keys(0)
            with act.Fori(0, NB - 1) as i:
                exps(i)
                keys(i + 1)
                turned(i)
            exps(NB - 1)
            turned(NB - 1)
            act.wait_ge(zero_out, 16 * NOVP)

        @block.tensor
        def _(pe):
            for sem in (ws_done, pt_done, pv_done, kt_done):
                pe.sem_inc(sem, 1)

            def keys(n):
                for c in range(KC):
                    if c == 0:
                        pe.wait_ge(kin[0], (n + 1) * (16 * HC))
                    if c == HC:
                        pe.wait_ge(kin[1], (n + 1) * (16 * (FC - HC + 1)))
                    pe.wait_ge(kt_ev[c % 2], n * HC + c // 2 + 1)
                    for q in range(NP):
                        last = pe.transpose(m.bank[(0, 7)[c % 2]][:, q * P:(q + 1) * P],
                                            k_half[c // HC][:, c % HC, q * P:(q + 1) * P], m.ident[:, :])
                    last.then_inc(kt_done, 1)

            def scores(n):
                pe.wait_ge(qb_done, n + 1)
                pe.wait_ge(pt_ev, n * 4 + 1)
                pe.wait_ge(sb_done, n * 4 + 1)
                for j, (lo, k) in enumerate(((0, 512), (512, 512), (1024, KC * P - 1024))):
                    for par in range(2):
                        pe.wait_ge(kt_ev[par], n * HC + ((lo + k) // P + 1 - par) // 2 + 1)
                    for q in range(NP):
                        last = pe.matmul(m.bank[2 + j][32 * q:32 * q + 32, :k], qb[:, q, :], kt[:, q, lo:lo + k],
                                         start=True, stop=True)
                    if j == 2:
                        for q in range(NP):
                            last = pe.matmul(m.bank[4][32 * q:32 * q + 32, k:k + NS], qb[:, q, :], ka_t[:, q, SEQ:T],
                                             start=True, stop=True)
                    last.then_inc(ws_done, 1)

            def products(n):
                pe.wait_ge(ex_done, n + 2)
                pe.wait_ge(pt_ev, n * 4 + 1)
                for j in range(3):
                    for c in range(4 * j, min(4 * j + 4, KC)):
                        last = pe.transpose(m.bank[(5, 6, 2)[j]][:, (c - 4 * j) * P:(c - 4 * j + 1) * P],
                                            pb[:, c * P:(c + 1) * P], m.ident[:, :])
                    if j == 2:
                        last = pe.transpose(m.bank[2][:NS, 256:384], pb[:, KC * P:], m.ident[:, :])
                    last.then_inc(pt_done, 1)
                pe.wait_ge(pt_ev, n * 4 + 5)
                pe.wait_ge(o_ev, n * 2 + 1)
                pe.wait_ge(vin[0], (n + 1) * (16 * HC))
                pe.wait_ge(vin[1], (n + 1) * (16 * (FC - HC + 1)))
                for c in range(KC + 1):
                    for q in range(NP):
                        v = v_half[c // HC][:, c % HC, q * P:(q + 1) * P] if c < KC else va[:NS, NT - 1, q * P:(q + 1) * P]
                        p = pt[:, c, 32 * q:32 * q + 32] if c < KC else pt[:NS, KC, 32 * q:32 * q + 32]
                        last = pe.matmul(m.bank[1][32 * q:32 * q + 32, 0:P], p, v, start=(c == 0), stop=(c == KC),
                                         skip_group_check=True)
                last.then_inc(pv_done, 1)

            def turn_out(n):
                pe.wait_ge(ow_done, n + 1)
                pe.transpose(m.bank[1][:, P:2 * P], ow[:], m.ident[:, :]).then_inc(ot_done, 1)

            keys(0)
            scores(0)
            with pe.Fori(0, NB - 1) as i:
                keys(i + 1)
                products(i)
                scores(i + 1)
                turn_out(i)
            products(NB - 1)
            turn_out(NB - 1)


def project_out(nc, m, a):
    residual(nc, m, "wo", a["w_o"], None, None)


def residual(nc, m, name, weight, src, gain):
    w = weight.rearrange("a (c p) n -> p (a c) n", p=P)
    res = m.sem(f"{name}_added")
    st = [m.at(f"{name}_rows{i}", m.Z + 512 * i, [512]) for i in range(2)]

    def store(act, bank, b, t):
        k = b * NT + t
        if k >= 2:
            act.wait_ge(res, k - 1)
        return act.activation(st[k % 2][:rows(t), :], bank[:rows(t), :], ACT.Copy)

    def vector(dve, b, t, stored, k):
        dve.wait_ge(stored, k + 1)
        x = m.x[:rows(t), t, 512 * b:512 * b + 512]
        dve.tensor_tensor(x, x, st[k % 2][:rows(t), :], ALU.add).then_inc(res, 1)

    dense(nc, m, name, src, [w[:, :, :512], w[:, :, 512:]], range(NT), gain, store, {"vector": vector},
          [rows(t) for t in range(NT)])


def project_memory(nc, m, a):
    mk = m.at("mem_k", m.Z + 5120, [2, D])
    mv = m.at("mem_v", m.Z + 7168, [2, D])
    mx = m.at("mem_rows", m.Z + 15872, [2, D])
    m.mem_k, m.mem_v = mk, mv
    arrive = m.sem("mem_in")
    with nc.Block() as block:
        @block.sync
        def _(sp):
            sp.dma_start(mx[:], a["mem_prompt"].rearrange("a (t p) d -> p (a t) d", p=P)).then_inc(arrive, 16)
            sp.wait_ge(arrive, 16)
    w = [a[n].rearrange("a (p c) n -> p (a c) n", p=P)[:, :, 512 * j:512 * j + 512] for n in ("w_mk", "w_mv") for j in range(2)]
    dsts = [mk, mk, mv, mv]
    store = lambda act, bank, b, t: act.activation(dsts[b][:, t, 512 * (b % 2):512 * (b % 2) + 512], bank[:], ACT.Copy)
    hooks = wide_norm(nc, m, "mem", [(0, 2), (1, 2)], mk, m.g_k_mem, 2, [P, P])
    dense(nc, m, "mem", mx[:], w, range(2), m.g_mem, store, hooks, [P, P])


def wide_norm(nc, m, name, blocks, dst, gain, nt, widths):
    squared, reduced, rstd, varied, ch = (m.sem(f"{name}_hsq"), m.sem(f"{name}_hred"), m.sem(f"{name}_hrstd"),
                                          m.sem(f"{name}_hvar"), m.sem(f"{name}_hchain"))
    sq = [m.scr[:, 0:512], m.scr[:, 512:1024]]
    hv = lambda ap: ap.rearrange("p (h d) -> p h d", h=2)
    chain = []

    def scalar(act, b, t, stored, k):
        if b < 2:
            if k >= 2:
                act.wait_ge(reduced, k - 1)
            act.wait_ge(stored, k + 1)
            r = widths[t]
            act.activation(sq[k % 2][:r, :], dst[:r, t, 512 * b:512 * b + 512], ACT.Square).then_inc(squared, 1)

    def vector(dve, b, t, stored, k):
        if b < 2:
            if not chain:
                chain.append(Chain(dve, ch))
            r = widths[t]
            z = hv(dst[:r, t, 512 * b:512 * b + 512])
            dve.wait_ge(squared, k + 1)
            dve.tensor_reduce(m.qms[:r, 2 * k:2 * k + 2], hv(sq[k % 2][:r, :]), AX.X, ALU.add).then_inc(reduced, 1)
            dve.wait_ge(rstd, k + 1)
            chain[0](dve.tensor_tensor(z, z, over(m.qrs[:r, 2 * k:2 * k + 2], MD), ALU.mult))
            chain[0](dve.tensor_tensor(z, z, across(gain[:r, :], 1, 2), ALU.mult))

    def gpsimd(pool):
        for k in range(2 * nt):
            r = widths[k % nt]
            c = slice(2 * k, 2 * k + 2)
            pool.wait_ge(reduced, k + 1)
            pool.tensor_scalar(m.qrs[:r, c], m.qms[:r, c], 1.0 / MD, EPS, ALU.mult, ALU.add).then_inc(varied, 1)
            pool.wait_ge(varied, k + 1)
            pool.tensor_tensor(m.qrs[:r, c], m.qrs[:r, c], m.neghalf[:r, 0:2], ALU.pow).then_inc(rstd, 1)

    return {"scalar": scalar, "vector": vector, "gpsimd": gpsimd}


def project_cross(nc, m, a):
    qm = m.at("cross_q", m.Z, [NT, D])
    m.cross_q = qm
    w = a["w_mq"].rearrange("a (p c) n -> p (a c) n", p=P)
    store = lambda act, bank, b, t: act.activation(qm[:rows(t), t, 512 * b:512 * b + 512], bank[:rows(t), :], ACT.Copy)
    widths = [rows(t) for t in range(NT)]
    hooks = wide_norm(nc, m, "cross", None, qm, m.g_q_mem, NT, widths)
    dense(nc, m, "cross", m.x, [w[:, :, :512], w[:, :, 512:]], range(NT), m.g_cross, store, hooks, widths)


def cross_attend(nc, m, a):
    qm, mk, mv = m.cross_q, m.mem_k, m.mem_v
    qt = m.at("cross_q_t", m.Z + 9216, [C8, T])
    kt = m.at("mem_k_t", m.Z + 9216 + C8 * T, [C8, MEM])
    sk = [m.at(f"cache_k{i}", m.W + 2048 * i, [2, D]) for i in range(2)]
    sv = [m.at(f"cache_v{i}", m.W + 4096 + 2048 * i, [2, D]) for i in range(2)]
    skt = m.at("cache_k_t", m.WH, [C8, MEM])
    pb = [m.at(f"cross_probs{i}", m.WH + 2048 + 1024 * i, [MH, MEM]) for i in range(2)]
    pt = m.at("cross_probs_t", m.WH + 4096, [2 * MH, P])
    spb = [m.at(f"cache_probs{i}", m.WH + 5120 + 256 * i, [MEM]) for i in range(2)]
    S = m.sem
    tr_done, tev = S("cr_turned"), [S("cr_stored_even"), S("cr_stored_odd")]
    sc_done, mx_done, ex_done, pn_done = S("cr_scored"), S("cr_max"), S("cr_exped"), S("cr_normed")
    pt_done, pt_ev, o_done, o_ev = S("cr_p_turned"), S("cr_p_stored"), S("cr_out"), S("cr_out_stored")
    kin, vin = [S("cache_k0_in"), S("cache_k1_in")], [S("cache_v0_in"), S("cache_v1_in")]
    qs = m.at("cache_q", m.WH + 5888, [C8, 32])
    ps = m.at("cache_probs_turned", m.WH + 6144, [2, P])
    so = m.at("cache_out", m.WH + 6400, [MD])
    so_done, st_done = m.sem("cs_out_normed"), m.sem("cs_out_turned")
    cq_done = S("cache_q_done")
    ch, stores = S("cr_chain"), S("cr_stores")
    kt_done, kt_ev = S("ck_turned"), [S("ck_stored_even"), S("ck_stored_odd")]
    s_sc, s_mx, s_ex, s_rl = S("cs_scored"), S("cs_max"), S("cs_exped"), S("cs_recip")
    s_pt, s_pev, s_o, s_oev = S("cs_p_turned"), S("cs_p_stored"), S("cs_out"), S("cs_out_stored")
    ckv = [a[n].rearrange("a b (t p) h d -> p (a b) t (h d)", p=P) for n in ("cache_mem_k", "cache_mem_v")]
    turns = [(qm, qt, t, j) for t in range(NT) for j in range(2)] + [(mk, kt, t, j) for t in range(2) for j in range(2)]
    four = lambda ap: ap.rearrange("p (c n) -> p c n", c=4)
    NQ = NT - 1
    SC = MD ** -0.5

    with nc.Block() as block:
        @block.sync
        def _(sp):
            for src, dst in ((mk, "o_mk"), (mv, "o_mv")):
                sp.dma_start(a[dst].rearrange("a b (t p) h d -> p (a b t) (h d)", p=P), src[:]).then_inc(stores, 16)
            for b in range(2):
                sp.dma_start(sk[b][:], ckv[0][:, b]).then_inc(kin[b], 16)
                sp.dma_start(sv[b][:], ckv[1][:, b]).then_inc(vin[b], 16)
            with sp.Fori(0, NB // 2 - 1) as i:
                for b in range(2):
                    nxt = bass.ds(i * 2 + 2 + b, 1)
                    sp.wait_ge(kt_done, i * 8 + 4 * b + 4)
                    sp.dma_start(sk[b][:], ckv[0][:, nxt].rearrange("p a t n -> p (a t) n")).then_inc(kin[b], 16)
                    sp.wait_ge(s_o, i * 2 + b + 2)
                    sp.dma_start(sv[b][:], ckv[1][:, nxt].rearrange("p a t n -> p (a t) n")).then_inc(vin[b], 16)
            sp.wait_ge(stores, 32)

        @block.tensor
        def _(pe):
            for k, (src, dst, t, j) in enumerate(turns):
                r = rows(t) if src is qm else P
                if k >= 2:
                    pe.wait_ge(tev[k % 2], k // 2)
                for c in range(4):
                    last = pe.transpose(m.bank[k % 2][:, c * P:c * P + r], src[:r, t, (4 * j + c) * P:(4 * j + c + 1) * P], m.ident[:r, :r])
                last.then_inc(tr_done, 1)
            pe.wait_ge(tev[0], len(turns) // 2)
            pe.wait_ge(tev[1], len(turns) // 2)

            def scores(t):
                if t:
                    pe.wait_ge(ex_done, 4 * t)
                for h in range(MH):
                    for k in range(2):
                        last = pe.matmul(m.bank[2 + h // 2][:, (h % 2) * MEM:(h % 2 + 1) * MEM], qt[:, 2 * h + k, tcol(t)],
                                         kt[:, 2 * h + k, :], start=(k == 0), stop=(k == 1))
                last.then_inc(sc_done, 1)

            scores(0)
            for t in range(NQ):
                pe.wait_ge(pn_done, t + 1)
                if t:
                    pe.wait_ge(pt_ev, 2 * t)
                for j in range(2):
                    for c in range(4):
                        h, k = divmod(4 * j + c, 2)
                        last = pe.transpose(m.bank[4 + j][:, c * P:(c + 1) * P], pb[t % 2][:, h, k * P:(k + 1) * P], m.ident[:, :])
                    last.then_inc(pt_done, 1)
                if t + 1 < NQ:
                    scores(t + 1)
                pe.wait_ge(pt_ev, 2 * t + 2)
                if t:
                    pe.wait_ge(o_ev, 2 * t)
                for j in range(2):
                    for c in range(4):
                        h = (4 * j + c) // 2
                        for k in range(2):
                            last = pe.matmul(m.bank[6 + j][:, c * P:(c + 1) * P], mv[:, k, (4 * j + c) * P:(4 * j + c + 1) * P],
                                             pt[:, 2 * h + k, :], start=(k == 0), stop=(k == 1))
                    last.then_inc(o_done, 1)
            pe.wait_ge(o_ev, 2 * NQ)
            pe.wait_ge(ex_done, 4 * NQ)
            for sem in (s_sc, s_pt, s_o):
                pe.sem_inc(sem, 1)

            def keys(n, b, use):
                pe.wait_ge(kin[b], use * 16 + 16)
                for k in range(4):
                    t, j = divmod(k, 2)
                    pe.wait_ge(kt_ev[k % 2], n * 2 + k // 2 + 1)
                    for c in range(4):
                        last = pe.transpose(m.bank[k % 2][:, c * P:(c + 1) * P], sk[b][:, t, (4 * j + c) * P:(4 * j + c + 1) * P], m.ident[:, :])
                    last.then_inc(kt_done, 1)

            def cache_scores(n):
                pe.wait_ge(kt_ev[0], n * 2 + 3)
                pe.wait_ge(kt_ev[1], n * 2 + 3)
                pe.wait_ge(s_ex, n + 1)
                pe.wait_ge(cq_done, n + 2)
                for k in range(2):
                    for h in range(MH):
                        last = pe.matmul(m.bank[2][32 * h:32 * h + 32, :MEM], qs[:, 2 * h + k, :],
                                         skt[:, 2 * h + k, :], start=(k == 0), stop=(k == 1), skip_group_check=True)
                last.then_inc(s_sc, 1)

            def products(n, b, use):
                pe.wait_ge(s_ex, n + 2)
                pe.wait_ge(s_pev, n + 1)
                for k in range(2):
                    last = pe.transpose(m.bank[4][:, k * P:(k + 1) * P], spb[0][:, k * P:(k + 1) * P], m.ident[:, :])
                last.then_inc(s_pt, 1)
                pe.wait_ge(s_pev, n + 2)
                pe.wait_ge(vin[b], use * 16 + 16)
                pe.wait_ge(s_oev, n * 2 + 1)
                for k in range(2):
                    for h in range(MH):
                        last = pe.matmul(m.bank[6][32 * h:32 * h + 32, :MD], ps[:, k, 32 * h:32 * h + 32],
                                         sv[b][:, k, h * MD:(h + 1) * MD], start=(k == 0), stop=(k == 1),
                                         skip_group_check=True)
                last.then_inc(s_o, 1)

            def turn_out(n):
                pe.wait_ge(so_done, n + 1)
                for k in range(2):
                    last = pe.transpose(m.bank[7][:, k * P:(k + 1) * P], so[:, k * P:(k + 1) * P], m.ident[:, :])
                last.then_inc(st_done, 1)

            keys(0, 0, 0)
            cache_scores(0)
            with pe.Fori(0, NB // 2 - 1) as i:
                for b in range(2):
                    keys(i * 2 + b + 1, 1 - b, i + b)
                    products(i * 2 + b, b, i)
                    cache_scores(i * 2 + b + 1)
                    turn_out(i * 2 + b)
            keys(NB - 1, 1, NB // 2 - 1)
            products(NB - 2, 0, NB // 2 - 1)
            cache_scores(NB - 1)
            turn_out(NB - 2)
            products(NB - 1, 1, NB // 2 - 1)
            turn_out(NB - 1)

        def store_turned(copy, eng, k):
            src, dst, t, j = turns[k]
            r = rows(t) if src is qm else P
            eng.wait_ge(tr_done, k + 1)
            copy(dst[:, 4 * j:4 * j + 4, t * P:t * P + r], four(m.bank[k % 2][:])[:, :, :r]).then_inc(tev[k % 2], 1)

        @block.scalar
        def _(act):
            copy = lambda dst, src: act.activation(dst, src, ACT.Copy)
            for k in range(1, len(turns), 2):
                store_turned(copy, act, k)
            for t in range(NQ):
                act.wait_ge(mx_done, t + 1)
                if t >= 2:
                    act.wait_ge(pt_done, 2 * (t - 1))
                for h in range(MH):
                    act.activation(pb[t % 2][:, h, :], m.bank[2 + h // 2][:, (h % 2) * MEM:(h % 2 + 1) * MEM], ACT.Exp,
                                   bias=m.amx[:, 4 * t + h:4 * t + h + 1], scale=SC,
                                   accum_out=m.asum[:, 4 * t + h:4 * t + h + 1]).then_inc(ex_done, 1)
                for j in range(2):
                    act.wait_ge(pt_done, 2 * t + j + 1)
                    if t and j == 0:
                        act.wait_ge(o_done, 2 * t)
                    copy(pt[:, 4 * j:4 * j + 4, :], four(m.bank[4 + j][:])).then_inc(pt_ev, 1)
                for j in range(2):
                    act.wait_ge(o_done, 2 * t + j + 1)
                    copy(m.ht[:, 4 * j:4 * j + 4, tcol(t)], four(m.bank[6 + j][:])).then_inc(o_ev, 1)
            for sem in (kt_ev[1], s_ex):
                act.sem_inc(sem, 1)

            def keys(n):
                act.wait_ge(s_sc, n + 1)
                for k in range(1, 4, 2):
                    t, j = divmod(k, 2)
                    act.wait_ge(kt_done, n * 4 + k + 1)
                    copy(skt[:, 4 * j:4 * j + 4, t * P:(t + 1) * P], four(m.bank[1][:])).then_inc(kt_ev[1], 1)

            def exps(n):
                act.wait_ge(s_mx, n + 1)
                act.wait_ge(s_pt, n + 1)
                act.activation(spb[0][:], m.bank[2][:, :MEM], ACT.Exp, bias=m.wmx[:, 0:1], scale=SC,
                               accum_out=m.wmx[:, 1:2]).then_inc(s_ex, 1)

            keys(0)
            with act.Fori(0, NB - 1) as i:
                exps(i)
                keys(i + 1)
            exps(NB - 1)

        @block.vector
        def _(dve):
            link = Chain(dve, ch)
            dve.memset(qs[:], 0.0).then_inc(cq_done, 1)
            dve.wait_ge(cq_done, 1)
            for k in range(0, len(turns), 2):
                store_turned(dve.tensor_copy, dve, k)
            for t in range(NQ):
                dve.wait_ge(sc_done, t + 1)
                c = slice(4 * t, 4 * t + 4)
                for j in range(2):
                    link(dve.tensor_reduce(m.amx[:, 4 * t + 2 * j:4 * t + 2 * j + 2],
                                           m.bank[2 + j][:].rearrange("p (h n) -> p h n", h=2), AX.X, ALU.max))
                dve.tensor_scalar(m.amx[:, c], m.amx[:, c], -SC, None, ALU.mult).then_inc(mx_done, 1)
                dve.wait_ge(ex_done, 4 * t + 4)
                link(dve.reciprocal(m.asum[:, c], m.asum[:, c]))
                dve.tensor_tensor(pb[t % 2][:], pb[t % 2][:], over(m.asum[:, c], MEM), ALU.mult).then_inc(pn_done, 1)
            for sem in (kt_ev[0], s_pev, s_oev):
                dve.sem_inc(sem, 1)

            def keys(n):
                dve.wait_ge(s_sc, n + 1)
                dve.tensor_copy(qs[:, :, 0:LS], qt[:, :, bass.ds(n * LS + SEQ, LS)]).then_inc(cq_done, 1)
                for k in range(0, 4, 2):
                    t, j = divmod(k, 2)
                    dve.wait_ge(kt_done, n * 4 + k + 1)
                    dve.tensor_copy(skt[:, 4 * j:4 * j + 4, t * P:(t + 1) * P], four(m.bank[0][:])).then_inc(kt_ev[0], 1)

            def maxima(n):
                dve.wait_ge(s_sc, n + 2)
                dve.tensor_reduce(m.wmx[:, 3:4], m.bank[2][:, :MEM], AX.X, ALU.max).then_inc(s_rl, 1)
                dve.wait_ge(s_rl, n * 2 + 1)
                dve.tensor_scalar(m.wmx[:, 0:1], m.wmx[:, 3:4], -SC, None, ALU.mult).then_inc(s_mx, 1)

            def outputs(n):
                dve.wait_ge(s_pt, n + 2)
                dve.wait_ge(s_o, n + 1)
                dve.tensor_copy(ps[:], m.bank[4][:, :2 * P].rearrange("p (k n) -> p k n", k=2)).then_inc(s_pev, 1)
                dve.wait_ge(s_ex, n + 2)
                dve.reciprocal(m.wmx[:, 2:3], m.wmx[:, 1:2]).then_inc(s_rl, 1)
                dve.wait_ge(s_rl, n * 2 + 2)
                dve.wait_ge(s_o, n + 2)
                dve.tensor_scalar(so[:], m.bank[6][:, :MD], m.wmx[:, 2:3], None, ALU.mult).then_inc(so_done, 1)
                dve.wait_ge(st_done, n + 1)
                for k in range(2):
                    dve.tensor_copy(m.ht[:, k::2, bass.ds(n * LS + SEQ, LS)],
                                    m.bank[7][:, k * P:(k + 1) * P].rearrange("p (h n) -> p h n", h=MH)[:, :, 0:LS]).then_inc(s_oev, 1)

            keys(0)
            with dve.Fori(0, NB - 1) as i:
                maxima(i)
                keys(i + 1)
                outputs(i)
            maxima(NB - 1)
            outputs(NB - 1)


def project_back(nc, m, a):
    residual(nc, m, "back", a["w_mo"], None, None)


CONST = {}
_at = 0
for _n, _w in (("iota", P), ("pairs", NPT), ("key4", NG), ("key8", EPG), ("by64", 8), ("ids", NE), ("evens", NPT - 1),
               ("ovs", OV), ("ovpairs", NOVP), ("valid", NT), ("token", NT), ("before", NE * NE)):
    CONST[_n] = slice(_at, _at + _w)
    _at += _w
NCONST = _at


def route(nc, m, a):
    xs = m.at("moe_rows", m.Z, [NT, D])
    k0 = m.W
    cst = m.at("route_const", k0, [NCONST])
    wr = m.at("router_w", m.WH, [C8, NG + NE])
    tri = m.at("earlier", m.WH + 512, [P])
    ones = m.at("ones", m.WH + 640, [P])
    big = m.at("route_big", m.WH + 768, [1024])
    sa = [m.at(f"slot_onehot{k}", m.WH + 1792 + 640 * k, [NT, P]) for k in range(2)]
    pbt = [m.at(f"pair_onehot{k}", m.WH + 3072 + 128 * k, [NT, NPT]) for k in range(2)]
    mk = [m.at(f"expert_mask{k}", m.WH + 3328 + 160 * k, [NT, NE]) for k in range(3)]
    rk = m.at("ranks", m.WH + 3808, [NT, NE])
    tmp = m.at("route_tmp", m.WH + 3968, [NT, NE])
    lgt = m.at("logits", m.WH + 4128, [NT, NG + NE])
    bias = m.at("router_bias", m.WH + 4312, [NG + NE])
    f = m.at("route_small", m.WH + 4352, [40, 8])
    e4 = [m.at(f"route_e{k}", m.WH + 4672 + 40 * k, [NT, 8]) for k in range(6)]
    cv = [m.at(f"route_v{k}", m.WH + 4912 + 32 * k, [NE]) for k in range(4)]
    S = m.sem
    consts, sq_done, var_done, rstd_done, xs_done = S("ro_consts"), S("ro_sq"), S("ro_var"), S("ro_rstd"), S("ro_rows")
    turned, ht_done, lg_done = S("ro_turned"), S("ro_ht"), S("ro_logits")
    exp_in, exp_out, mask_done, rank_done, oh_done, ix_done = (S("ro_exp_in"), S("ro_exp_out"), S("ro_masks"),
                                                              S("ro_ranks"), S("ro_onehots"), S("ro_index"))
    ch, stores, ones_done = S("ro_chain"), S("ro_stores"), S("ro_ones")
    C = lambda n: cst[:, CONST[n]]
    v = lambda k: f[:, k, 0:NT]
    widths = [rows(t) for t in range(NT)]

    with nc.Block() as block:
        @block.sync
        def _(sp):
            w = wr[:].rearrange("p c n -> p c n")
            sp.dma_start(cst[:], a["c_route"]).then_inc(consts, 16)
            sp.dma_start(tri[:], a["c_tri"]).then_inc(consts, 16)
            sp.dma_start(w[:, :, 0:NG], a["w_router_group"].rearrange("a (p c) g -> p (a c) g", p=P)).then_inc(consts, 16)
            for g in range(NG):
                sp.dma_start(w[:, :, NG + EPG * g:NG + EPG * (g + 1)],
                             a["w_router_expert"][0, g].rearrange("(p c) e -> p c e", p=P)).then_inc(consts, 16)
            sp.dma_start(bias[:, 0:NG], a["b_router_group"].partition_broadcast(P).rearrange("p a g -> p (a g)")).then_inc(consts, 16)
            sp.dma_start(bias[:, NG:], a["b_router_expert"].partition_broadcast(P).rearrange("p a g e -> p (a g e)")).then_inc(consts, 16)
            for t in range(NT):
                sp.wait_ge(xs_done, t + 1)
                sp.dma_start(m.rows_dram[t * P:t * P + rows(t), :], xs[:rows(t), t, :]).then_inc(stores, 16)
            sp.wait_ge(stores, 16 * NT)

        @block.gpsimd
        def _(pool):
            pool.memset(ones[:], 1.0).then_inc(ones_done, 1)
            for t, r in enumerate(widths):
                pool.wait_ge(sq_done, t + 1)
                pool.tensor_scalar(m.stat[:r, 8 + t:9 + t], m.stat[:r, t:t + 1], 1.0 / D, EPS, ALU.mult, ALU.add).then_inc(var_done, 1)
                pool.wait_ge(var_done, t + 1)
                pool.tensor_tensor(m.stat[:r, 16 + t:17 + t], m.stat[:r, 8 + t:9 + t], m.neghalf[:r, 0:1], ALU.pow).then_inc(rstd_done, 1)

        @block.scalar
        def _(act):
            for t, r in enumerate(widths):
                act.activation(xs[:r, t, :], m.x[:r, t, :], ACT.Square, accum_out=m.stat[:r, t:t + 1]).then_inc(sq_done, 1)
                act.wait_ge(rstd_done, t + 1)
                act.activation(xs[:r, t, :], m.x[:r, t, :], ACT.Copy, scale=m.stat[:r, 16 + t:17 + t]).then_inc(xs_done, 1)
            act.wait_ge(exp_in, 1)
            act.activation(e4[0][:, :, 0:NG], e4[0][:, :, 0:NG], ACT.Exp).then_inc(exp_out, 1)
            act.wait_ge(exp_in, 2)
            act.activation(v(2), v(2), ACT.Exp).then_inc(exp_out, 1)

        @block.tensor
        def _(pe):
            for t, r in enumerate(widths):
                pe.wait_ge(xs_done, t + 1)
                for j in range(2):
                    if t:
                        pe.wait_ge(ht_done, 2 * t - 1 + j)
                    for c in range(4):
                        last = pe.transpose(m.bank[4 + j][:, c * P:c * P + r], xs[:r, t, :].rearrange("n (p c) -> n c p", c=C8)[:, 4 * j + c, :], m.ident[:r, :r])
                    last.then_inc(turned, 1)
            pe.wait_ge(consts, 16 * 9)
            for t, r in enumerate(widths):
                pe.wait_ge(ht_done, 2 * t + 2)
                for c in range(C8):
                    last = pe.matmul(m.bank[0][:r, 64 * t:64 * t + NG + NE], m.ht[:, c, tcol(t)], wr[:, c, :],
                                     start=(c == 0), stop=(c == C8 - 1))
            last.then_inc(lg_done, 1)
            pe.wait_ge(mask_done, 1)
            pe.wait_ge(ones_done, 1)
            for t in range(NT):
                o = m.bank[1][:, NE * t:NE * (t + 1)]
                for u in range(t):
                    pe.matmul(o, ones[:], mk[2][:, u, :], start=(u == 0), stop=False)
                pe.matmul(o, tri[:], mk[2][:, t, :], start=(t == 0), stop=True)
            for t in range(NT):
                last = pe.matmul(m.bank[1][:, NE * NT:NE * (NT + 1)], ones[:], mk[2][:, t, :], start=(t == 0), stop=(t == NT - 1))
            last.then_inc(rank_done, 1)
            pe.wait_ge(oh_done, 4)
            for k in range(2):
                for t in range(NT):
                    last = pe.matmul(m.bank[2][:, 0:NPT], sa[k][:, t, :], pbt[k][:, t, :],
                                     start=(k == 0 and t == 0), stop=(k == 1 and t == NT - 1))
            last.then_inc(ix_done, 1)

        @block.vector
        def _(dve):
            link = Chain(dve, ch)
            for t, r in enumerate(widths):
                for j in range(2):
                    dve.wait_ge(turned, 2 * t + j + 1)
                    dve.tensor_tensor(m.ht[:, 4 * j:4 * j + 4, t * P:t * P + r],
                                      m.bank[4 + j][:].rearrange("p (c n) -> p c n", c=4)[:, :, :r],
                                      over(m.g_moe[:, 4 * j:4 * j + 4], r), ALU.mult).then_inc(ht_done, 1)
            link(dve.memset(lgt[:], 0.0))
            dve.wait_ge(lg_done, 1)
            dve.wait_ge(consts, 16 * 9)
            lp = m.bank[0][:, 0:64 * NT].rearrange("p (t n) -> p t n", t=NT)[:, :, 0:NG + NE]
            link(dve.tensor_tensor(lgt[:, 0:NT - 1, :], lp[:, 0:NT - 1, :], across(bias[:], 1, NT - 1), ALU.add))
            link(dve.tensor_tensor(lgt[:NS, NT - 1, :], lp[:NS, NT - 1, :], bias[:NS], ALU.add))

            def first_best(best, x, keys, n, d, onehot):
                link(dve.tensor_reduce(v(best), x, AX.X, ALU.max))
                link(dve.tensor_tensor(d, x, over(v(best), n), ALU.subtract))
                link(dve.scalar_tensor_tensor(onehot, d, 0.0, across(keys, 1, NT), ALU.is_ge, ALU.mult))
                link(dve.tensor_reduce(v(9), onehot, AX.X, ALU.max))
                link(dve.tensor_tensor(onehot, onehot, over(v(9), n), ALU.is_equal))

            d4, og = e4[0][:, :, 0:NG], e4[1][:, :, 0:NG]
            first_best(0, lgt[:, :, 0:NG], C("key4"), NG, d4, og)
            dve.tensor_copy(v(8), v(0)).then_inc(exp_in, 1)
            dve.wait_ge(exp_out, 1)
            link(dve.tensor_reduce(v(1), d4, AX.X, ALU.add))
            link(dve.reciprocal(v(1), v(1)))
            link(dve.tensor_tensor(tmp[:].rearrange("p t (g e) -> p t g e", g=NG),
                                   lgt[:, :, NG:].rearrange("p t (g e) -> p t g e", g=NG), over(og, EPG), ALU.mult))
            sel, d8, o1, o2 = e4[2][:], e4[3][:], e4[4][:], e4[5][:]
            link(dve.tensor_reduce(sel, tmp[:].rearrange("p t (g e) -> p t e g", g=NG), AX.X, ALU.add))
            first_best(3, sel, C("key8"), EPG, d8, o1)
            link(dve.scalar_tensor_tensor(sel, o1, NEG, sel, ALU.mult, ALU.add))
            first_best(4, sel, C("key8"), EPG, d8, o2)
            dve.tensor_tensor(v(2), v(4), v(3), ALU.subtract).then_inc(exp_in, 1)
            dve.wait_ge(exp_out, 2)
            link(dve.tensor_scalar(v(5), v(2), 1.0, None, ALU.add))
            link(dve.reciprocal(v(5), v(5)))
            link(dve.tensor_tensor(m.wt[:, 0, :], v(5), v(1), ALU.mult))
            link(dve.tensor_tensor(m.wt[:, 1, :], m.wt[:, 0, :], v(2), ALU.mult))
            link(dve.tensor_tensor(og, og, over(C("valid"), NG), ALU.mult))
            for k, o in enumerate((o1, o2)):
                link(dve.tensor_tensor(mk[k][:].rearrange("p t (g e) -> p t g e", g=NG), over(og, EPG), across(o, 2, NG), ALU.mult))
            dve.tensor_tensor(mk[2][:], mk[0][:], mk[1][:], ALU.add).then_inc(mask_done, 1)
            dve.wait_ge(rank_done, 1)
            link(dve.tensor_copy(rk[:], m.bank[1][:, 0:NE * NT].rearrange("p (t e) -> p t e", t=NT)))
            cnt, ov, ovb, ove = cv[0][:], cv[1][:], cv[2][:], cv[3][:]
            link(dve.tensor_copy(cnt, m.bank[1][:, NE * NT:NE * (NT + 1)]))
            b8 = big[:, 0:NE * 8].rearrange("p (e j) -> p e j", e=NE)
            link(dve.tensor_tensor(b8, over(cnt, 8), across(C("by64"), 1, NE), ALU.is_gt))
            link(dve.tensor_reduce(ov, b8, AX.X, ALU.add))
            be = big[:].rearrange("p (e j) -> p e j", e=NE)
            link(dve.tensor_tensor(be, across(ov, 1, NE), C("before").rearrange("p (e j) -> p e j", e=NE), ALU.mult))
            link(dve.tensor_reduce(ovb, be, AX.X, ALU.add))
            link(dve.tensor_tensor(ove, ovb, ov, ALU.add))
            for k in range(2):
                r, e, ob, q, tau, pair = 10, 11, 12, 13, 14, 15
                for dst, other in ((r, rk[:]), (e, across(C("ids"), 1, NT)), (ob, across(ovb, 1, NT))):
                    link(dve.tensor_tensor(tmp[:], mk[k][:], other, ALU.mult))
                    link(dve.tensor_reduce(v(dst), tmp[:], AX.X, ALU.add))
                t8 = tmp[:, :, 0:8]
                link(dve.tensor_tensor(t8, over(v(r), 8), across(C("by64"), 1, NT), ALU.is_ge))
                link(dve.tensor_reduce(v(q), t8, AX.X, ALU.add))
                link(dve.scalar_tensor_tensor(v(r), v(q), -float(SLOT), v(r), ALU.mult, ALU.add))
                link(dve.tensor_tensor(v(ob), v(ob), v(q), ALU.add))
                link(dve.scalar_tensor_tensor(v(ob), v(ob), NE - 1.0, v(e), ALU.add, ALU.subtract))
                link(dve.tensor_scalar(v(q), v(q), 1.0, None, ALU.min))
                link(dve.tensor_tensor(v(ob), v(ob), v(q), ALU.mult))
                link(dve.tensor_tensor(v(tau), v(e), v(ob), ALU.add))
                t24 = tmp[:, :, 0:NPT - 1]
                link(dve.tensor_tensor(t24, over(v(tau), NPT - 1), across(C("evens"), 1, NT), ALU.is_ge))
                link(dve.tensor_reduce(v(pair), t24, AX.X, ALU.add))
                link(dve.scalar_tensor_tensor(v(8), v(tau), float(SLOT), v(r), ALU.mult, ALU.add))
                link(dve.tensor_copy(m.place[:, k, :], v(8)))
                link(dve.scalar_tensor_tensor(v(tau), v(pair), -2.0, v(tau), ALU.mult, ALU.add))
                link(dve.scalar_tensor_tensor(v(tau), v(tau), float(SLOT), v(r), ALU.mult, ALU.add))
                dve.tensor_tensor(sa[k][:], across(C("iota"), 1, NT), over(v(tau), P), ALU.is_equal).then_inc(oh_done, 1)
                link(dve.tensor_tensor(pbt[k][:], across(C("pairs"), 1, NT), over(v(pair), NPT), ALU.is_equal))
                dve.tensor_tensor(pbt[k][:], pbt[k][:], over(C("token"), NPT), ALU.mult).then_inc(oh_done, 1)
                dve.wait_ge(oh_done, 2 * k + 2)
            bo = big[0:1, 0:OV * NE].rearrange("p (j e) -> p j e", j=OV)
            link(dve.tensor_tensor(bo, across(ove[0:1], 1, OV), over(C("ovs")[0:1], NE), ALU.is_le))
            eo = big[0:1, 600:600 + OV]
            link(dve.tensor_reduce(eo, bo, AX.X, ALU.add))
            link(dve.tensor_scalar(eo, eo, NE - 1.0, None, ALU.min))
            link(dve.tensor_copy(m.ovexp[0:1, 0:OV], eo))
            np_ = big[0:1, 640:640 + NOVP]
            link(dve.tensor_tensor(np_, ove[0:1, NE - 1:NE].to_broadcast([1, NOVP]), C("ovpairs")[0:1], ALU.is_gt))
            link(dve.tensor_reduce(big[0:1, 660:661], np_, AX.X, ALU.add))
            link(dve.tensor_copy(m.novp[0:1, 0:1], big[0:1, 660:661]))
            dve.wait_ge(ix_done, 1)
            link(dve.tensor_copy(m.idx[:], m.bank[2][:, 0:NPT]))


class ExpertBuffers:
    def __init__(self, m):
        z = m.Z
        e = z + 2 * 12288
        self.gu = [[m.at(f"gate_up{s}{h}", z + 12288 * s + 4096 * h, [2, C8, FE]) for h in range(2)] for s in range(2)]
        self.dn = [[m.at(f"down{s}{h}", z + 12288 * s + 8192 + 2048 * h, [2, D]) for h in range(2)] for s in range(2)]
        self.rows = [m.at(f"slot_rows{s}", e + 1024 * s, [D]) for s in range(2)]
        self.xt = [m.at(f"slot_rows_t{s}", e + 2048 + 1024 * s, [C8, P]) for s in range(2)]
        self.hid = [m.at(f"hidden{s}", e + 4096 + 256 * s, [FE]) for s in range(2)]
        self.sig = [m.at(f"swish{s}", e + 4608 + 256 * s, [FE]) for s in range(2)]
        self.hidt = [m.at(f"hidden_t{s}", e + 5120 + 256 * s, [2, P]) for s in range(2)]
        self.y = [m.at(f"slot_out{s}", e + 5632 + 1024 * s, [D]) for s in range(2)]


def experts(nc, m, a):
    B = ExpertBuffers(m)
    wsrc = [a[n].rearrange("a e (p c) f -> (a e) p c f", p=P) for n in ("w_exp_gate", "w_exp_up")]
    dsrc = a["w_exp_down"].rearrange("a e (p k) d -> (a e) p k d", p=P)
    y_out = m.slots_dram

    def load_weights(sp, s, ids, sem):
        for h in range(2):
            for j in range(2):
                sp.dma_start(B.gu[s][h][:, j], wsrc[j][ids[h]].rearrange("a p c f -> p (a c) f")).then_inc(sem, 16)
            sp.dma_start(B.dn[s][h][:], dsrc[ids[h]].rearrange("a p k d -> p (a k) d")).then_inc(sem, 16)

    for over_tiles in (False, True):
        n_ = "ov_" if over_tiles else "ex_"
        S = lambda n: m.sem(n_ + n)
        w_in, r_in = [S("weights0_in"), S("weights1_in")], [S("rows0_in"), S("rows1_in")]
        xt_done, xt_ev, gu_done, ex_done, hid_done = S("rows_turned"), S("rows_t_stored"), S("gate_up"), S("exped"), S("hidden")
        ht_done, ht_ev, y_done, y_ev, y_out_s = S("hidden_turned"), S("hidden_t_stored"), S("down"), S("out_copied"), S("out_written")
        ch, ix, y_ev2 = S("swish_chain"), S("index_copied"), S("out_copied2")
        four = lambda ap: ap.rearrange("p (c n) -> p c n", c=4)

        def pe_pair(pe, n, s, use):
            pe.wait_ge(r_in[s], use * 16 + 16)
            pe.wait_ge(xt_ev, n * 2 + 1)
            xr = B.rows[s][:].rearrange("p (d c) -> p d c", c=C8)
            for j in range(2):
                for c in range(4):
                    last = pe.transpose(m.bank[j][:, c * P:(c + 1) * P], xr[:, :, 4 * j + c], m.ident[:, :])
                last.then_inc(xt_done, 1)
            pe.wait_ge(w_in[s], use * 96 + 96)
            pe.wait_ge(xt_ev, n * 2 + 2 + 1)
            pe.wait_ge(hid_done, n + 1)
            for c in range(C8):
                for h in range(2):
                    last = pe.matmul(m.bank[2][64 * h:64 * h + 64, :], B.xt[s][:, c, 64 * h:64 * h + 64],
                                     B.gu[s][h][:, :, c, :], start=(c == 0), stop=(c == C8 - 1), skip_group_check=True)
            last.then_inc(gu_done, 1)
            pe.wait_ge(hid_done, n + 2)
            for k in range(2):
                last = pe.transpose(m.bank[3][:, k * P:(k + 1) * P],
                                    B.hid[s][:].rearrange("p (f k) -> p f k", k=2)[:, :, k], m.ident[:, :])
            last.then_inc(ht_done, 1)
            pe.wait_ge(ht_ev, n + 1)
            pe.wait_ge(y_ev, n + 1)
            pe.wait_ge(y_ev2, n + 1)
            for j in range(2):
                for k in range(2):
                    for h in range(2):
                        last = pe.matmul(m.bank[4 + j][64 * h:64 * h + 64, :], B.hidt[s][:, k, 64 * h:64 * h + 64],
                                         B.dn[s][h][:, k, 512 * j:512 * j + 512], start=(k == 0), stop=(k == 1),
                                         skip_group_check=True)
            last.then_inc(y_done, 1)

        def act_pair(act, n, s, dst):
            act.wait_ge(gu_done, n + 2)
            act.wait_ge(hid_done, n + 1)
            act.activation(B.sig[s][:], m.bank[2][:, 0:FE], ACT.Exp, scale=-1.0).then_inc(ex_done, 1)
            act.wait_ge(y_done, n + 2)
            act.wait_ge(y_out_s, n * 16 + 16)
            act.activation(B.y[s][:, 0:512], m.bank[4][:], ACT.Copy).then_inc(y_ev, 1)
            act.wait_ge(y_ev, n + 2)
            act.wait_ge(y_ev2, n + 2)
            act.dma_start(dst, B.y[s][:]).then_inc(y_out_s, 16)

        def dve_pair(dve, n, s):
            for j in range(2):
                dve.wait_ge(xt_done, n * 2 + 1 + j)
                dve.wait_ge(gu_done, n + 1)
                dve.tensor_tensor(B.xt[s][:, 4 * j:4 * j + 4, :], four(m.bank[j][:]),
                                  over(m.g_moe[:, 4 * j:4 * j + 4], P), ALU.mult).then_inc(xt_ev, 1)
            dve.wait_ge(ex_done, n + 1)
            g = B.sig[s][:]
            dve.tensor_scalar(g, g, 1.0, None, ALU.add).then_inc(ch, 1)
            dve.wait_ge(ch, n * 3 + 1)
            dve.reciprocal(g, g).then_inc(ch, 1)
            dve.wait_ge(ch, n * 3 + 2)
            dve.tensor_tensor(g, g, m.bank[2][:, 0:FE], ALU.mult).then_inc(ch, 1)
            dve.wait_ge(ch, n * 3 + 3)
            dve.wait_ge(ht_done, n + 1)
            dve.tensor_tensor(B.hid[s][:], g, m.bank[2][:, FE:2 * FE], ALU.mult).then_inc(hid_done, 1)
            dve.wait_ge(ht_done, n + 2)
            dve.wait_ge(y_done, n + 1)
            dve.tensor_copy(B.hidt[s][:], m.bank[3][:, 0:2 * P].rearrange("p (k n) -> p k n", k=2)).then_inc(ht_ev, 1)
            dve.wait_ge(y_done, n + 2)
            dve.wait_ge(y_out_s, n * 16 + 16)
            dve.tensor_copy(B.y[s][:, 512:], m.bank[5][:]).then_inc(y_ev2, 1)

        def credit(eng, **of):
            for sem in {"pe": (gu_done, ht_done, y_done), "dve": (xt_ev, hid_done, y_ev2), "act": (y_ev,)}[of["on"]]:
                eng.sem_inc(sem, 1)
            if of["on"] == "act":
                eng.sem_inc(y_out_s, 16)

        if not over_tiles:
            with nc.Block() as block:
                @block.sync
                def _(sp):
                    for s in range(2):
                        load_weights(sp, s, [bass.ds(2 * s + h, 1) for h in range(2)], w_in[s])
                    with sp.Fori(0, NPAIR // 2 - 1) as i:
                        for s in range(2):
                            sp.wait_ge(y_done, i * 2 + s + 2)
                            load_weights(sp, s, [bass.ds(i * 4 + 4 + 2 * s + h, 1) for h in range(2)], w_in[s])

                @block.gpsimd
                def _(pool):
                    for n in range(NPAIR):
                        if n >= 2:
                            pool.wait_ge(xt_done, 2 * n - 2)
                        pool.indirect_dma_start(B.rows[n % 2][:], None, m.rows_dram,
                                                bass.IndirectOffsetOnAxis(m.idx[:, n:n + 1], 0)).then_inc(r_in[n % 2], 16)

                @block.tensor
                def _(pe):
                    credit(pe, on="pe")
                    with pe.Fori(0, NPAIR // 2) as i:
                        for s in range(2):
                            pe_pair(pe, i * 2 + s, s, i)

                @block.scalar
                def _(act):
                    credit(act, on="act")
                    with act.Fori(0, NPAIR // 2) as i:
                        for s in range(2):
                            act_pair(act, i * 2 + s, s, y_out[bass.ds((i * 2 + s) * P, P), :])
                    act.wait_ge(y_out_s, 16 * NPAIR + 16)

                @block.vector
                def _(dve):
                    credit(dve, on="dve")
                    with dve.Fori(0, NPAIR // 2) as i:
                        for s in range(2):
                            dve_pair(dve, i * 2 + s, s)
        else:
            with nc.Block() as block:
                @block.sync
                def _(sp):
                    n = sp.value_load(m.novp[0:1, 0:1], min_val=0, max_val=NOVP)
                    for j in range(NOVP):
                        with sp.If(n > j):
                            if j:
                                sp.wait_ge(y_done, j + 1)
                            ids = [bass.ds(sp.value_load(m.ovexp[0:1, 2 * j + h:2 * j + h + 1], min_val=0, max_val=NE - 1), 1)
                                   for h in range(2)]
                            load_weights(sp, 0, ids, w_in[0])
                        with sp.Else():
                            pass

                @block.gpsimd
                def _(pool):
                    n = pool.value_load(m.novp[0:1, 0:1], min_val=0, max_val=NOVP)
                    for j in range(NOVP):
                        with pool.If(n > j):
                            if j:
                                pool.wait_ge(xt_done, 2 * j)
                            pool.indirect_dma_start(B.rows[0][:], None, m.rows_dram,
                                                    bass.IndirectOffsetOnAxis(m.idx[:, NPAIR + j:NPAIR + j + 1], 0)
                                                    ).then_inc(r_in[0], 16)
                        with pool.Else():
                            pass

                @block.tensor
                def _(pe):
                    credit(pe, on="pe")
                    n = pe.value_load(m.novp[0:1, 0:1], min_val=0, max_val=NOVP)
                    for j in range(NOVP):
                        with pe.If(n > j):
                            pe_pair(pe, j, 0, j)
                        with pe.Else():
                            pass

                @block.scalar
                def _(act):
                    credit(act, on="act")
                    n = act.value_load(m.novp[0:1, 0:1], min_val=0, max_val=NOVP)
                    for j in range(NOVP):
                        with act.If(n > j):
                            act_pair(act, j, 0, y_out[(NPAIR + j) * P:(NPAIR + j + 1) * P, :])
                            act.wait_ge(y_out_s, 16 * (j + 2))
                        with act.Else():
                            pass

                @block.vector
                def _(dve):
                    credit(dve, on="dve")
                    n = dve.value_load(m.novp[0:1, 0:1], min_val=0, max_val=NOVP)
                    for j in range(NOVP):
                        with dve.If(n > j):
                            dve_pair(dve, j, 0)
                        with dve.Else():
                            pass


def combine(nc, m, a):
    got = [[m.at(f"expert_rows{s}{k}", m.Z + 2048 * s + 1024 * k, [D]) for k in range(2)] for s in range(2)]
    arrived, added, stores = [m.sem("co_rows0"), m.sem("co_rows1")], m.sem("co_added"), m.sem("co_stores")
    with nc.Block() as block:
        @block.gpsimd
        def _(pool):
            for t in range(NT):
                r = rows(t)
                if t >= 2:
                    pool.wait_ge(added, 2 * (t - 1))
                for k in range(2):
                    pool.indirect_dma_start(got[t % 2][k][:r], None, m.slots_dram,
                                            bass.IndirectOffsetOnAxis(m.place[:r, k, t:t + 1], 0)).then_inc(arrived[t % 2], 16)

        @block.vector
        def _(dve):
            for t in range(NT):
                r = rows(t)
                dve.wait_ge(arrived[t % 2], 32 * (t // 2 + 1))
                for k in range(2):
                    dve.scalar_tensor_tensor(m.x[:r, t, :], got[t % 2][k][:r], m.wt[:r, k, t:t + 1], m.x[:r, t, :],
                                             ALU.mult, ALU.add).then_inc(added, 1)
                    dve.wait_ge(added, 2 * t + k + 1)

        @block.sync
        def _(sp):
            yp = a["o_yp"].rearrange("a (t p) d -> p (a t) d", p=P)
            for t in range(NT):
                sp.wait_ge(added, 2 * t + 2)
                if t < NT - 1:
                    sp.dma_start(yp[:, t, :], m.x[:, t, :]).then_inc(stores, 16)
                else:
                    sp.dma_start(a["o_ys"].rearrange("b i d -> (b i) d"), m.x[:NS, t, :]).then_inc(stores, 16)
            sp.wait_ge(stores, 16 * NT)


def trunk_step(nc, a):
    with ExitStack() as ctx:
        m = Plan(nc, ctx)
        m.z = [m.at(f"z{i}", m.Z + 2560 * i, [NT, RW]) for i in range(7)]
        m.junk = [m.at(f"normed{i}", m.WH + 4096 + 1024 * i, [D]) for i in range(2)]
        m.ident = m.keep("ident", [P])
        m.scr = m.keep("scr", [1024])
        m.g_mix, m.g_cross, m.g_moe, m.g_mem = (m.keep(n, [C8]) for n in ("g_mix", "g_cross", "g_moe", "g_mem"))
        m.g_qk = [m.keep("g_q", [HD]), m.keep("g_k", [HD])]
        m.g_ret = m.keep("g_ret", [RW])
        m.g_q_mem, m.g_k_mem = m.keep("g_q_mem", [MD]), m.keep("g_k_mem", [MD])
        m.wk, m.wks, m.decay_chunk, m.decay_steps, m.bmask = (m.keep(n, [w]) for n, w in (("wk", H), ("wks", H), ("gc", NP), ("gcs", NP), ("bmask", NB)))
        m.neghalf = m.keep("neghalf", [8])
        m.stat = m.keep("stat", [32])
        m.qms, m.qrs = m.keep("head_sums", [80]), m.keep("head_rstd", [80])
        m.gnm, m.gnv, m.gnr = m.keep("gn_mean", [H]), m.keep("gn_var", [H]), m.keep("gn_rstd", [H])
        m.amx, m.asum, m.wmx = m.keep("att_max", [32]), m.keep("att_sum", [32]), m.keep("win_stat", [4])
        m.state = m.keep("state", [NP, HD])
        m.wt = m.keep("route_w", [2, NT])
        m.place, m.idx = m.keep("place", [2, NT], U32), m.keep("slot_token", [NPT], U32)
        m.ovexp, m.novp = m.keep("overflow_expert", [OV], I32), m.keep("overflow_pairs", [1], I32)
        m.rows_dram = nc.dram_tensor("moe_rows_dram", (T, D), F32).ap()
        m.slots_dram = nc.dram_tensor("slot_out_dram", (NPT * P, D), F32).ap()
        chunks = lambda n: a[n].rearrange("a (p c) -> p (a c)", p=P)
        wide = lambda n: a[n].partition_broadcast(P).rearrange("p a n -> p (a n)")
        m.constant_loads = [
            (m.ident[:], a["c_ident"]), (m.g_mix[:], chunks("g_mix")), (m.g_cross[:], chunks("g_cross")),
            (m.g_moe[:], chunks("g_moe")), (m.g_mem[:], chunks("g_mem")), (m.g_qk[0][:], wide("g_q_att")),
            (m.g_qk[1][:], wide("g_k_att")), (m.g_ret[:], wide("g_ret_out")), (m.g_q_mem[:], wide("g_q_mem")),
            (m.g_k_mem[:], wide("g_k_mem")), (m.wk[:], a["c_wk"]), (m.wks[:], a["c_wks"]), (m.decay_chunk[:], a["c_gc"]),
            (m.decay_steps[:], a["c_gcs"]), (m.bmask[:], a["c_bmask"])]
        stages = (load_constants, project_in, mix_prompt, mix_windows, project_out, project_memory, project_cross,
                  cross_attend, project_back, route, experts, combine)
        for stage in stages:
            stage(nc, m, a)
            if stage in (mix_windows, project_back):
                m.free_sems()


def constants():
    f = np.float32
    i, j = np.arange(P), np.arange(P)
    gamma = 1.0 - 2.0 ** (-5.0 - np.arange(H))
    slope = 2.0 ** (-8.0 * np.arange(1, H + 1) / H)

    def bias(d, window_ok):
        n = sum(((d >= 0) & (d % dil == 0) & (d <= win)).astype(int) for win, dil in PATTERNS)
        n = n * window_ok
        return np.where(n > 0, np.log(np.maximum(n, 1)), 0.0), n > 0

    c = {}
    c["c_ident"] = np.eye(P)
    c["c_tri"] = (i[:, None] < j[None, :])
    d = i[:, None] + (512 - P) - np.arange(512)[None, :]
    logn, ok = bias(d, 1)
    c["c_tab"] = np.stack([np.where(ok, logn - s * d, NEG) for s in slope], axis=1)
    rel = i[None, :] - j[:, None]
    c["c_dm"] = np.stack([np.where(rel >= 0, HD ** -0.5 * g ** np.maximum(rel, 0), 0) for g in gamma], axis=1)
    t = np.arange(NS)
    rel = (t[None, :] - t[:, None])
    same = (t[None, :] // LS == t[:, None] // LS) & (rel >= 0)
    dms = np.zeros((P, H, NS))
    dms[:NS] = np.stack([np.where(same, HD ** -0.5 * g ** np.maximum(rel, 0), 0) for g in gamma], axis=1)
    c["c_dms"] = dms[:NS]
    by_pair = np.stack([np.repeat(gamma[2 * q:2 * q + 2], HD) for q in range(NP)], axis=1)
    c["c_wq"] = (by_pair[:, :, None] ** (i[None, None, :] + 1)).reshape(P, -1)
    c["c_wqs"] = (by_pair[:, :, None] ** (t[None, None, :] % LS + 1)).reshape(P, -1)
    c["c_gc"], c["c_gcs"] = by_pair ** P, by_pair ** LS
    c["c_wk"] = HD ** -0.5 * gamma[None, :] ** (P - 1 - j[:, None])
    c["c_wks"] = HD ** -0.5 * gamma[None, :] ** (LS - 1 - j[:, None] % LS)
    c["c_bmask"] = (j[:, None] // LS == np.arange(NB)[None, :])
    r = np.arange(FAR)
    far = 16 * (r // LS) + r % LS
    near = WBUF - NEAR + 4 * np.arange(P)[None, :] + np.arange(NEAR // P)[:, None]
    key = np.concatenate([far, near.reshape(-1), WBUF + np.arange(2 * NS - LS) - (NS - LS)])
    own = np.concatenate([np.ones(KC * P), (key[KC * P:] >= WBUF) & (key[KC * P:] < WBUF + LS)])
    tab = np.zeros((P, len(key)))
    for h in range(H):
        for s in range(LS):
            d = WBUF + s - key
            logn, ok = bias(d, own)
            tab[32 * (h // 2) + 8 * (h % 2) + s] = np.where(ok, logn - slope[h] * d, NEG)
    c["c_btab"] = tab
    route = np.zeros((P, NCONST))
    put = lambda n, x: route.__setitem__((slice(None), CONST[n]), x)
    put("iota", np.arange(P))
    put("pairs", np.arange(NPT))
    put("key4", NG - np.arange(NG))
    put("key8", EPG - np.arange(EPG))
    put("by64", SLOT * np.arange(1, 9))
    put("ids", np.arange(NE))
    put("evens", 2 * np.arange(1, NPT))
    put("ovs", np.arange(OV))
    put("ovpairs", 2 * np.arange(NOVP))
    tok = np.arange(NT)[None, :] * P + i[:, None]
    put("valid", tok < T)
    put("token", tok * (tok < T))
    e = np.arange(NE)
    put("before", (e[None, :] < e[:, None]).reshape(-1)[None, :])
    c["c_route"] = route
    return {k: np.ascontiguousarray(x, dtype=f) for k, x in c.items()}


_INS = ["x_prompt", "x_sample", "mem_prompt", "state_ret", "cache_win_k", "cache_win_v", "cache_mem_k", "cache_mem_v",
        "g_mix", "w_in", "g_ret_out", "g_q_att", "g_k_att", "w_o", "g_cross", "g_mem", "w_mq", "w_mk", "w_mv",
        "g_q_mem", "g_k_mem", "w_mo", "g_moe", "w_router_group", "b_router_group", "w_router_expert",
        "b_router_expert", "w_exp_gate", "w_exp_up", "w_exp_down"]
_OUTS = [("o_yp", (1, SEQ, D)), ("o_ys", (NB, LS, D)), ("o_rp", (1, 1, H, HD, HD)), ("o_wkp", (1, 1, SEQ, H, HD)),
         ("o_wvp", (1, 1, SEQ, H, HD)), ("o_mk", (1, 1, MEM, MH, MD)), ("o_mv", (1, 1, MEM, MH, MD)),
         ("o_rs", (1, NB, H, HD, HD)), ("o_wks", (1, NB, LS, H, HD)), ("o_wvs", (1, NB, LS, H, HD))]


def kernel(**inputs):
    import concourse.bacc as bacc
    from concourse.bass_utils import run_bass_kernel_spmd

    nc = bacc.Bacc("TRN2", target_bir_lowering=False, num_devices=1)
    arrays, a = {}, {}
    for name, x in [*((n, np.ascontiguousarray(inputs[n])) for n in _INS), *constants().items()]:
        arrays[name] = x
        a[name] = nc.dram_tensor(name, x.shape, F32, kind="ExternalInput").ap()
    for name, shape in _OUTS:
        a[name] = nc.dram_tensor(name, shape, F32, kind="ExternalOutput").ap()
    trunk_step(nc, a)
    got = run_bass_kernel_spmd(nc, [arrays], core_ids=[0]).results[0]
    return tuple(got[name] for name, _ in _OUTS)
```

```python
from contextlib import ExitStack

import numpy as np

import concourse.bass as bass
from concourse import mybir

F32 = mybir.dt.float32
F32R = mybir.dt.float32r
I32 = mybir.dt.int32
U32 = mybir.dt.uint32
ALU = mybir.AluOpType
ACT = mybir.ActivationFunctionType
AX = mybir.AxisListType

P = 128
D = 1024
C8 = D // P
SEQ = 512
NB, LS = 8, 8
NS = NB * LS
T = SEQ + NS
TP = SEQ + P
NT = 5
H, HD = 8, 64
NP = H // 2
RW = H * HD
PAST, WBUF = 4096, 2048
PATTERNS = ((128, 1), (512, 4), (2048, 16))
NEAR = 512
FAR = (WBUF - NEAR) // 16 * LS
KC = (FAR + NEAR) // P
FC = FAR // P
WK = KC * P + NS
MEM, MH, MD = 256, 4, 256
NG, EPG, NE, FE = 4, 8, 32, 256
SLOT = 64
OV = 18
NPAIR, NOVP = NE // 2, OV // 2
NPT = NPAIR + NOVP
EPS = 1e-6
NEG = -1e30


def rows(t):
    return P if t < NT - 1 else NS


def tcol(t):
    return slice(t * P, t * P + rows(t))


class Chain:

    def __init__(self, eng, sem, start=0):
        self.eng, self.sem, self.n = eng, sem, start

    def __call__(self, ins):
        self.n += 1
        ins.then_inc(self.sem, 1)
        self.eng.wait_ge(self.sem, self.n)


class Plan:

    X, HT, HTH, Z, W, WH, SMALL, END = 0, 5120, 10240, 15360, 33280, 41472, 49664, 53200

    def __init__(self, nc, ctx):
        self.nc, self.ctx = nc, ctx
        self.base = 16512
        self.open = []
        self.small = self.SMALL
        self.bank = [ctx.enter_context(nc.psum_tensor(f"bank{i}", [P, 512], F32)) for i in range(8)]
        self.x = self.at("x", self.X, [NT, D])
        self.ht = self.at("ht", self.HT, [C8, TP])

    def at(self, name, word, shape, dt=F32):
        n = int(np.prod(shape))
        assert word + n <= self.END, (name, word, n)
        return self.nc.alloc_sbuf_tensor_at(name, [P, *shape], dt, offset=self.base + 4 * word)

    def keep(self, name, shape, dt=F32):
        t = self.at(name, self.small, shape, dt)
        self.small += (int(np.prod(shape)) + 7) // 8 * 8
        return t

    def sem(self, name):
        self.open.append(self.nc.alloc_semaphore(name=name))
        return self.open[-1]

    def free_sems(self):
        self.nc.clear_and_free_semaphores(self.open)
        self.nc.all_engine_barrier()
        self.open = []


def over(ap, n):
    k = len(ap.shape)
    return ap.unsqueeze(k).to_broadcast([*ap.shape, n])


def across(ap, at, n):
    s = list(ap.shape)
    return ap.unsqueeze(at).to_broadcast(s[:at] + [n] + s[at:])


class Weights:

    def __init__(self, nc, m, name, blocks, at, hi_at):
        self.blocks, self.sent = blocks, 0
        self.w = [m.at(f"{name}_w{i}", at[i], [C8, 512]) for i in range(2)]
        self.lo = [m.at(f"{name}_wl{i}", at[i], [C8, 512], F32R) for i in range(2)]
        self.hi = [m.at(f"{name}_wh{i}", hi_at[i], [C8, 512], F32R) for i in range(2)]
        self.loaded = [nc.alloc_semaphore(name=f"{name}_w_loaded{i}") for i in range(2)]

    def load(self, eng):
        i = self.sent % 2
        eng.dma_start(self.w[i][:], self.blocks[self.sent]).then_inc(self.loaded[i], 16)
        self.sent += 1


def dense(nc, m, name, src, weights, tiles, store, hooks={}, gain=None, widths=None, junk_at=None, arrived=None, later=None):
    nt, nb, BANKS = len(tiles), len(weights.blocks), 4
    hth = m.at(f"{name}_hth", m.HTH, [C8, TP], F32R)
    htl = m.at(f"{name}_htl", m.HT, [C8, TP], F32R)
    w, wl, wh, loaded = weights.w, weights.lo, weights.hi, weights.loaded
    s = lambda n: m.sem(f"{name}_{n}")
    sq_done, var_done, rstd_done, xs_done = s("sq_done"), s("var_done"), s("rstd_done"), s("xs_done")
    turned, ht_done, hth_done, htl_done = s("turned"), s("ht_done"), s("hth_done"), s("htl_done")
    padded = s("padded")
    wh_done, wl_done, mm_done, stored = s("wh_done"), s("wl_done"), s("mm_done"), s("stored")
    normed = src is not None
    if normed:
        junk = [m.at(f"{name}_normed{i}", junk_at + 1024 * i, [D]) for i in range(2)]
    full = lambda n: slice(n * P, (n + 1) * P)

    with nc.Block() as block:
        @block.sync
        def _(sp):
            for b in range(weights.sent, nb):
                if b >= 2:
                    sp.wait_ge(mm_done, (b - 1) * nt)
                weights.load(sp)
            if later is not None:
                later(sp, mm_done)

        @block.gpsimd
        def _(pool):
            if normed:
                for n in range(nt):
                    r = widths[n]
                    pool.wait_ge(sq_done, n + 1)
                    pool.tensor_scalar(m.stat[:r, 8 + n:9 + n], m.stat[:r, n:n + 1], 1.0 / D, EPS,
                                       ALU.mult, ALU.add).then_inc(var_done, 1)
                    pool.wait_ge(var_done, n + 1)
                    pool.tensor_tensor(m.stat[:r, 16 + n:17 + n], m.stat[:r, 8 + n:9 + n],
                                       m.neghalf[:r, 0:1], ALU.pow).then_inc(rstd_done, 1)
            if "gpsimd" in hooks:
                hooks["gpsimd"](pool)

        @block.scalar
        def _(act):
            def norm(n):
                r = widths[n]
                if arrived is not None:
                    arrived(act, n)
                if n >= 2:
                    act.wait_ge(turned, 2 * (n - 1))
                act.activation(junk[n % 2][:r, :], src[:r, n, :], ACT.Square,
                               accum_out=m.stat[:r, n:n + 1]).then_inc(sq_done, 1)
                act.wait_ge(rstd_done, n + 1)
                act.activation(junk[n % 2][:r, :], src[:r, n, :], ACT.Copy,
                               scale=m.stat[:r, 16 + n:17 + n]).then_inc(xs_done, 1)

            def split_w(b):
                act.wait_ge(loaded[b % 2], 16 * (b // 2 + 1))
                if b >= 2:
                    act.wait_ge(mm_done, (b - 1) * nt)
                act.activation(wh[b % 2][:], w[b % 2][:], ACT.Copy).then_inc(wh_done, 1)

            def split_rows(n):
                if normed:
                    act.wait_ge(ht_done, 2 * n + 2)
                elif nt == NT:
                    act.wait_ge(padded, 1)
                act.activation(hth[:, :, full(n)], m.ht[:, :, full(n)], ACT.Copy).then_inc(hth_done, 1)

            def finish(k):
                b, n = divmod(k, nt)
                act.wait_ge(mm_done, k + 1)
                store(act, m.bank[k % BANKS], b, n).then_inc(stored, 1)
                if "scalar" in hooks:
                    hooks["scalar"](act, b, n, stored, k)

            for n in range(2):
                if normed:
                    norm(n)
                if n == 0:
                    split_w(0)
            split_rows(0)
            split_rows(1)
            if normed:
                for n in range(2, min(4, nt)):
                    norm(n)
            for n in range(2, nt):
                split_rows(n)
                if n == nt - 1:
                    split_w(1)
                finish(n - 2)
                if normed and n + 2 < nt:
                    norm(n + 2)
            if nt == 2:
                split_w(1)
            for k in range(nt - 2, nb * nt):
                if k % nt == 0 and nt <= k < (nb - 1) * nt:
                    split_w(k // nt + 1)
                finish(k)

        @block.vector
        def _(dve):
            if nt == NT:
                dve.memset(m.ht[:, :, T:TP], 0.0).then_inc(padded, 1)
                dve.wait_ge(padded, 1)
            if normed and arrived is not None:
                arrived(dve, 0)

            def scale_rows(n):
                r = widths[n]
                for j in range(2):
                    dve.wait_ge(turned, 2 * n + j + 1)
                    dve.tensor_tensor(m.ht[:, 4 * j:4 * j + 4, n * P:n * P + r],
                                      m.bank[4 + j][:].rearrange("p (c n) -> p c n", c=4)[:, :, :r],
                                      over(gain[:, 4 * j:4 * j + 4], r), ALU.mult).then_inc(ht_done, 1)

            def split_rows(n):
                dve.wait_ge(hth_done, n + 1)
                dve.tensor_tensor(htl[:, :, full(n)], m.ht[:, :, full(n)], hth[:, :, full(n)].bitcast(F32),
                                  ALU.subtract).then_inc(htl_done, 1)

            def split_w(b):
                dve.wait_ge(wh_done, b + 1)
                dve.tensor_tensor(wl[b % 2][:], w[b % 2][:], wh[b % 2][:].bitcast(F32),
                                  ALU.subtract).then_inc(wl_done, 1)

            for n in range(2):
                if normed:
                    scale_rows(n)
            split_w(0)
            for n in range(nt):
                if normed and n >= 2:
                    scale_rows(n)
                split_rows(n)
            for b in range(nb):
                if b + 1 < nb:
                    split_w(b + 1)
                if "vector" in hooks:
                    for n in range(nt):
                        hooks["vector"](dve, b, n, stored, b * nt + n)

        @block.tensor
        def _(pe):
            if normed and arrived is not None:
                arrived(pe, 0)

            def turn(n):
                r = widths[n]
                pe.wait_ge(xs_done, n + 1)
                rows_ = junk[n % 2][:r, :].rearrange("n (p c) -> n c p", c=C8)
                for j in range(2):
                    if n:
                        pe.wait_ge(ht_done, 2 * n - 1 + j)
                    for c in range(4):
                        last = pe.transpose(m.bank[4 + j][:, c * P:c * P + r], rows_[:, 4 * j + c, :], m.ident[:r, :r])
                    last.then_inc(turned, 1)

            def product(k):
                b, n = divmod(k, nt)
                if n == 0:
                    pe.wait_ge(wh_done, b + 1)
                    pe.wait_ge(wl_done, b + 1)
                if b == 0:
                    pe.wait_ge(hth_done, n + 1)
                    pe.wait_ge(htl_done, n + 1)
                if k >= BANKS:
                    pe.wait_ge(stored, k - BANKS + 1)
                o = m.bank[k % BANKS][:]
                for c in range(C8):
                    hi, lo = hth[:, c, full(n)], htl[:, c, full(n)]
                    pe.matmul(o, hi, wh[b % 2][:, c, :], start=(c == 0), stop=False)
                    pe.matmul(o, hi, wl[b % 2][:, c, :], start=False, stop=False)
                    last = pe.matmul(o, lo, wh[b % 2][:, c, :], start=False, stop=(c == C8 - 1))
                last.then_inc(mm_done, 1)

            if normed:
                for n in range(nt):
                    turn(n)
                    if n:
                        product(n - 1)
                product(nt - 1)
            for k in range(nt if normed else 0, nb * nt):
                product(k)


def load_constants(nc, m, a):
    with nc.Block() as block:
        zeroed = m.sem("neghalf_set")

        @block.sync
        def _(sp):
            xp = a["x_prompt"].rearrange("a (t p) d -> p (a t) d", p=P)
            for t in range(NT - 1):
                sp.dma_start(m.x[:, t, :], xp[:, t, :]).then_inc(m.rows_in[t], 16)
                if t == 1:
                    m.w_in.load(sp)
            sp.dma_start(m.x[:NS, NT - 1, :], a["x_sample"].rearrange("b i d -> (b i) d")).then_inc(m.rows_in[NT - 1], 16)
            m.w_in.load(sp)

        @block.scalar
        def _(act):
            for n, (dst, src) in enumerate(m.constant_loads):
                act.dma_start(dst, src).then_inc(m.first_in if n < 2 else m.constants_in, 16)

        @block.vector
        def _(dve):
            dve.memset(m.neghalf[:], -0.5).then_inc(zeroed, 1)


def project_in(nc, m, a):
    squared, reduced, rstd = m.sem("qk_squared"), m.sem("qk_reduced"), m.sem("qk_rstd")
    exped, gated, chain_s = m.sem("gate_exped"), m.sem("gate_gated"), m.sem("in_dve_chain")
    varied = m.sem("qk_varied")
    sq = [m.scr[:, 0:512], m.scr[:, 512:1024]]

    def store(act, bank, b, t):
        return act.activation(m.z[b][:rows(t), t, :], bank[:rows(t), :], ACT.Copy)

    def scalar(act, b, t, stored, k):
        r = rows(t)
        if b < 2:
            if k >= 2:
                act.wait_ge(reduced, k - 1)
            act.wait_ge(stored, k + 1)
            act.activation(sq[k % 2][:r, :], m.z[b][:r, t, :], ACT.Square).then_inc(squared, 1)
        elif b == 2:
            if k - 2 < 2 * NT:
                act.wait_ge(reduced, 2 * NT)
            else:
                act.wait_ge(gated, k - 2 * NT - 1)
            act.wait_ge(stored, k + 1)
            act.activation(sq[k % 2][:r, :], m.z[2][:r, t, :], ACT.Exp, scale=-1.0).then_inc(exped, 1)

    chain = []

    def vector(dve, b, t, stored, k):
        if not chain:
            chain.append(Chain(dve, chain_s))
            dve.wait_ge(m.constants_in, 16 * (len(m.constant_loads) - 2))
        link, r = chain[0], rows(t)
        heads = lambda ap: ap.rearrange("p (h d) -> p h d", h=H)
        z = m.z[b][:r, t, :]
        if b < 2:
            dve.wait_ge(squared, k + 1)
            dve.tensor_reduce(m.qms[:r, 8 * k:8 * k + 8], heads(sq[k % 2][:r, :]), AX.X, ALU.add).then_inc(reduced, 1)
            dve.wait_ge(rstd, k + 1)
            link(dve.tensor_tensor(heads(z), heads(z), over(m.qrs[:r, 8 * k:8 * k + 8], HD), ALU.mult))
            link(dve.tensor_tensor(heads(z), heads(z), across(m.g_qk[b][:r, :], 1, H), ALU.mult))
        elif b == 2:
            e = sq[k % 2][:r, :]
            dve.wait_ge(exped, k - 2 * NT + 1)
            link(dve.tensor_scalar(e, e, 1.0, None, ALU.add))
            link(dve.reciprocal(e, e))
            link(dve.tensor_tensor(e, e, m.g_ret[:r, :], ALU.mult))
            dve.tensor_tensor(z, z, e, ALU.mult).then_inc(gated, 1)
            dve.wait_ge(gated, k - 2 * NT + 1)

    def gpsimd(pool):
        for k in range(2 * NT):
            r = rows(k % NT)
            c = slice(8 * k, 8 * k + 8)
            pool.wait_ge(reduced, k + 1)
            pool.tensor_scalar(m.qrs[:r, c], m.qms[:r, c], 1.0 / HD, EPS, ALU.mult, ALU.add).then_inc(varied, 1)
            pool.wait_ge(varied, k + 1)
            pool.tensor_tensor(m.qrs[:r, c], m.qrs[:r, c], m.neghalf[:r, 0:8], ALU.pow).then_inc(rstd, 1)

    def arrived(eng, n):
        if eng is nc.scalar:
            eng.wait_ge(m.rows_in[n], 16)
        else:
            eng.wait_ge(m.first_in, 32)

    dense(nc, m, "in", m.x, m.w_in, range(NT), store, {"scalar": scalar, "vector": vector, "gpsimd": gpsimd},
          m.g_mix, [rows(t) for t in range(NT)], m.Z + 6 * NT * RW, arrived)


def mix_prompt(nc, m, a):
    QA, KA, GR, QR, KR, VR, VA = range(7)
    tr = [m.at(n, m.W + i * NP * T, [NP, T]) for i, n in enumerate(("qr_t", "kr_t", "qa_t", "ka_t"))]
    qr_t, kr_t, qa_t, ka_t = tr
    m.qa_t, m.ka_t = qa_t, ka_t
    w0 = m.W + 4 * NP * T
    tab = m.at("tab", w0, [H, 512])
    dm = m.at("dm", w0 + 4096, [H, P])
    sb = [m.at(f"scored{i}", w0 + 5120 + 512 * i, [512]) for i in range(2)]
    pt = [m.at(f"probs_t{i}", w0 + 6144 + 512 * i, [512]) for i in range(2)]
    h0 = m.HTH
    pb = [m.at(f"probs{i}", h0 + 512 * i, [512]) for i in range(2)]
    sd = m.at("decayed", h0 + 1024, [H, P])
    qw = m.at("q_weighted", h0 + 2048, [NP, P])
    kw = m.at("k_weighted", h0 + 2560, [RW])
    cc = m.at("centred", h0 + 3072, [RW])
    sq = m.at("centred_sq", h0 + 3584, [RW])
    ot = [m.at(f"out_rows{i}", h0 + 4096 + 512 * i, [RW]) for i in range(2)]
    s0 = m.at("state_in", m.Z, [NP, NB * HD])
    vx = [m.at(f"v_spread{i}", m.Z + 2560 * i + 2048, [NB * HD]) for i in range(2)]
    s1 = m.at("state_out", m.Z + 2560, [NP, NB * HD])
    z3 = m.Z + QR * 2560
    dms = m.at("dms", z3, [H, NS])
    qws = m.at("qs_weighted", z3 + 512, [NP, NS])
    ots = m.at("os_t", z3 + 768, [NP, NS])
    wq, wqs = m.scr[:, 0:512], m.scr[:, 512:768]
    st = m.state
    z = m.z
    S = m.sem
    tabs_in, dms_in, state_in = S("tabs_in"), S("dms_in"), S("state_in")
    tr_done, tev = S("tr_done"), [S("tr_stored_even"), S("tr_stored_odd")]
    sc_done, sd_done, qw_done, kw_done = S("ret_scored"), S("ret_decayed"), S("q_weighted"), S("k_weighted")
    o_done, kv_done, st_done, gn_c = S("ret_out"), S("kv_out"), S("state_done"), S("gn_centred")
    gn_sq, gn_red, gn_var, gn_rstd = S("gn_squared"), S("gn_reduced"), S("gn_varied"), S("gn_rstd")
    out_ready, out_turned, out_stored = S("out_ready"), S("out_turned"), S("out_stored")
    vx_done, kvs_done, ots_done, os_done = S("v_spread"), S("kvs_out"), S("os_t_stored"), S("os_turned")
    osT_done = S("os_t_done")
    s1_done = S("state_out_done")
    as_done, sb_done, mx_done, ex_done = S("att_scored"), S("att_biased"), S("att_max"), S("att_exped")
    pt_done, pt_ev, pv_done = S("probs_turned"), S("probs_t_stored"), S("pv_done")
    stores = S("mix_stores")
    ch = S("mix_dve_chain")
    hv = lambda ap, h=H: ap.rearrange("p (h d) -> p h d", h=h)
    AT = [(qb, h) for qb in range(SEQ // P) for h in range(H)]

    with nc.Block() as block:
        @block.sync
        def _(sp):
            n = 0
            sp.dma_start(tab[:], a["c_tab"]).then_inc(tabs_in, 16)
            sp.dma_start(dm[:], a["c_dm"]).then_inc(tabs_in, 16)
            sp.dma_start(wq, a["c_wq"]).then_inc(tabs_in, 16)
            sp.dma_start(wqs, a["c_wqs"]).then_inc(tabs_in, 16)
            for src, dst_p, dst_s in ((KA, "o_wkp", "o_wks"), (VA, "o_wvp", "o_wvs")):
                sp.dma_start(a[dst_p].rearrange("a b (t p) h d -> p (a b t) (h d)", p=P),
                             z[src][:, 0:NT - 1, :]).then_inc(stores, 16)
                sp.dma_start(a[dst_s].rearrange("a b i h d -> (a b i) (h d)"), z[src][:NS, NT - 1, :]).then_inc(stores, 16)
                n += 32
            sp.wait_ge(stores, n)
            sp.wait_ge(tev[0], 10)
            sp.wait_ge(tev[1], 10)
            sp.dma_start(dms[:NS], a["c_dms"]).then_inc(dms_in, 16)
            src = a["state_ret"].rearrange("a b (q e) d f -> e q d (a b) f", e=2)
            for e in range(2):
                for q in range(NP):
                    sp.dma_start(s0[64 * e:64 * e + 64, q, :].rearrange("d (b f) -> d b f", b=NB),
                                 src[e, q]).then_inc(state_in, 16)
            sp.wait_ge(st_done, SEQ // P)
            dst = a["o_rp"].rearrange("a b (q e) d f -> e d (a b q) f", e=2)
            for e in range(2):
                sp.dma_start(dst[e], st[64 * e:64 * e + 64]).then_inc(stores, 16)
                n += 16
            sp.wait_ge(s1_done, NP)
            dst = a["o_rs"].rearrange("a b (q e) d f -> e q d (a b) f", e=2)
            for e in range(2):
                for q in range(NP):
                    sp.dma_start(dst[e, q], s1[64 * e:64 * e + 64, q, :].rearrange("d (b f) -> d b f", b=NB)
                                 ).then_inc(stores, 16)
                    n += 16
            sp.wait_ge(stores, n)

        @block.tensor
        def _(pe):
            for k in range(20):
                j, t = divmod(k, NT)
                r = rows(t)
                if k >= 2:
                    pe.wait_ge(tev[k % 2], k // 2)
                for p in range(NP):
                    last = pe.transpose(m.bank[k % 2][:, p * P:p * P + r],
                                        z[(QR, KR, QA, KA)[j]][:r, t, p * P:(p + 1) * P], m.ident[:r, :r])
                last.then_inc(tr_done, 1)
            pe.wait_ge(tev[0], 10)
            pe.wait_ge(tev[1], 10)

            def turn_out(i, r):
                pe.wait_ge(out_ready, i + 1)
                if i:
                    pe.wait_ge(out_stored, i)
                for c in range(4):
                    last = pe.transpose(m.bank[6][:, c * P:c * P + r], ot[i % 2][:r, c * P:(c + 1) * P],
                                        m.ident[:r, :r])
                last.then_inc(out_turned, 1)

            def half(ap, h):
                return ap[64 * (h % 2):64 * (h % 2) + 64]

            for n in range(SEQ // P):
                tc = slice(n * P, (n + 1) * P)
                for j in range(2):
                    if n:
                        pe.wait_ge(sd_done, 2 * n - 1 + j)
                    for h in range(j, H, 2):
                        last = pe.matmul(m.bank[2 + j][:, (h // 2) * P:(h // 2 + 1) * P],
                                         half(kr_t, h)[:, h // 2, tc], half(qr_t, h)[:, h // 2, tc],
                                         start=True, stop=True)
                    last.then_inc(sc_done, 1)
                pe.wait_ge(kw_done, n + 1)
                if n:
                    pe.wait_ge(st_done, n)
                    pe.wait_ge(gn_c, n)
                for h in range(H):
                    last = pe.matmul(half(m.bank[5], h)[:, (h // 2) * HD:(h // 2 + 1) * HD],
                                     kw[:, h * HD:(h + 1) * HD], z[VR][:, n, h * HD:(h + 1) * HD],
                                     start=True, stop=True)
                last.then_inc(kv_done, 1)
                pe.wait_ge(sd_done, 2 * n + 2)
                if n:
                    pe.wait_ge(qw_done, n)
                for h in range(H):
                    o = m.bank[(4, 7)[h % 2]][:, (h // 2) * HD:(h // 2 + 1) * HD]
                    last = pe.matmul(o, sd[:, h, :], z[VR][:, n, h * HD:(h + 1) * HD], start=True, stop=(n == 0))
                    if n:
                        last = pe.matmul(o, half(qw, h)[:, h // 2, :], half(st, h)[:, h // 2, :], start=False, stop=True)
                last.then_inc(o_done, 1)
                if n:
                    turn_out(n - 1, P)
            turn_out(3, P)

            sc = slice(SEQ, T)
            for h in range(H):
                last = pe.matmul(m.bank[2 + h % 2][:NS, (h // 2) * NS:(h // 2 + 1) * NS], half(kr_t, h)[:, h // 2, sc],
                                 half(qr_t, h)[:, h // 2, sc], start=True, stop=True)
            last.then_inc(sc_done, 1)
            pe.wait_ge(sd_done, 2 * 4 + 2)
            pe.wait_ge(qw_done, 4)
            pe.wait_ge(state_in, 16 * H)
            pe.wait_ge(gn_c, 4)
            for h in range(H):
                o = half(m.bank[4], h)[:, (h // 2) * NS:(h // 2 + 1) * NS]
                pe.matmul(o, z[VR][:NS, NT - 1, h * HD:(h + 1) * HD], sd[:NS, h, :NS], start=True, stop=True)
                o = half(m.bank[h % 2], h)[:, (h // 2) * NS:(h // 2 + 1) * NS]
                for b in range(NB):
                    last = pe.matmul(o[:, LS * b:LS * b + LS], half(s0, h)[:, h // 2, b * HD:(b + 1) * HD],
                                     half(qws, h)[:, h // 2, LS * b:LS * b + LS], start=True, stop=True)
            last.then_inc(osT_done, 1)
            pe.wait_ge(kw_done, 5)
            for h in range(H):
                q = h // 2
                if q >= 2 and h % 2 == 0:
                    pe.wait_ge(s1_done, q - 1)
                pe.wait_ge(vx_done, h + 1)
                last = pe.matmul(half(m.bank[(5, 7)[q % 2]], h)[:, :], kw[:NS, h * HD:(h + 1) * HD], vx[h % 2][:NS, :],
                                 start=True, stop=True)
                last.then_inc(kvs_done, 1)
            pe.wait_ge(ots_done, 3)
            for q in range(NP):
                last = pe.transpose(m.bank[3][:NS, q * P:(q + 1) * P], ots[:, q, :], m.ident[:, :])
            last.then_inc(os_done, 1)

            def scores(k):
                qb, h = AT[k]
                n = (qb + 1) * P
                if k >= 2:
                    pe.wait_ge(sb_done, k - 1)
                pe.matmul(m.bank[k % 2][:, :n], half(qa_t, h)[:, h // 2, qb * P:(qb + 1) * P],
                          half(ka_t, h)[:, h // 2, :n], start=True, stop=True).then_inc(as_done, 1)

            def probs_v(k):
                qb, h = AT[k]
                pe.wait_ge(pt_ev, k + 1)
                if h == 0 and qb >= 2:
                    pe.wait_ge(out_ready, qb + 4)
                if k == 0:
                    pe.wait_ge(gn_c, 5)
                    pe.wait_ge(ots_done, 3)
                for j in range(qb + 1):
                    last = pe.matmul(m.bank[4 + qb % 2][:, h * HD:(h + 1) * HD], pt[k % 2][:, j * P:(j + 1) * P],
                                     z[VA][:, j, h * HD:(h + 1) * HD], start=(j == 0), stop=(j == qb))
                last.then_inc(pv_done, 1)

            scores(0)
            for k, (qb, h) in enumerate(AT):
                if k + 1 < len(AT):
                    scores(k + 1)
                if k:
                    probs_v(k - 1)
                pe.wait_ge(ex_done, k + 1)
                if k >= 2:
                    pe.wait_ge(pt_ev, k - 1)
                if k == 0:
                    pe.wait_ge(sd_done, 10)
                    pe.wait_ge(gn_c, 5)
                for j in range(qb + 1):
                    last = pe.transpose(m.bank[2 + k % 2][:, j * P:(j + 1) * P], pb[k % 2][:, j * P:(j + 1) * P], m.ident[:, :])
                last.then_inc(pt_done, 1)
                if k == 4:
                    turn_out(4, NS)
                if h == 4 and qb:
                    turn_out(4 + qb, P)
            probs_v(len(AT) - 1)
            turn_out(8, P)

        @block.scalar
        def _(act):
            def store_turned(k):
                t = k % NT
                act.wait_ge(tr_done, k + 1)
                act.activation(tr[k // NT][:, :, tcol(t)],
                               m.bank[k % 2][:].rearrange("p (c n) -> p c n", c=4)[:, :, :rows(t)], ACT.Copy).then_inc(tev[1], 1)

            def store_out(i, t, off):
                act.wait_ge(out_turned, i + 1)
                act.activation(m.ht[:, off:off + 4, tcol(t)],
                               m.bank[6][:].rearrange("p (c n) -> p c n", c=4)[:, :, :rows(t)], ACT.Copy).then_inc(out_stored, 1)

            def square(i, r):
                act.wait_ge(gn_c, i + 1)
                if i:
                    act.wait_ge(gn_red, i)
                act.activation(sq[:r, :], cc[:r, :], ACT.Square).then_inc(gn_sq, 1)

            for k in range(1, 20, 2):
                store_turned(k)
            for n in range(4):
                square(n, P)
                store_out(n, n, 0)
            act.wait_ge(osT_done, 1)
            act.activation(ots[:], m.bank[4][:, :NP * NS].rearrange("p (q n) -> p q n", q=NP), ACT.Copy).then_inc(ots_done, 1)
            square(4, NS)

            def exps(k):
                n = (AT[k][0] + 1) * P
                act.wait_ge(mx_done, k + 1)
                if k >= 2:
                    act.wait_ge(pt_done, k - 1)
                act.activation(pb[k % 2][:, :n], sb[k % 2][:, :n], ACT.Exp, bias=m.amx[:, k:k + 1],
                               accum_out=m.asum[:, k:k + 1]).then_inc(ex_done, 1)

            for k, (qb, h) in enumerate(AT):
                exps(k)
                if k:
                    i, n = k - 1, (AT[k - 1][0] + 1) * P
                    act.wait_ge(pt_done, i + 1)
                    if i >= 2:
                        act.wait_ge(pv_done, i - 1)
                    act.activation(pt[i % 2][:, :n], m.bank[2 + i % 2][:, :n], ACT.Copy).then_inc(pt_ev, 1)
                if k == 5:
                    store_out(4, 4, 0)
                if h == 5 and qb:
                    store_out(4 + qb, qb - 1, 4)
            i = len(AT) - 1
            act.wait_ge(pt_done, i + 1)
            act.wait_ge(pv_done, i - 1)
            act.activation(pt[i % 2][:], m.bank[2 + i % 2][:], ACT.Copy).then_inc(pt_ev, 1)
            store_out(8, 3, 4)

        @block.gpsimd
        def _(pool):
            pool.wait_ge(tabs_in, 64)
            pool.wait_ge(tev[0], 10)
            pool.wait_ge(tev[1], 10)

            def norm(i, r):
                pool.wait_ge(gn_red, i + 1)
                pool.tensor_scalar(m.gnr[:r, :], m.gnv[:r, :], 1.0 / HD, EPS, ALU.mult, ALU.add).then_inc(gn_var, 1)
                pool.wait_ge(gn_var, i + 1)
                pool.tensor_tensor(m.gnr[:r, :], m.gnr[:r, :], m.neghalf[:r, 0:8], ALU.pow).then_inc(gn_rstd, 1)

            for n in range(4):
                if n:
                    pool.wait_ge(kv_done, n)
                pool.tensor_tensor(hv(kw[:]), hv(z[KR][:, n, :]), over(m.wk[:, :], HD), ALU.mult).then_inc(kw_done, 1)
                if n:
                    pool.wait_ge(o_done, n)
                    pool.tensor_tensor(qw[:], qr_t[:, :, n * P:(n + 1) * P], hv(wq, NP), ALU.mult).then_inc(qw_done, 1)
                norm(n, P)
            pool.wait_ge(kv_done, 4)
            pool.wait_ge(dms_in, 16)
            pool.tensor_tensor(qws[:], qr_t[:, :, SEQ:T], hv(wqs, NP), ALU.mult).then_inc(qw_done, 1)
            pool.tensor_tensor(hv(kw[:NS]), hv(z[KR][:NS, NT - 1, :]), over(m.wks[:NS, :], HD), ALU.mult).then_inc(kw_done, 1)
            for h in range(H):
                if h >= 2:
                    pool.wait_ge(kvs_done, h - 1)
                pool.tensor_tensor(hv(vx[h % 2][:NS]), across(z[VR][:NS, NT - 1, h * HD:(h + 1) * HD], 1, NB),
                                   over(m.bmask[:NS, :], HD), ALU.mult).then_inc(vx_done, 1)
            norm(4, NS)

        @block.vector
        def _(dve):
            link = Chain(dve, ch)
            for k in range(0, 20, 2):
                t = k % NT
                dve.wait_ge(tr_done, k + 1)
                dve.tensor_copy(tr[k // NT][:, :, tcol(t)],
                                m.bank[k % 2][:].rearrange("p (c n) -> p c n", c=4)[:, :, :rows(t)]).then_inc(tev[0], 1)
            dve.wait_ge(tabs_in, 64)

            def group_norm(i, t, o):
                r = rows(t)
                for e in range(2):
                    link(dve.tensor_reduce(m.gnm[:r, e::2], o[e], AX.X, ALU.add))
                link(dve.tensor_scalar(m.gnm[:r, :], m.gnm[:r, :], -1.0 / HD, None, ALU.mult))
                link(dve.tensor_tensor(hv(cc[:r])[:, 0::2], o[0], over(m.gnm[:r, 0::2], HD), ALU.add))
                dve.tensor_tensor(hv(cc[:r])[:, 1::2], o[1], over(m.gnm[:r, 1::2], HD), ALU.add).then_inc(gn_c, 1)
                dve.wait_ge(gn_sq, i + 1)
                dve.tensor_reduce(m.gnv[:r, :], hv(sq[:r]), AX.X, ALU.add).then_inc(gn_red, 1)
                dve.wait_ge(gn_rstd, i + 1)
                link(dve.tensor_tensor(hv(cc[:r]), hv(cc[:r]), over(m.gnr[:r, :], HD), ALU.mult))
                if i >= 2:
                    dve.wait_ge(out_turned, i - 1)
                dve.tensor_tensor(ot[i % 2][:r], cc[:r], z[GR][:r, t, :], ALU.mult).then_inc(out_ready, 1)

            for n in range(4):
                for j in range(2):
                    dve.wait_ge(sc_done, 2 * n + j + 1)
                    if n:
                        dve.wait_ge(o_done, n)
                    dve.tensor_tensor(sd[:, j::2, :], hv(m.bank[2 + j][:], 4), dm[:, j::2, :],
                                      ALU.mult).then_inc(sd_done, 1)
                dve.wait_ge(kv_done, n + 1)
                dve.wait_ge(o_done, n + 1)
                kv = hv(m.bank[5][:, :NP * HD], NP)
                if n == 0:
                    dve.tensor_copy(st[:], kv).then_inc(st_done, 1)
                else:
                    link(dve.tensor_tensor(st[:], st[:], over(m.decay_chunk[:, :], HD), ALU.mult))
                    dve.tensor_tensor(st[:], st[:], kv, ALU.add).then_inc(st_done, 1)
                group_norm(n, n, [hv(m.bank[k][:, :NP * HD], NP) for k in (4, 7)])
            dve.wait_ge(dms_in, 16)
            dve.wait_ge(sc_done, 9)
            dve.wait_ge(o_done, 4)
            for j in range(2):
                dve.tensor_tensor(sd[:NS, j::2, :NS], hv(m.bank[2 + j][:NS, :NP * NS], NP), dms[:NS, j::2, :],
                                  ALU.mult).then_inc(sd_done, 1)
            dve.wait_ge(ots_done, 1)
            for e in range(2):
                dve.tensor_tensor(ots[64 * e:64 * e + 64], ots[64 * e:64 * e + 64],
                                  m.bank[e][64 * e:64 * e + 64, :NP * NS].rearrange("p (q n) -> p q n", q=NP),
                                  ALU.add).then_inc(ots_done, 1)
            dve.wait_ge(state_in, 16 * H)
            for q in range(NP):
                dve.wait_ge(kvs_done, 2 * q + 2)
                link(dve.tensor_scalar(s1[:, q, :], s0[:, q, :], m.decay_steps[:, q:q + 1], None, ALU.mult))
                dve.tensor_tensor(s1[:, q, :], s1[:, q, :], m.bank[(5, 7)[q % 2]][:], ALU.add).then_inc(s1_done, 1)
            dve.wait_ge(os_done, 1)
            os_ = m.bank[3][:NS].rearrange("p (q e d) -> p e q d", e=2, d=HD)
            group_norm(4, 4, [os_[:, 0], os_[:, 1]])

            def out_rows(qb):
                i = 5 + qb
                dve.wait_ge(pv_done, 8 * qb + 8)
                link(dve.reciprocal(m.asum[:, 8 * qb:8 * qb + 8], m.asum[:, 8 * qb:8 * qb + 8]))
                dve.wait_ge(out_turned, i - 1)
                dve.tensor_tensor(hv(ot[i % 2][:]), hv(m.bank[4 + qb % 2][:]), over(m.asum[:, 8 * qb:8 * qb + 8], HD),
                                  ALU.mult).then_inc(out_ready, 1)

            for k, (qb, h) in enumerate(AT):
                n = (qb + 1) * P
                dve.wait_ge(as_done, k + 1)
                if k >= 2:
                    dve.wait_ge(ex_done, k - 1)
                dve.scalar_tensor_tensor(sb[k % 2][:, :n], m.bank[k % 2][:, :n], HD ** -0.5, tab[:, h, 512 - n:],
                                         ALU.mult, ALU.add).then_inc(sb_done, 1)
                dve.wait_ge(sb_done, k + 1)
                dve.tensor_reduce(m.amx[:, k:k + 1], sb[k % 2][:, :n], AX.X, ALU.max, negate=True).then_inc(mx_done, 1)
                if h == 2 and qb:
                    out_rows(qb - 1)
            out_rows(3)


def mix_windows(nc, m, a):
    qa_t, ka_t = m.qa_t, m.ka_t
    kv = [m.at(f"{n}_half{i}", m.Z + 2560 * j, [KC // 2, RW])
          for j, (n, i) in enumerate((("k", 0), ("k", 1), ("v", 0), ("v", 1)))]
    k_half, v_half = kv[:2], kv[2:]
    kt = m.at("window_k_t", m.Z + 4 * 2560, [NP, KC * P])
    btab = m.at("window_tab", m.W, [KC * P + 2 * NS - LS])
    pb = m.at("window_probs", m.W + 1408, [WK])
    pt = m.at("window_probs_t", m.W + 2752, [KC + 1, P])
    sb = m.at("window_scored", m.HTH, [WK])
    qb_all = m.at("q_blocks", m.HTH + 1344, [NB, NP, 32])
    qb = m.at("q_block", m.HTH + 2368, [NP, 32])
    va = m.z[6]
    ow = m.at("window_out", m.HTH + 3600, [P])
    ow_done, ot_done = m.sem("window_out_normed"), m.sem("window_out_turned")
    zero = m.at("zero_rows", m.HTH + 2560, [D])
    S = m.sem
    zero_done, zero_out = S("zero_rows_done"), S("zero_rows_out")
    tab_in, qz, qb_done = S("window_tab_in"), S("q_blocks_zeroed"), S("q_block_done")
    kin, vin = [S("k_half0_in"), S("k_half1_in")], [S("v_half0_in"), S("v_half1_in")]
    kt_done, kt_ev = S("window_k_turned"), [S("k_t_stored_even"), S("k_t_stored_odd")]
    ws_done, sb_done, mx_done, ex_done = (S("window_scored"), S("window_biased"), S("window_max"), S("window_exped"))
    rl = S("window_recip")
    pt_done, pt_ev, pv_done, o_ev = S("window_p_turned"), S("window_p_stored"), S("window_pv"), S("window_out")
    ck, cv = a["cache_win_k"], a["cache_win_v"]
    HC = KC // 2
    far = [c.rearrange("a b (c g r) h d -> (a b) g r c (h d)", g=16, r=16) for c in (ck, cv)]
    near = [c[:, :, WBUF - NEAR:].rearrange("a b (p c) h d -> (a b) p c (h d)", p=P) for c in (ck, cv)]
    out4 = lambda e: m.ht[64 * e:64 * e + 64, 4:8, :]

    with nc.Block() as block:
        @block.sync
        def _(sp):
            sp.dma_start(btab[:], a["c_btab"]).then_inc(tab_in, 16)

            def far_rows(dst, src, b, c0, n, sem):
                for c in range(n):
                    sp.dma_start(dst[:, c, :], src[b, :, 0:LS, c0 + c, :].rearrange("a g r n -> (a g) r n")
                                 ).then_inc(sem, 16)

            def load(b, is_v):
                half, sems = (v_half, vin) if is_v else (k_half, kin)
                i = bass.ds(b, 1)
                far_rows(half[0], far[is_v], i, 0, HC, sems[0])
                return half, sems, i

            def second(half, sems, i, is_v):
                far_rows(half[1], far[is_v], i, HC, FC - HC, sems[1])
                sp.dma_start(half[1][:, FC - HC:, :], near[is_v][i].rearrange("a p c n -> (a p) c n")).then_inc(sems[1], 16)

            def keys(n):
                sp.wait_ge(kt_done, n * KC - KC + HC + 1)
                half, sems, i = load(n, 0)
                sp.wait_ge(kt_done, n * KC + 1)
                second(half, sems, i, 0)

            def values(n):
                sp.wait_ge(pv_done, n + 1)
                second(*load(n, 1), 1)

            second(*load(0, 0), 0)
            second(*load(0, 1), 1)
            keys(1)
            with sp.Fori(0, NB - 2) as i:
                keys(i + 2)
                values(i + 1)
            values(NB - 1)
            m.w_o.load(sp)

        @block.vector
        def _(dve):
            for sem in (sb_done, kt_ev[0], o_ev):
                dve.sem_inc(sem, 1)
            dve.memset(zero[:], 0.0).then_inc(zero_done, 1)
            dve.memset(qb_all[:], 0.0).then_inc(qz, 1)
            dve.wait_ge(qz, 1)
            for e in range(2):
                for q in range(NP):
                    dve.tensor_copy(qb_all[64 * e:64 * e + 64, :, q, 8 * e:8 * e + 8],
                                    qa_t[64 * e:64 * e + 64, q, SEQ:T].rearrange("p (b i) -> p b i", b=NB)).then_inc(qz, 1)
            dve.wait_ge(qz, 1 + 2 * NP)
            dve.wait_ge(tab_in, 16)

            def keys(n):
                for c in range(0, KC, 2):
                    dve.wait_ge(kt_done, n * KC + c + 2)
                    if c == 0:
                        dve.wait_ge(ws_done, n * 3 + 1)
                    dve.tensor_copy(kt[:, :, c * P:(c + 1) * P], m.bank[0][:].rearrange("p (q n) -> p q n", q=NP)
                                    ).then_inc(kt_ev[0], 1)
                dve.tensor_copy(qb[:], qb_all[:, bass.ds(n, 1)].rearrange("p a q n -> p (a q) n")).then_inc(qb_done, 1)

            def biased(n):
                dve.wait_ge(ex_done, n + 1)
                for j, lo in enumerate((0, 512)):
                    dve.wait_ge(ws_done, n * 3 + j + 2)
                    dve.scalar_tensor_tensor(sb[:, lo:lo + 512], m.bank[2 + j][:], HD ** -0.5, btab[:, lo:lo + 512],
                                             ALU.mult, ALU.add).then_inc(sb_done, 1)
                k = KC * P - 1024
                dve.wait_ge(ws_done, n * 3 + 4)
                dve.scalar_tensor_tensor(sb[:, 1024:KC * P], m.bank[4][:, :k], HD ** -0.5, btab[:, 1024:KC * P],
                                         ALU.mult, ALU.add).then_inc(sb_done, 1)
                dve.scalar_tensor_tensor(sb[:, KC * P:], m.bank[4][:, k:k + NS], HD ** -0.5,
                                         btab[:, bass.ds((n * -1 + (NB - 1)) * LS + KC * P, NS)],
                                         ALU.mult, ALU.add).then_inc(sb_done, 1)
                dve.wait_ge(sb_done, n * 4 + 5)
                dve.tensor_reduce(m.wmx[:, 0:1], sb[:], AX.X, ALU.max, negate=True).then_inc(mx_done, 1)

            def outputs(n):
                dve.wait_ge(pt_done, n * 3 + 3)
                dve.wait_ge(pv_done, n + 1)
                dve.tensor_copy(pt[:, 4:8, :], m.bank[6][:].rearrange("p (c n) -> p c n", c=4)).then_inc(pt_ev, 1)
                dve.wait_ge(ex_done, n + 2)
                dve.reciprocal(m.wmx[:, 2:3], m.wmx[:, 1:2]).then_inc(rl, 1)
                dve.wait_ge(rl, n + 1)
                dve.wait_ge(pv_done, n + 2)
                dve.tensor_scalar(ow[:], m.bank[1][:, 0:P], m.wmx[:, 2:3], None, ALU.mult).then_inc(ow_done, 1)
                dve.wait_ge(ot_done, n + 1)
                for e in range(2):
                    dve.tensor_copy(out4(e)[:, :, bass.ds(n * LS + SEQ, LS)],
                                    m.bank[1][64 * e:64 * e + 64, P:2 * P].rearrange("p (q n) -> p q n", q=NP)[:, :, 8 * e:8 * e + 8]
                                    ).then_inc(o_ev, 1)

            keys(0)
            with dve.Fori(0, NB - 1) as i:
                biased(i)
                keys(i + 1)
                outputs(i)
            biased(NB - 1)
            outputs(NB - 1)

        @block.scalar
        def _(act):
            for sem in (kt_ev[1], pt_ev, ex_done):
                act.sem_inc(sem, 1)
            act.wait_ge(zero_done, 1)
            for n in range(NPAIR, NPT):
                act.dma_start(m.slots_dram[n * P:(n + 1) * P, :], zero[:]).then_inc(zero_out, 16)

            def keys(n):
                for c in range(1, KC, 2):
                    act.wait_ge(kt_done, n * KC + c + 2)
                    if c == 1:
                        act.wait_ge(ws_done, n * 3 + 1)
                    act.activation(kt[:, :, c * P:(c + 1) * P], m.bank[7][:].rearrange("p (q n) -> p q n", q=NP),
                                   ACT.Copy).then_inc(kt_ev[1], 1)

            def exps(n):
                act.wait_ge(mx_done, n + 1)
                act.wait_ge(pt_done, n * 3 + 1)
                act.activation(pb[:], sb[:], ACT.Exp, bias=m.wmx[:, 0:1], accum_out=m.wmx[:, 1:2]).then_inc(ex_done, 1)

            def turned(n):
                act.wait_ge(pt_done, n * 3 + 2)
                act.wait_ge(pv_done, n + 1)
                act.activation(pt[:, 0:4, :], m.bank[5][:].rearrange("p (c n) -> p c n", c=4), ACT.Copy).then_inc(pt_ev, 1)
                act.wait_ge(pt_done, n * 3 + 4)
                act.activation(pt[:, 8:10, :], m.bank[2][:, 0:256].rearrange("p (c n) -> p c n", c=2), ACT.Copy).then_inc(pt_ev, 1)
                act.activation(pt[:NS, 10, :], m.bank[2][:NS, 256:384], ACT.Copy).then_inc(pt_ev, 1)

            keys(0)
            with act.Fori(0, NB - 1) as i:
                exps(i)
                keys(i + 1)
                turned(i)
            exps(NB - 1)
            turned(NB - 1)
            act.wait_ge(zero_out, 16 * NOVP)

        @block.tensor
        def _(pe):
            for sem in (ws_done, pt_done, pv_done, kt_done):
                pe.sem_inc(sem, 1)

            def keys(n):
                for c in range(KC):
                    if c == 0:
                        pe.wait_ge(kin[0], (n + 1) * (16 * HC))
                    if c == HC:
                        pe.wait_ge(kin[1], (n + 1) * (16 * (FC - HC + 1)))
                    pe.wait_ge(kt_ev[c % 2], n * HC + c // 2 + 1)
                    for q in range(NP):
                        last = pe.transpose(m.bank[(0, 7)[c % 2]][:, q * P:(q + 1) * P],
                                            k_half[c // HC][:, c % HC, q * P:(q + 1) * P], m.ident[:, :])
                    last.then_inc(kt_done, 1)

            def scores(n):
                pe.wait_ge(qb_done, n + 1)
                pe.wait_ge(pt_ev, n * 4 + 1)
                pe.wait_ge(sb_done, n * 4 + 1)
                for j, (lo, k) in enumerate(((0, 512), (512, 512), (1024, KC * P - 1024))):
                    for par in range(2):
                        pe.wait_ge(kt_ev[par], n * HC + ((lo + k) // P + 1 - par) // 2 + 1)
                    for q in range(NP):
                        last = pe.matmul(m.bank[2 + j][32 * q:32 * q + 32, :k], qb[:, q, :], kt[:, q, lo:lo + k],
                                         start=True, stop=True)
                    if j == 2:
                        for q in range(NP):
                            last = pe.matmul(m.bank[4][32 * q:32 * q + 32, k:k + NS], qb[:, q, :], ka_t[:, q, SEQ:T],
                                             start=True, stop=True)
                    last.then_inc(ws_done, 1)

            def products(n):
                pe.wait_ge(ex_done, n + 2)
                pe.wait_ge(pt_ev, n * 4 + 1)
                for j in range(3):
                    for c in range(4 * j, min(4 * j + 4, KC)):
                        last = pe.transpose(m.bank[(5, 6, 2)[j]][:, (c - 4 * j) * P:(c - 4 * j + 1) * P],
                                            pb[:, c * P:(c + 1) * P], m.ident[:, :])
                    if j == 2:
                        last = pe.transpose(m.bank[2][:NS, 256:384], pb[:, KC * P:], m.ident[:, :])
                    last.then_inc(pt_done, 1)
                pe.wait_ge(pt_ev, n * 4 + 5)
                pe.wait_ge(o_ev, n * 2 + 1)
                pe.wait_ge(vin[0], (n + 1) * (16 * HC))
                pe.wait_ge(vin[1], (n + 1) * (16 * (FC - HC + 1)))
                for c in range(KC + 1):
                    for q in range(NP):
                        v = v_half[c // HC][:, c % HC, q * P:(q + 1) * P] if c < KC else va[:NS, NT - 1, q * P:(q + 1) * P]
                        p = pt[:, c, 32 * q:32 * q + 32] if c < KC else pt[:NS, KC, 32 * q:32 * q + 32]
                        last = pe.matmul(m.bank[1][32 * q:32 * q + 32, 0:P], p, v, start=(c == 0), stop=(c == KC),
                                         skip_group_check=True)
                last.then_inc(pv_done, 1)

            def turn_out(n):
                pe.wait_ge(ow_done, n + 1)
                pe.transpose(m.bank[1][:, P:2 * P], ow[:], m.ident[:, :]).then_inc(ot_done, 1)

            keys(0)
            scores(0)
            with pe.Fori(0, NB - 1) as i:
                keys(i + 1)
                products(i)
                scores(i + 1)
                turn_out(i)
            products(NB - 1)
            turn_out(NB - 1)


def project_out(nc, m, a):
    m.mem_in = m.sem("mem_in")

    def later(sp, mm_done):
        sp.dma_start(m.mem_rows[:], a["mem_prompt"].rearrange("a (t p) d -> p (a t) d", p=P)).then_inc(m.mem_in, 16)
        sp.wait_ge(mm_done, NT)
        m.w_mem.load(sp)

    residual(nc, m, "wo", m.w_o, m.Z, later)


def residual(nc, m, name, weights, rows_at, later):
    res = m.sem(f"{name}_added")
    st = [m.at(f"{name}_rows{i}", rows_at + 512 * i, [512]) for i in range(2)]

    def store(act, bank, b, t):
        k = b * NT + t
        if k >= 2:
            act.wait_ge(res, k - 1)
        return act.activation(st[k % 2][:rows(t), :], bank[:rows(t), :], ACT.Copy)

    def vector(dve, b, t, stored, k):
        dve.wait_ge(stored, k + 1)
        x = m.x[:rows(t), t, 512 * b:512 * b + 512]
        dve.tensor_tensor(x, x, st[k % 2][:rows(t), :], ALU.add).then_inc(res, 1)

    dense(nc, m, name, None, weights, range(NT), store, {"vector": vector}, later=later)


def project_memory(nc, m, a):
    mk = m.at("mem_k", m.Z + 5120, [2, D])
    mv = m.at("mem_v", m.Z + 7168, [2, D])
    m.mem_k, m.mem_v = mk, mv
    dsts = [mk, mk, mv, mv]
    store = lambda act, bank, b, t: act.activation(dsts[b][:, t, 512 * (b % 2):512 * (b % 2) + 512], bank[:], ACT.Copy)
    hooks = wide_norm(nc, m, "mem", [(0, 2), (1, 2)], mk, m.g_k_mem, 2, [P, P])
    arrived = lambda eng, n: eng.wait_ge(m.mem_in, 16)

    def later(sp, mm_done):
        for b in range(2):
            sp.wait_ge(mm_done, 2 * (b + 3))
            m.w_mq.load(sp)

    dense(nc, m, "mem", m.mem_rows, m.w_mem, range(2), store, hooks, m.g_mem, [P, P], m.Z + 10240, arrived, later)


def wide_norm(nc, m, name, blocks, dst, gain, nt, widths):
    squared, reduced, rstd, varied, ch = (m.sem(f"{name}_hsq"), m.sem(f"{name}_hred"), m.sem(f"{name}_hrstd"),
                                          m.sem(f"{name}_hvar"), m.sem(f"{name}_hchain"))
    sq = [m.scr[:, 0:512], m.scr[:, 512:1024]]
    hv = lambda ap: ap.rearrange("p (h d) -> p h d", h=2)
    chain = []

    def scalar(act, b, t, stored, k):
        if b < 2:
            if k >= 2:
                act.wait_ge(reduced, k - 1)
            act.wait_ge(stored, k + 1)
            r = widths[t]
            act.activation(sq[k % 2][:r, :], dst[:r, t, 512 * b:512 * b + 512], ACT.Square).then_inc(squared, 1)

    def vector(dve, b, t, stored, k):
        if b < 2:
            if not chain:
                chain.append(Chain(dve, ch))
            r = widths[t]
            z = hv(dst[:r, t, 512 * b:512 * b + 512])
            dve.wait_ge(squared, k + 1)
            dve.tensor_reduce(m.qms[:r, 2 * k:2 * k + 2], hv(sq[k % 2][:r, :]), AX.X, ALU.add).then_inc(reduced, 1)
            dve.wait_ge(rstd, k + 1)
            chain[0](dve.tensor_tensor(z, z, over(m.qrs[:r, 2 * k:2 * k + 2], MD), ALU.mult))
            chain[0](dve.tensor_tensor(z, z, across(gain[:r, :], 1, 2), ALU.mult))

    def gpsimd(pool):
        for k in range(2 * nt):
            r = widths[k % nt]
            c = slice(2 * k, 2 * k + 2)
            pool.wait_ge(reduced, k + 1)
            pool.tensor_scalar(m.qrs[:r, c], m.qms[:r, c], 1.0 / MD, EPS, ALU.mult, ALU.add).then_inc(varied, 1)
            pool.wait_ge(varied, k + 1)
            pool.tensor_tensor(m.qrs[:r, c], m.qrs[:r, c], m.neghalf[:r, 0:2], ALU.pow).then_inc(rstd, 1)

    return {"scalar": scalar, "vector": vector, "gpsimd": gpsimd}


def project_cross(nc, m, a):
    qm = m.at("cross_q", m.Z, [NT, D])
    m.cross_q = qm
    store = lambda act, bank, b, t: act.activation(qm[:rows(t), t, 512 * b:512 * b + 512], bank[:rows(t), :], ACT.Copy)
    widths = [rows(t) for t in range(NT)]
    hooks = wide_norm(nc, m, "cross", None, qm, m.g_q_mem, NT, widths)
    dense(nc, m, "cross", m.x, m.w_mq, range(NT), store, hooks, m.g_cross, widths, m.Z + 10240)


def cross_attend(nc, m, a):
    qm, mk, mv = m.cross_q, m.mem_k, m.mem_v
    qt = m.at("cross_q_t", m.Z + 9216, [C8, T])
    kt = m.at("mem_k_t", m.Z + 9216 + C8 * T, [C8, MEM])
    sk = [m.at(f"cache_k{i}", m.W + 2048 * i, [2, D]) for i in range(2)]
    sv = [m.at(f"cache_v{i}", m.W + 4096 + 2048 * i, [2, D]) for i in range(2)]
    skt = m.at("cache_k_t", m.WH, [C8, MEM])
    pb = [m.at(f"cross_probs{i}", m.WH + 2048 + 1024 * i, [MH, MEM]) for i in range(2)]
    pt = m.at("cross_probs_t", m.WH + 4096, [2 * MH, P])
    spb = [m.at(f"cache_probs{i}", m.WH + 5120 + 256 * i, [MEM]) for i in range(2)]
    S = m.sem
    tr_done, tev = S("cr_turned"), [S("cr_stored_even"), S("cr_stored_odd")]
    sc_done, mx_done, ex_done, pn_done = S("cr_scored"), S("cr_max"), S("cr_exped"), S("cr_normed")
    pt_done, pt_ev, o_done, o_ev = S("cr_p_turned"), S("cr_p_stored"), S("cr_out"), S("cr_out_stored")
    kin, vin = [S("cache_k0_in"), S("cache_k1_in")], [S("cache_v0_in"), S("cache_v1_in")]
    qs = m.at("cache_q", m.WH + 5888, [C8, 32])
    ps = m.at("cache_probs_turned", m.WH + 6144, [2, P])
    so = m.at("cache_out", m.WH + 6400, [MD])
    so_done, st_done = m.sem("cs_out_normed"), m.sem("cs_out_turned")
    cq_done = S("cache_q_done")
    ch, stores = S("cr_chain"), S("cr_stores")
    kt_done, kt_ev = S("ck_turned"), [S("ck_stored_even"), S("ck_stored_odd")]
    s_sc, s_mx, s_ex, s_rl = S("cs_scored"), S("cs_max"), S("cs_exped"), S("cs_recip")
    s_pt, s_pev, s_o, s_oev = S("cs_p_turned"), S("cs_p_stored"), S("cs_out"), S("cs_out_stored")
    ckv = [a[n].rearrange("a b (t p) h d -> p (a b) t (h d)", p=P) for n in ("cache_mem_k", "cache_mem_v")]
    turns = [(qm, qt, t, j) for t in range(NT) for j in range(2)] + [(mk, kt, t, j) for t in range(2) for j in range(2)]
    four = lambda ap: ap.rearrange("p (c n) -> p c n", c=4)
    NQ = NT - 1
    SC = MD ** -0.5

    with nc.Block() as block:
        @block.sync
        def _(sp):
            for src, dst in ((mk, "o_mk"), (mv, "o_mv")):
                sp.dma_start(a[dst].rearrange("a b (t p) h d -> p (a b t) (h d)", p=P), src[:]).then_inc(stores, 16)
            for b in range(2):
                sp.dma_start(sk[b][:], ckv[0][:, b]).then_inc(kin[b], 16)
                sp.dma_start(sv[b][:], ckv[1][:, b]).then_inc(vin[b], 16)
            for par in range(2):
                sp.wait_ge(tev[par], len(turns) // 2)
            m.w_mo.load(sp)
            with sp.Fori(0, NB // 2 - 1) as i:
                for b in range(2):
                    nxt = bass.ds(i * 2 + 2 + b, 1)
                    sp.wait_ge(kt_done, i * 8 + 4 * b + 4)
                    sp.dma_start(sk[b][:], ckv[0][:, nxt].rearrange("p a t n -> p (a t) n")).then_inc(kin[b], 16)
                    sp.wait_ge(s_o, i * 2 + b + 2)
                    sp.dma_start(sv[b][:], ckv[1][:, nxt].rearrange("p a t n -> p (a t) n")).then_inc(vin[b], 16)
            sp.wait_ge(stores, 32)

        @block.tensor
        def _(pe):
            for k, (src, dst, t, j) in enumerate(turns):
                r = rows(t) if src is qm else P
                if k >= 2:
                    pe.wait_ge(tev[k % 2], k // 2)
                for c in range(4):
                    last = pe.transpose(m.bank[k % 2][:, c * P:c * P + r], src[:r, t, (4 * j + c) * P:(4 * j + c + 1) * P], m.ident[:r, :r])
                last.then_inc(tr_done, 1)
            pe.wait_ge(tev[0], len(turns) // 2)
            pe.wait_ge(tev[1], len(turns) // 2)

            def scores(t):
                if t:
                    pe.wait_ge(ex_done, 4 * t)
                for h in range(MH):
                    for k in range(2):
                        last = pe.matmul(m.bank[2 + h // 2][:, (h % 2) * MEM:(h % 2 + 1) * MEM], qt[:, 2 * h + k, tcol(t)],
                                         kt[:, 2 * h + k, :], start=(k == 0), stop=(k == 1))
                last.then_inc(sc_done, 1)

            scores(0)
            for t in range(NQ):
                pe.wait_ge(pn_done, t + 1)
                if t:
                    pe.wait_ge(pt_ev, 2 * t)
                for j in range(2):
                    for c in range(4):
                        h, k = divmod(4 * j + c, 2)
                        last = pe.transpose(m.bank[4 + j][:, c * P:(c + 1) * P], pb[t % 2][:, h, k * P:(k + 1) * P], m.ident[:, :])
                    last.then_inc(pt_done, 1)
                if t + 1 < NQ:
                    scores(t + 1)
                pe.wait_ge(pt_ev, 2 * t + 2)
                if t:
                    pe.wait_ge(o_ev, 2 * t)
                for j in range(2):
                    for c in range(4):
                        h = (4 * j + c) // 2
                        for k in range(2):
                            last = pe.matmul(m.bank[6 + j][:, c * P:(c + 1) * P], mv[:, k, (4 * j + c) * P:(4 * j + c + 1) * P],
                                             pt[:, 2 * h + k, :], start=(k == 0), stop=(k == 1))
                    last.then_inc(o_done, 1)
            pe.wait_ge(o_ev, 2 * NQ)
            pe.wait_ge(ex_done, 4 * NQ)
            for sem in (s_sc, s_pt, s_o):
                pe.sem_inc(sem, 1)

            def keys(n, b, use):
                pe.wait_ge(kin[b], use * 16 + 16)
                for k in range(4):
                    t, j = divmod(k, 2)
                    pe.wait_ge(kt_ev[k % 2], n * 2 + k // 2 + 1)
                    for c in range(4):
                        last = pe.transpose(m.bank[k % 2][:, c * P:(c + 1) * P], sk[b][:, t, (4 * j + c) * P:(4 * j + c + 1) * P], m.ident[:, :])
                    last.then_inc(kt_done, 1)

            def cache_scores(n):
                pe.wait_ge(kt_ev[0], n * 2 + 3)
                pe.wait_ge(kt_ev[1], n * 2 + 3)
                pe.wait_ge(s_ex, n + 1)
                pe.wait_ge(cq_done, n + 2)
                for k in range(2):
                    for h in range(MH):
                        last = pe.matmul(m.bank[2][32 * h:32 * h + 32, :MEM], qs[:, 2 * h + k, :],
                                         skt[:, 2 * h + k, :], start=(k == 0), stop=(k == 1), skip_group_check=True)
                last.then_inc(s_sc, 1)

            def products(n, b, use):
                pe.wait_ge(s_ex, n + 2)
                pe.wait_ge(s_pev, n + 1)
                for k in range(2):
                    last = pe.transpose(m.bank[4][:, k * P:(k + 1) * P], spb[0][:, k * P:(k + 1) * P], m.ident[:, :])
                last.then_inc(s_pt, 1)
                pe.wait_ge(s_pev, n + 2)
                pe.wait_ge(vin[b], use * 16 + 16)
                pe.wait_ge(s_oev, n * 2 + 1)
                for k in range(2):
                    for h in range(MH):
                        last = pe.matmul(m.bank[6][32 * h:32 * h + 32, :MD], ps[:, k, 32 * h:32 * h + 32],
                                         sv[b][:, k, h * MD:(h + 1) * MD], start=(k == 0), stop=(k == 1),
                                         skip_group_check=True)
                last.then_inc(s_o, 1)

            def turn_out(n):
                pe.wait_ge(so_done, n + 1)
                for k in range(2):
                    last = pe.transpose(m.bank[7][:, k * P:(k + 1) * P], so[:, k * P:(k + 1) * P], m.ident[:, :])
                last.then_inc(st_done, 1)

            keys(0, 0, 0)
            cache_scores(0)
            with pe.Fori(0, NB // 2 - 1) as i:
                for b in range(2):
                    keys(i * 2 + b + 1, 1 - b, i + b)
                    products(i * 2 + b, b, i)
                    cache_scores(i * 2 + b + 1)
                    turn_out(i * 2 + b)
            keys(NB - 1, 1, NB // 2 - 1)
            products(NB - 2, 0, NB // 2 - 1)
            cache_scores(NB - 1)
            turn_out(NB - 2)
            products(NB - 1, 1, NB // 2 - 1)
            turn_out(NB - 1)

        def store_turned(copy, eng, k):
            src, dst, t, j = turns[k]
            r = rows(t) if src is qm else P
            eng.wait_ge(tr_done, k + 1)
            copy(dst[:, 4 * j:4 * j + 4, t * P:t * P + r], four(m.bank[k % 2][:])[:, :, :r]).then_inc(tev[k % 2], 1)

        @block.scalar
        def _(act):
            copy = lambda dst, src: act.activation(dst, src, ACT.Copy)
            for k in range(1, len(turns), 2):
                store_turned(copy, act, k)
            for t in range(NQ):
                act.wait_ge(mx_done, t + 1)
                if t >= 2:
                    act.wait_ge(pt_done, 2 * (t - 1))
                for h in range(MH):
                    act.activation(pb[t % 2][:, h, :], m.bank[2 + h // 2][:, (h % 2) * MEM:(h % 2 + 1) * MEM], ACT.Exp,
                                   bias=m.amx[:, 4 * t + h:4 * t + h + 1], scale=SC,
                                   accum_out=m.asum[:, 4 * t + h:4 * t + h + 1]).then_inc(ex_done, 1)
                for j in range(2):
                    act.wait_ge(pt_done, 2 * t + j + 1)
                    if t and j == 0:
                        act.wait_ge(o_done, 2 * t)
                    copy(pt[:, 4 * j:4 * j + 4, :], four(m.bank[4 + j][:])).then_inc(pt_ev, 1)
                for j in range(2):
                    act.wait_ge(o_done, 2 * t + j + 1)
                    copy(m.ht[:, 4 * j:4 * j + 4, tcol(t)], four(m.bank[6 + j][:])).then_inc(o_ev, 1)
            for sem in (kt_ev[1], s_ex):
                act.sem_inc(sem, 1)

            def keys(n):
                act.wait_ge(s_sc, n + 1)
                for k in range(1, 4, 2):
                    t, j = divmod(k, 2)
                    act.wait_ge(kt_done, n * 4 + k + 1)
                    copy(skt[:, 4 * j:4 * j + 4, t * P:(t + 1) * P], four(m.bank[1][:])).then_inc(kt_ev[1], 1)

            def exps(n):
                act.wait_ge(s_mx, n + 1)
                act.wait_ge(s_pt, n + 1)
                act.activation(spb[0][:], m.bank[2][:, :MEM], ACT.Exp, bias=m.wmx[:, 0:1], scale=SC,
                               accum_out=m.wmx[:, 1:2]).then_inc(s_ex, 1)

            keys(0)
            with act.Fori(0, NB - 1) as i:
                exps(i)
                keys(i + 1)
            exps(NB - 1)

        @block.vector
        def _(dve):
            link = Chain(dve, ch)
            dve.memset(qs[:], 0.0).then_inc(cq_done, 1)
            dve.wait_ge(cq_done, 1)
            for k in range(0, len(turns), 2):
                store_turned(dve.tensor_copy, dve, k)
            for t in range(NQ):
                dve.wait_ge(sc_done, t + 1)
                c = slice(4 * t, 4 * t + 4)
                for j in range(2):
                    link(dve.tensor_reduce(m.amx[:, 4 * t + 2 * j:4 * t + 2 * j + 2],
                                           m.bank[2 + j][:].rearrange("p (h n) -> p h n", h=2), AX.X, ALU.max))
                dve.tensor_scalar(m.amx[:, c], m.amx[:, c], -SC, None, ALU.mult).then_inc(mx_done, 1)
                dve.wait_ge(ex_done, 4 * t + 4)
                link(dve.reciprocal(m.asum[:, c], m.asum[:, c]))
                dve.tensor_tensor(pb[t % 2][:], pb[t % 2][:], over(m.asum[:, c], MEM), ALU.mult).then_inc(pn_done, 1)
            for sem in (kt_ev[0], s_pev, s_oev):
                dve.sem_inc(sem, 1)

            def keys(n):
                dve.wait_ge(s_sc, n + 1)
                dve.tensor_copy(qs[:, :, 0:LS], qt[:, :, bass.ds(n * LS + SEQ, LS)]).then_inc(cq_done, 1)
                for k in range(0, 4, 2):
                    t, j = divmod(k, 2)
                    dve.wait_ge(kt_done, n * 4 + k + 1)
                    dve.tensor_copy(skt[:, 4 * j:4 * j + 4, t * P:(t + 1) * P], four(m.bank[0][:])).then_inc(kt_ev[0], 1)

            def maxima(n):
                dve.wait_ge(s_sc, n + 2)
                dve.tensor_reduce(m.wmx[:, 3:4], m.bank[2][:, :MEM], AX.X, ALU.max).then_inc(s_rl, 1)
                dve.wait_ge(s_rl, n * 2 + 1)
                dve.tensor_scalar(m.wmx[:, 0:1], m.wmx[:, 3:4], -SC, None, ALU.mult).then_inc(s_mx, 1)

            def outputs(n):
                dve.wait_ge(s_pt, n + 2)
                dve.wait_ge(s_o, n + 1)
                dve.tensor_copy(ps[:], m.bank[4][:, :2 * P].rearrange("p (k n) -> p k n", k=2)).then_inc(s_pev, 1)
                dve.wait_ge(s_ex, n + 2)
                dve.reciprocal(m.wmx[:, 2:3], m.wmx[:, 1:2]).then_inc(s_rl, 1)
                dve.wait_ge(s_rl, n * 2 + 2)
                dve.wait_ge(s_o, n + 2)
                dve.tensor_scalar(so[:], m.bank[6][:, :MD], m.wmx[:, 2:3], None, ALU.mult).then_inc(so_done, 1)
                dve.wait_ge(st_done, n + 1)
                for k in range(2):
                    dve.tensor_copy(m.ht[:, k::2, bass.ds(n * LS + SEQ, LS)],
                                    m.bank[7][:, k * P:(k + 1) * P].rearrange("p (h n) -> p h n", h=MH)[:, :, 0:LS]).then_inc(s_oev, 1)

            keys(0)
            with dve.Fori(0, NB - 1) as i:
                maxima(i)
                keys(i + 1)
                outputs(i)
            maxima(NB - 1)
            outputs(NB - 1)


def project_back(nc, m, a):
    residual(nc, m, "back", m.w_mo, m.Z + 8192, lambda sp, mm_done: m.experts.load(sp, 1, 1))


NPW = NPT + NPT % 2

CONST = {}
_at = 0
for _n, _w in (("iota", P), ("pairs", NPW), ("key4", NG), ("key8", EPG), ("by64", 8), ("ids", NE), ("evens", NPT - 1),
               ("ovs", OV), ("ovpairs", NOVP), ("valid", NT), ("token", NT), ("before", NE * NE)):
    CONST[_n] = slice(_at, _at + _w)
    _at += _w
NCONST = _at


def route(nc, m, a):
    xs = m.at("moe_rows", m.HTH, [NT, D])
    cst = m.at("route_const", m.experts.END, [NCONST])
    wr = m.at("router_w", m.WH, [C8, NG + NE])
    tri = m.at("earlier", m.WH + 512, [P])
    ones = m.at("ones", m.WH + 640, [P])
    big = m.at("route_big", m.WH + 768, [1024])
    sa = m.at("slot_onehot", m.WH + 1792, [2, NT, P], F32R)
    ph = m.at("pair_onehot", m.WH + 5872, [2, NT, NPW])
    pbt = m.at("pair_token", m.WH + 6144, [2, NT, NPW], F32R)
    mk = m.at("expert_mask", m.WH + 3328, [2, NT, NE])
    both = m.at("expert_chosen", m.WH + 5680, [NT + 1, NE])
    rk = m.at("ranks", m.WH + 3808, [NT, NE])
    tmp = m.at("route_tmp", m.WH + 5360, [2, NT, NE])
    lgt = m.at("logits", m.WH + 4128, [NT, NG + NE])
    bias = m.at("router_bias", m.WH + 4312, [NG + NE])
    f = m.at("route_small", m.WH + 4352, [40, 8])
    e4 = [m.at(f"route_e{k}", m.WH + 4672 + 40 * k, [NT, 8]) for k in range(6)]
    cv = [m.at(f"route_v{k}", m.WH + 4912 + 32 * k, [NE]) for k in range(4)]
    S = m.sem
    consts, sq_done, var_done, rstd_done, xs_done = S("ro_consts"), S("ro_sq"), S("ro_var"), S("ro_rstd"), S("ro_rows")
    turned, ht_done, lg_done = S("ro_turned"), S("ro_ht"), S("ro_logits")
    exp_in, exp_out, mask_done, rank_done, oh_done, ix_done = (S("ro_exp_in"), S("ro_exp_out"), S("ro_masks"),
                                                              S("ro_ranks"), S("ro_onehots"), S("ro_index"))
    ch, stores, ones_done = S("ro_chain"), S("ro_stores"), S("ro_ones")
    C = lambda n: cst[:, CONST[n]]
    v = lambda k: f[:, k, 0:NT]
    v2 = lambda k: f[:, 16 + 2 * k:18 + 2 * k, 0:NT]
    widths = [rows(t) for t in range(NT)]

    with nc.Block() as block:
        @block.sync
        def _(sp):
            w = wr[:].rearrange("p c n -> p c n")
            sp.dma_start(cst[:], a["c_route"]).then_inc(consts, 16)
            sp.dma_start(tri[:], a["c_tri"]).then_inc(consts, 16)
            sp.dma_start(w[:, :, 0:NG], a["w_router_group"].rearrange("a (p c) g -> p (a c) g", p=P)).then_inc(consts, 16)
            for g in range(NG):
                sp.dma_start(w[:, :, NG + EPG * g:NG + EPG * (g + 1)],
                             a["w_router_expert"][0, g].rearrange("(p c) e -> p c e", p=P)).then_inc(consts, 16)
            sp.dma_start(bias[:, 0:NG], a["b_router_group"].partition_broadcast(P).rearrange("p a g -> p (a g)")).then_inc(consts, 16)
            sp.dma_start(bias[:, NG:], a["b_router_expert"].partition_broadcast(P).rearrange("p a g e -> p (a g e)")).then_inc(consts, 16)
            m.experts.load(sp, 0, 0)
            for t in range(NT):
                sp.wait_ge(xs_done, t + 1)
                sp.dma_start(m.rows_dram[t * P:t * P + rows(t), :], xs[:rows(t), t, :]).then_inc(stores, 16)
            sp.wait_ge(stores, 16 * NT)

        @block.gpsimd
        def _(pool):
            pool.memset(ones[:], 1.0).then_inc(ones_done, 1)
            pool.memset(both[:, NT, :], 0.0).then_inc(ones_done, 1)
            for t, r in enumerate(widths):
                pool.wait_ge(sq_done, t + 1)
                pool.tensor_scalar(m.stat[:r, 8 + t:9 + t], m.stat[:r, t:t + 1], 1.0 / D, EPS, ALU.mult, ALU.add).then_inc(var_done, 1)
                pool.wait_ge(var_done, t + 1)
                pool.tensor_tensor(m.stat[:r, 16 + t:17 + t], m.stat[:r, 8 + t:9 + t], m.neghalf[:r, 0:1], ALU.pow).then_inc(rstd_done, 1)

        @block.scalar
        def _(act):
            for t, r in enumerate(widths):
                act.activation(xs[:r, t, :], m.x[:r, t, :], ACT.Square, accum_out=m.stat[:r, t:t + 1]).then_inc(sq_done, 1)
                act.wait_ge(rstd_done, t + 1)
                act.activation(xs[:r, t, :], m.x[:r, t, :], ACT.Copy, scale=m.stat[:r, 16 + t:17 + t]).then_inc(xs_done, 1)
            act.wait_ge(exp_in, 1)
            act.activation(e4[0][:, :, 0:NG], e4[0][:, :, 0:NG], ACT.Exp).then_inc(exp_out, 1)
            act.wait_ge(exp_in, 2)
            act.activation(v(2), v(2), ACT.Exp).then_inc(exp_out, 1)

        @block.tensor
        def _(pe):
            def logits(t):
                if t == 0:
                    pe.wait_ge(consts, 16 * 9)
                pe.wait_ge(ht_done, 2 * t + 2)
                for c in range(C8):
                    for g in range(rows(t) // 64):
                        last = pe.matmul(m.bank[0][64 * g:64 * g + 64, 64 * t:64 * t + NG + NE],
                                         m.ht[:, c, t * P + 64 * g:t * P + 64 * g + 64], wr[:, c, :],
                                         start=(c == 0), stop=(c == C8 - 1), skip_group_check=True)
                return last

            for t, r in enumerate(widths):
                pe.wait_ge(xs_done, t + 1)
                for j in range(2):
                    if t:
                        pe.wait_ge(ht_done, 2 * t - 1 + j)
                    for c in range(4):
                        last = pe.transpose(m.bank[4 + j][:, c * P:c * P + r], xs[:r, t, :].rearrange("n (p c) -> n c p", c=C8)[:, 4 * j + c, :], m.ident[:r, :r])
                    last.then_inc(turned, 1)
                if t:
                    logits(t - 1)
            logits(NT - 1).then_inc(lg_done, 1)
            pe.wait_ge(mask_done, 1)
            pe.wait_ge(ones_done, 2)
            counts = m.bank[1][:, 0:NE * (NT + 1)].rearrange("p (t e) -> p t e", t=NT + 1)
            pe.matmul(counts, ones[:], across(both[:, NT, :], 1, NT + 1), start=True, stop=False)
            for u in range(NT):
                pe.matmul(counts[:, u + 1:, :], ones[:], across(both[:, u, :], 1, NT - u), start=False, stop=False,
                          skip_group_check=True)
            pe.matmul(counts, tri[:], both[:], start=False, stop=True).then_inc(rank_done, 1)
            pe.wait_ge(oh_done, 2)
            for k in range(2):
                for t in range(NT):
                    last = pe.matmul(m.bank[2][:, 0:NPW], sa[:, k, t, :], pbt[:, k, t, :],
                                     start=(k == 0 and t == 0), stop=(k == 1 and t == NT - 1))
            last.then_inc(ix_done, 1)

        @block.vector
        def _(dve):
            link = Chain(dve, ch)
            for t, r in enumerate(widths):
                for j in range(2):
                    dve.wait_ge(turned, 2 * t + j + 1)
                    dve.tensor_tensor(m.ht[:, 4 * j:4 * j + 4, t * P:t * P + r],
                                      m.bank[4 + j][:].rearrange("p (c n) -> p c n", c=4)[:, :, :r],
                                      over(m.g_moe[:, 4 * j:4 * j + 4], r), ALU.mult).then_inc(ht_done, 1)
            link(dve.memset(lgt[:], 0.0))
            dve.wait_ge(lg_done, 1)
            dve.wait_ge(consts, 16 * 9)
            lp = m.bank[0][:, 0:64 * NT].rearrange("p (t n) -> p t n", t=NT)[:, :, 0:NG + NE]
            link(dve.tensor_tensor(lgt[:, 0:NT - 1, :], lp[:, 0:NT - 1, :], across(bias[:], 1, NT - 1), ALU.add))
            link(dve.tensor_tensor(lgt[:NS, NT - 1, :], lp[:NS, NT - 1, :], bias[:NS], ALU.add))

            def first_best(best, x, keys, n, d, onehot):
                link(dve.tensor_reduce(v(best), x, AX.X, ALU.max))
                link(dve.tensor_tensor(d, x, over(v(best), n), ALU.subtract))
                link(dve.scalar_tensor_tensor(onehot, d, 0.0, across(keys, 1, NT), ALU.is_ge, ALU.mult))
                link(dve.tensor_reduce(v(9), onehot, AX.X, ALU.max))
                link(dve.tensor_tensor(onehot, onehot, over(v(9), n), ALU.is_equal))

            d4, og = e4[0][:, :, 0:NG], e4[1][:, :, 0:NG]
            first_best(0, lgt[:, :, 0:NG], C("key4"), NG, d4, og)
            dve.tensor_copy(v(8), v(0)).then_inc(exp_in, 1)
            dve.wait_ge(exp_out, 1)
            link(dve.tensor_reduce(v(1), d4, AX.X, ALU.add))
            link(dve.reciprocal(v(1), v(1)))
            link(dve.tensor_tensor(tmp[:, 0].rearrange("p t (g e) -> p t g e", g=NG),
                                   lgt[:, :, NG:].rearrange("p t (g e) -> p t g e", g=NG), over(og, EPG), ALU.mult))
            sel, d8, o1, o2 = e4[2][:], e4[3][:], e4[4][:], e4[5][:]
            link(dve.tensor_reduce(sel, tmp[:, 0].rearrange("p t (g e) -> p t e g", g=NG), AX.X, ALU.add))
            first_best(3, sel, C("key8"), EPG, d8, o1)
            link(dve.scalar_tensor_tensor(sel, o1, NEG, sel, ALU.mult, ALU.add))
            first_best(4, sel, C("key8"), EPG, d8, o2)
            dve.tensor_tensor(v(2), v(4), v(3), ALU.subtract).then_inc(exp_in, 1)
            dve.wait_ge(exp_out, 2)
            link(dve.tensor_scalar(v(5), v(2), 1.0, None, ALU.add))
            link(dve.reciprocal(v(5), v(5)))
            link(dve.tensor_tensor(m.wt[:, 0, :], v(5), v(1), ALU.mult))
            link(dve.tensor_tensor(m.wt[:, 1, :], m.wt[:, 0, :], v(2), ALU.mult))
            link(dve.tensor_tensor(og, og, over(C("valid"), NG), ALU.mult))
            for k, o in enumerate((o1, o2)):
                link(dve.tensor_tensor(mk[:, k].rearrange("p t (g e) -> p t g e", g=NG), over(og, EPG), across(o, 2, NG), ALU.mult))
            dve.tensor_tensor(both[:, 0:NT], mk[:, 0], mk[:, 1], ALU.add).then_inc(mask_done, 1)
            dve.wait_ge(rank_done, 1)
            link(dve.tensor_copy(rk[:], m.bank[1][:, 0:NE * NT].rearrange("p (t e) -> p t e", t=NT)))
            cnt, ov, ovb, ove = cv[0][:], cv[1][:], cv[2][:], cv[3][:]
            link(dve.tensor_copy(cnt, m.bank[1][:, NE * NT:NE * (NT + 1)]))
            b8 = big[:, 0:NE * 8].rearrange("p (e j) -> p e j", e=NE)
            link(dve.tensor_tensor(b8, over(cnt, 8), across(C("by64"), 1, NE), ALU.is_gt))
            link(dve.tensor_reduce(ov, b8, AX.X, ALU.add))
            be = big[:].rearrange("p (e j) -> p e j", e=NE)
            link(dve.tensor_tensor(be, across(ov, 1, NE), C("before").rearrange("p (e j) -> p e j", e=NE), ALU.mult))
            link(dve.tensor_reduce(ovb, be, AX.X, ALU.add))
            link(dve.tensor_tensor(ove, ovb, ov, ALU.add))
            r, e, ob, q, tau, pair = (v2(k) for k in range(6))
            each = lambda ap: across(across(ap, 1, NT), 1, 2)
            for dst, other in ((r, across(rk[:], 1, 2)), (e, each(C("ids"))), (ob, each(ovb))):
                link(dve.tensor_tensor(tmp[:], mk[:, 0:2], other, ALU.mult))
                link(dve.tensor_reduce(dst, tmp[:], AX.X, ALU.add))
            t8 = tmp[:, :, :, 0:8]
            link(dve.tensor_tensor(t8, over(r, 8), each(C("by64")), ALU.is_ge))
            link(dve.tensor_reduce(q, t8, AX.X, ALU.add))
            link(dve.scalar_tensor_tensor(r, q, -float(SLOT), r, ALU.mult, ALU.add))
            link(dve.tensor_tensor(ob, ob, q, ALU.add))
            link(dve.scalar_tensor_tensor(ob, ob, NE - 1.0, e, ALU.add, ALU.subtract))
            link(dve.tensor_scalar(q, q, 1.0, None, ALU.min))
            link(dve.tensor_tensor(ob, ob, q, ALU.mult))
            link(dve.tensor_tensor(tau, e, ob, ALU.add))
            t24 = tmp[:, :, :, 0:NPT - 1]
            link(dve.tensor_tensor(t24, over(tau, NPT - 1), each(C("evens")), ALU.is_ge))
            link(dve.tensor_reduce(pair, t24, AX.X, ALU.add))
            link(dve.scalar_tensor_tensor(q, tau, float(SLOT), r, ALU.mult, ALU.add))
            link(dve.tensor_copy(m.place[:], q))
            link(dve.scalar_tensor_tensor(tau, pair, -2.0, tau, ALU.mult, ALU.add))
            link(dve.scalar_tensor_tensor(tau, tau, float(SLOT), r, ALU.mult, ALU.add))
            dve.tensor_tensor(sa[:], each(C("iota")), over(tau, P), ALU.is_equal).then_inc(oh_done, 1)
            link(dve.tensor_tensor(ph[:], each(C("pairs")), over(pair, NPW), ALU.is_equal))
            dve.tensor_tensor(pbt[:], ph[:], across(over(C("token"), NPW), 1, 2), ALU.mult).then_inc(oh_done, 1)
            bo = big[0:1, 0:OV * NE].rearrange("p (j e) -> p j e", j=OV)
            link(dve.tensor_tensor(bo, across(ove[0:1], 1, OV), over(C("ovs")[0:1], NE), ALU.is_le))
            eo = big[0:1, 600:600 + OV]
            link(dve.tensor_reduce(eo, bo, AX.X, ALU.add))
            link(dve.tensor_scalar(eo, eo, NE - 1.0, None, ALU.min))
            link(dve.tensor_copy(m.ovexp[0:1, 0:OV], eo))
            np_ = big[0:1, 640:640 + NOVP]
            link(dve.tensor_tensor(np_, ove[0:1, NE - 1:NE].to_broadcast([1, NOVP]), C("ovpairs")[0:1], ALU.is_gt))
            link(dve.tensor_reduce(big[0:1, 660:661], np_, AX.X, ALU.add))
            link(dve.tensor_copy(m.novp[0:1, 0:1], big[0:1, 660:661]))
            dve.wait_ge(ix_done, 1)
            link(dve.tensor_copy(m.idx[:], m.bank[2][:, 0:NPT]))


class Experts:

    def __init__(self, nc, m, a):
        z = m.Z
        e = self.END = z + 2 * 12288
        self.gu = [[m.at(f"gate_up{s}{h}", z + 12288 * s + 4096 * h, [2, C8, FE]) for h in range(2)] for s in range(2)]
        self.dn = [[m.at(f"down{s}{h}", z + 12288 * s + 8192 + 2048 * h, [2, D]) for h in range(2)] for s in range(2)]
        self.rows = [m.at(f"slot_rows{s}", e + 1024 * s, [D]) for s in range(2)]
        self.xt = [m.at(f"slot_rows_t{s}", e + 2048 + 1024 * s, [C8, P]) for s in range(2)]
        self.hid = [m.at(f"hidden{s}", e + 4096 + 256 * s, [FE]) for s in range(2)]
        self.sig = [m.at(f"swish{s}", e + 4608 + 256 * s, [FE]) for s in range(2)]
        self.hidt = [m.at(f"hidden_t{s}", e + 5120 + 256 * s, [2, P]) for s in range(2)]
        self.y = [m.at(f"slot_out{s}", e + 5632 + 1024 * s, [D]) for s in range(2)]
        self.gate_up_src = [a[n].rearrange("a e (p c) f -> (a e) p c f", p=P) for n in ("w_exp_gate", "w_exp_up")]
        self.down_src = a["w_exp_down"].rearrange("a e (p k) d -> (a e) p k d", p=P)
        sems = lambda n: [nc.alloc_semaphore(name=f"expert_{n}{i}_in") for i in range(2)]
        self.gate_up_in, self.down_in = sems("gate_up"), sems("down")

    def load_gate_up(self, sp, s, ids, sem):
        for h in range(2):
            for j in range(2):
                sp.dma_start(self.gu[s][h][:, j], self.gate_up_src[j][ids[h]].rearrange("a p c f -> p (a c) f")).then_inc(sem, 16)

    def load_down(self, sp, s, ids, sem):
        for h in range(2):
            sp.dma_start(self.dn[s][h][:], self.down_src[ids[h]].rearrange("a p k d -> p (a k) d")).then_inc(sem, 16)

    def load(self, sp, s, pair, gate_up_free=None, down_free=None):
        ids = [bass.ds(pair * 2 + h, 1) for h in range(2)]
        if gate_up_free is not None:
            gate_up_free()
        self.load_gate_up(sp, s, ids, self.gate_up_in[s])
        if down_free is not None:
            down_free()
        self.load_down(sp, s, ids, self.down_in[s])


def experts(nc, m, a):
    B = m.experts
    y_out = m.slots_dram

    for over_tiles in (False, True):
        n_ = "ov_" if over_tiles else "ex_"
        S = lambda n: m.sem(n_ + n)
        gate_up_in, down_in = ([S("gate_up_in")], [S("down_in")]) if over_tiles else (B.gate_up_in, B.down_in)
        r_in = [S("rows0_in"), S("rows1_in")]
        xt_done, xt_ev, gu_done, ex_done, hid_done = S("rows_turned"), S("rows_t_stored"), S("gate_up"), S("exped"), S("hidden")
        ht_done, ht_ev, y_done, y_ev, y_out_s = S("hidden_turned"), S("hidden_t_stored"), S("down"), S("out_copied"), S("out_written")
        ch, ix, y_ev2 = S("swish_chain"), S("index_copied"), S("out_copied2")
        four = lambda ap: ap.rearrange("p (c n) -> p c n", c=4)

        def turn_rows(pe, n, s, use):
            pe.wait_ge(r_in[s], use * 16 + 16)
            pe.wait_ge(xt_ev, n * 2 + 1)
            xr = B.rows[s][:].rearrange("p (d c) -> p d c", c=C8)
            for j in range(2):
                for c in range(4):
                    last = pe.transpose(m.bank[j][:, c * P:(c + 1) * P], xr[:, :, 4 * j + c], m.ident[:, :])
                last.then_inc(xt_done, 1)

        def gate_up(pe, n, s, use):
            pe.wait_ge(gate_up_in[s], use * 64 + 64)
            pe.wait_ge(xt_ev, n * 2 + 2 + 1)
            pe.wait_ge(hid_done, n + 1)
            for c in range(C8):
                for h in range(2):
                    last = pe.matmul(m.bank[2][64 * h:64 * h + 64, :], B.xt[s][:, c, 64 * h:64 * h + 64],
                                     B.gu[s][h][:, :, c, :], start=(c == 0), stop=(c == C8 - 1), skip_group_check=True)
            last.then_inc(gu_done, 1)

        def down(pe, n, s, use):
            pe.wait_ge(hid_done, n + 2)
            for k in range(2):
                last = pe.transpose(m.bank[3][:, k * P:(k + 1) * P],
                                    B.hid[s][:].rearrange("p (f k) -> p f k", k=2)[:, :, k], m.ident[:, :])
            last.then_inc(ht_done, 1)
            pe.wait_ge(down_in[s], use * 32 + 32)
            pe.wait_ge(ht_ev, n + 1)
            pe.wait_ge(y_ev, n + 1)
            pe.wait_ge(y_ev2, n + 1)
            for j in range(2):
                for k in range(2):
                    for h in range(2):
                        last = pe.matmul(m.bank[4 + j][64 * h:64 * h + 64, :], B.hidt[s][:, k, 64 * h:64 * h + 64],
                                         B.dn[s][h][:, k, 512 * j:512 * j + 512], start=(k == 0), stop=(k == 1),
                                         skip_group_check=True)
            last.then_inc(y_done, 1)

        def act_pair(act, n, s, dst):
            act.wait_ge(gu_done, n + 2)
            act.wait_ge(hid_done, n + 1)
            act.activation(B.sig[s][:], m.bank[2][:, 0:FE], ACT.Exp, scale=-1.0).then_inc(ex_done, 1)
            act.wait_ge(ht_done, n + 1)
            act.wait_ge(y_done, n + 1)
            act.activation(B.hidt[s][:], m.bank[3][:, 0:2 * P].rearrange("p (k n) -> p k n", k=2), ACT.Copy).then_inc(ht_ev, 1)
            act.wait_ge(y_done, n + 2)
            act.wait_ge(y_out_s, n * 16 + 16)
            act.activation(B.y[s][:, 0:512], m.bank[4][:], ACT.Copy).then_inc(y_ev, 1)
            act.wait_ge(y_ev, n + 2)
            act.wait_ge(y_ev2, n + 2)
            act.dma_start(dst, B.y[s][:]).then_inc(y_out_s, 16)

        def store_rows(dve, n, s):
            for j in range(2):
                dve.wait_ge(xt_done, n * 2 + 1 + j)
                dve.wait_ge(gu_done, n + 1)
                dve.tensor_tensor(B.xt[s][:, 4 * j:4 * j + 4, :], four(m.bank[j][:]),
                                  over(m.g_moe[:, 4 * j:4 * j + 4], P), ALU.mult).then_inc(xt_ev, 1)

        def swish(dve, n, s):
            dve.wait_ge(ex_done, n + 1)
            g = B.sig[s][:]
            dve.tensor_scalar(g, g, 1.0, None, ALU.add).then_inc(ch, 1)
            dve.wait_ge(ch, n * 3 + 1)
            dve.reciprocal(g, g).then_inc(ch, 1)
            dve.wait_ge(ch, n * 3 + 2)
            dve.tensor_tensor(g, g, m.bank[2][:, 0:FE], ALU.mult).then_inc(ch, 1)
            dve.wait_ge(ch, n * 3 + 3)
            dve.tensor_tensor(B.hid[s][:], g, m.bank[2][:, FE:2 * FE], ALU.mult).then_inc(hid_done, 1)

        def store_out(dve, n, s):
            dve.wait_ge(y_done, n + 2)
            dve.wait_ge(y_out_s, n * 16 + 16)
            dve.tensor_copy(B.y[s][:, 512:], m.bank[5][:]).then_inc(y_ev2, 1)

        def credit(eng, **of):
            for sem in {"pe": (gu_done, y_done), "dve": (xt_ev, hid_done, y_ev2), "act": (y_ev,)}[of["on"]]:
                eng.sem_inc(sem, 1)
            if of["on"] == "act":
                eng.sem_inc(y_out_s, 16)

        if not over_tiles:
            with nc.Block() as block:
                @block.sync
                def _(sp):
                    with sp.Fori(0, NPAIR // 2 - 1) as i:
                        for s in range(2):
                            B.load(sp, s, i * 2 + (2 + s), lambda: sp.wait_ge(gu_done, i * 2 + s + 2),
                                   lambda: sp.wait_ge(y_done, i * 2 + s + 2))

                @block.gpsimd
                def _(pool):
                    for n in range(NPAIR):
                        if n >= 2:
                            pool.wait_ge(xt_done, 2 * n - 2)
                        pool.indirect_dma_start(B.rows[n % 2][:], None, m.rows_dram,
                                                bass.IndirectOffsetOnAxis(m.idx[:, n:n + 1], 0)).then_inc(r_in[n % 2], 16)

                @block.tensor
                def _(pe):
                    credit(pe, on="pe")
                    turn_rows(pe, 0, 0, 0)
                    with pe.Fori(0, NPAIR // 2 - 1) as i:
                        for s in range(2):
                            gate_up(pe, i * 2 + s, s, i)
                            turn_rows(pe, i * 2 + (s + 1), 1 - s, i + s)
                            down(pe, i * 2 + s, s, i)
                    use = NPAIR // 2 - 1
                    gate_up(pe, NPAIR - 2, 0, use)
                    turn_rows(pe, NPAIR - 1, 1, use)
                    down(pe, NPAIR - 2, 0, use)
                    gate_up(pe, NPAIR - 1, 1, use)
                    down(pe, NPAIR - 1, 1, use)

                @block.scalar
                def _(act):
                    credit(act, on="act")
                    with act.Fori(0, NPAIR // 2) as i:
                        for s in range(2):
                            act_pair(act, i * 2 + s, s, y_out[bass.ds((i * 2 + s) * P, P), :])
                    act.wait_ge(y_out_s, 16 * NPAIR + 16)

                @block.vector
                def _(dve):
                    credit(dve, on="dve")
                    store_rows(dve, 0, 0)
                    with dve.Fori(0, NPAIR // 2 - 1) as i:
                        for s in range(2):
                            swish(dve, i * 2 + s, s)
                            store_rows(dve, i * 2 + (s + 1), 1 - s)
                            store_out(dve, i * 2 + s, s)
                    swish(dve, NPAIR - 2, 0)
                    store_rows(dve, NPAIR - 1, 1)
                    store_out(dve, NPAIR - 2, 0)
                    swish(dve, NPAIR - 1, 1)
                    store_out(dve, NPAIR - 1, 1)
        else:
            with nc.Block() as block:
                @block.sync
                def _(sp):
                    n = sp.value_load(m.novp[0:1, 0:1], min_val=0, max_val=NOVP)
                    for j in range(NOVP):
                        with sp.If(n > j):
                            if j:
                                sp.wait_ge(y_done, j + 1)
                            ids = [bass.ds(sp.value_load(m.ovexp[0:1, 2 * j + h:2 * j + h + 1], min_val=0, max_val=NE - 1), 1)
                                   for h in range(2)]
                            B.load_gate_up(sp, 0, ids, gate_up_in[0])
                            B.load_down(sp, 0, ids, down_in[0])
                        with sp.Else():
                            pass

                @block.gpsimd
                def _(pool):
                    n = pool.value_load(m.novp[0:1, 0:1], min_val=0, max_val=NOVP)
                    for j in range(NOVP):
                        with pool.If(n > j):
                            if j:
                                pool.wait_ge(xt_done, 2 * j)
                            pool.indirect_dma_start(B.rows[0][:], None, m.rows_dram,
                                                    bass.IndirectOffsetOnAxis(m.idx[:, NPAIR + j:NPAIR + j + 1], 0)
                                                    ).then_inc(r_in[0], 16)
                        with pool.Else():
                            pass

                @block.tensor
                def _(pe):
                    credit(pe, on="pe")
                    n = pe.value_load(m.novp[0:1, 0:1], min_val=0, max_val=NOVP)
                    for j in range(NOVP):
                        with pe.If(n > j):
                            turn_rows(pe, j, 0, j)
                            gate_up(pe, j, 0, j)
                            down(pe, j, 0, j)
                        with pe.Else():
                            pass

                @block.scalar
                def _(act):
                    credit(act, on="act")
                    n = act.value_load(m.novp[0:1, 0:1], min_val=0, max_val=NOVP)
                    for j in range(NOVP):
                        with act.If(n > j):
                            act_pair(act, j, 0, y_out[(NPAIR + j) * P:(NPAIR + j + 1) * P, :])
                            act.wait_ge(y_out_s, 16 * (j + 2))
                        with act.Else():
                            pass

                @block.vector
                def _(dve):
                    credit(dve, on="dve")
                    n = dve.value_load(m.novp[0:1, 0:1], min_val=0, max_val=NOVP)
                    for j in range(NOVP):
                        with dve.If(n > j):
                            store_rows(dve, j, 0)
                            swish(dve, j, 0)
                            store_out(dve, j, 0)
                        with dve.Else():
                            pass


def combine(nc, m, a):
    got = [[m.at(f"expert_rows{s}{k}", m.Z + 2048 * s + 1024 * k, [D]) for k in range(2)] for s in range(2)]
    arrived, added, stores = [m.sem("co_rows0"), m.sem("co_rows1")], m.sem("co_added"), m.sem("co_stores")
    with nc.Block() as block:
        @block.gpsimd
        def _(pool):
            for t in range(NT):
                r = rows(t)
                if t >= 2:
                    pool.wait_ge(added, 2 * (t - 1))
                for k in range(2):
                    pool.indirect_dma_start(got[t % 2][k][:r], None, m.slots_dram,
                                            bass.IndirectOffsetOnAxis(m.place[:r, k, t:t + 1], 0)).then_inc(arrived[t % 2], 16)

        @block.vector
        def _(dve):
            for t in range(NT):
                r = rows(t)
                dve.wait_ge(arrived[t % 2], 32 * (t // 2 + 1))
                for k in range(2):
                    dve.scalar_tensor_tensor(m.x[:r, t, :], got[t % 2][k][:r], m.wt[:r, k, t:t + 1], m.x[:r, t, :],
                                             ALU.mult, ALU.add).then_inc(added, 1)
                    dve.wait_ge(added, 2 * t + k + 1)

        @block.sync
        def _(sp):
            yp = a["o_yp"].rearrange("a (t p) d -> p (a t) d", p=P)
            for t in range(NT):
                sp.wait_ge(added, 2 * t + 2)
                if t < NT - 1:
                    sp.dma_start(yp[:, t, :], m.x[:, t, :]).then_inc(stores, 16)
                else:
                    sp.dma_start(a["o_ys"].rearrange("b i d -> (b i) d"), m.x[:NS, t, :]).then_inc(stores, 16)
            sp.wait_ge(stores, 16 * NT)


def trunk_step(nc, a):
    with ExitStack() as ctx:
        m = Plan(nc, ctx)
        m.z = [m.at(f"z{i}", m.Z + 2560 * i, [NT, RW]) for i in range(7)]
        m.ident = m.keep("ident", [P])
        m.scr = m.keep("scr", [1024])
        m.g_mix, m.g_cross, m.g_moe, m.g_mem = (m.keep(n, [C8]) for n in ("g_mix", "g_cross", "g_moe", "g_mem"))
        m.g_qk = [m.keep("g_q", [HD]), m.keep("g_k", [HD])]
        m.g_ret = m.keep("g_ret", [RW])
        m.g_q_mem, m.g_k_mem = m.keep("g_q_mem", [MD]), m.keep("g_k_mem", [MD])
        m.wk, m.wks, m.decay_chunk, m.decay_steps, m.bmask = (m.keep(n, [w]) for n, w in (("wk", H), ("wks", H), ("gc", NP), ("gcs", NP), ("bmask", NB)))
        m.neghalf = m.keep("neghalf", [8])
        m.stat = m.keep("stat", [32])
        m.qms, m.qrs = m.keep("head_sums", [80]), m.keep("head_rstd", [80])
        m.gnm, m.gnv, m.gnr = m.keep("gn_mean", [H]), m.keep("gn_var", [H]), m.keep("gn_rstd", [H])
        m.amx, m.asum, m.wmx = m.keep("att_max", [32]), m.keep("att_sum", [32]), m.keep("win_stat", [4])
        m.state = m.keep("state", [NP, HD])
        m.wt = m.keep("route_w", [2, NT])
        m.place, m.idx = m.keep("place", [2, NT], U32), m.keep("slot_token", [NPT], U32)
        m.ovexp, m.novp = m.keep("overflow_expert", [OV], I32), m.keep("overflow_pairs", [1], I32)
        m.rows_dram = nc.dram_tensor("moe_rows_dram", (T, D), F32).ap()
        m.slots_dram = nc.dram_tensor("slot_out_dram", (NPT * P, D), F32).ap()
        chunks = lambda n: a[n].rearrange("a (p c) -> p (a c)", p=P)
        wide = lambda n: a[n].partition_broadcast(P).rearrange("p a n -> p (a n)")
        m.constant_loads = [
            (m.ident[:], a["c_ident"]), (m.g_mix[:], chunks("g_mix")), (m.g_cross[:], chunks("g_cross")),
            (m.g_moe[:], chunks("g_moe")), (m.g_mem[:], chunks("g_mem")), (m.g_qk[0][:], wide("g_q_att")),
            (m.g_qk[1][:], wide("g_k_att")), (m.g_ret[:], wide("g_ret_out")), (m.g_q_mem[:], wide("g_q_mem")),
            (m.g_k_mem[:], wide("g_k_mem")), (m.wk[:], a["c_wk"]), (m.wks[:], a["c_wks"]), (m.decay_chunk[:], a["c_gc"]),
            (m.decay_steps[:], a["c_gcs"]), (m.bmask[:], a["c_bmask"])]
        m.rows_in = [nc.alloc_semaphore(name=f"token_rows{t}_in") for t in range(NT)]
        m.first_in = nc.alloc_semaphore(name="first_constants_in")
        m.constants_in = nc.alloc_semaphore(name="constants_in")
        halves = lambda n, r: [a[n].rearrange(r, p=P)[:, :, 512 * j:512 * j + 512] for j in range(2)]
        by_p, by_c = "a (p c) n -> p (a c) n", "a (c p) n -> p (a c) n"
        w_in = a["w_in"].rearrange(by_p, p=P)
        w_in = [w_in[:, :, 512 * j:512 * j + 512] for j in (4, 5, 3, 0, 1, 2, 6)]
        low, high = (m.W, m.W + 4096), (m.WH + 4096, m.WH)
        m.w_in = Weights(nc, m, "in", w_in, low, (m.WH, m.WH + 4096))
        m.w_o = Weights(nc, m, "wo", halves("w_o", by_c), high, low)
        m.w_mem = Weights(nc, m, "mem", halves("w_mk", by_p) + halves("w_mv", by_p), high, low)
        m.w_mq = Weights(nc, m, "cross", halves("w_mq", by_p), high, low)
        m.w_mo = Weights(nc, m, "back", halves("w_mo", by_c), (m.Z, m.Z + 4096), (m.WH, m.WH + 4096))
        m.mem_rows = m.at("mem_rows", m.Z + 15872, [2, D])
        m.experts = Experts(nc, m, a)
        stages = (load_constants, project_in, mix_prompt, mix_windows, project_out, project_memory, project_cross,
                  cross_attend, project_back, route, experts, combine)
        for stage in stages:
            stage(nc, m, a)
            if stage in (mix_windows, project_back):
                m.free_sems()


def constants():
    f = np.float32
    i, j = np.arange(P), np.arange(P)
    gamma = 1.0 - 2.0 ** (-5.0 - np.arange(H))
    slope = 2.0 ** (-8.0 * np.arange(1, H + 1) / H)

    def bias(d, window_ok):
        n = sum(((d >= 0) & (d % dil == 0) & (d <= win)).astype(int) for win, dil in PATTERNS)
        n = n * window_ok
        return np.where(n > 0, np.log(np.maximum(n, 1)), 0.0), n > 0

    c = {}
    c["c_ident"] = np.eye(P)
    c["c_tri"] = (i[:, None] < j[None, :])
    d = i[:, None] + (512 - P) - np.arange(512)[None, :]
    logn, ok = bias(d, 1)
    c["c_tab"] = np.stack([np.where(ok, logn - s * d, NEG) for s in slope], axis=1)
    rel = i[None, :] - j[:, None]
    c["c_dm"] = np.stack([np.where(rel >= 0, HD ** -0.5 * g ** np.maximum(rel, 0), 0) for g in gamma], axis=1)
    t = np.arange(NS)
    rel = (t[None, :] - t[:, None])
    same = (t[None, :] // LS == t[:, None] // LS) & (rel >= 0)
    dms = np.zeros((P, H, NS))
    dms[:NS] = np.stack([np.where(same, HD ** -0.5 * g ** np.maximum(rel, 0), 0) for g in gamma], axis=1)
    c["c_dms"] = dms[:NS]
    by_pair = np.stack([np.repeat(gamma[2 * q:2 * q + 2], HD) for q in range(NP)], axis=1)
    c["c_wq"] = (by_pair[:, :, None] ** (i[None, None, :] + 1)).reshape(P, -1)
    c["c_wqs"] = (by_pair[:, :, None] ** (t[None, None, :] % LS + 1)).reshape(P, -1)
    c["c_gc"], c["c_gcs"] = by_pair ** P, by_pair ** LS
    c["c_wk"] = HD ** -0.5 * gamma[None, :] ** (P - 1 - j[:, None])
    c["c_wks"] = HD ** -0.5 * gamma[None, :] ** (LS - 1 - j[:, None] % LS)
    c["c_bmask"] = (j[:, None] // LS == np.arange(NB)[None, :])
    r = np.arange(FAR)
    far = 16 * (r // LS) + r % LS
    near = WBUF - NEAR + 4 * np.arange(P)[None, :] + np.arange(NEAR // P)[:, None]
    key = np.concatenate([far, near.reshape(-1), WBUF + np.arange(2 * NS - LS) - (NS - LS)])
    own = np.concatenate([np.ones(KC * P), (key[KC * P:] >= WBUF) & (key[KC * P:] < WBUF + LS)])
    tab = np.zeros((P, len(key)))
    for h in range(H):
        for s in range(LS):
            d = WBUF + s - key
            logn, ok = bias(d, own)
            tab[32 * (h // 2) + 8 * (h % 2) + s] = np.where(ok, logn - slope[h] * d, NEG)
    c["c_btab"] = tab
    route = np.zeros((P, NCONST))
    put = lambda n, x: route.__setitem__((slice(None), CONST[n]), x)
    put("iota", np.arange(P))
    put("pairs", np.arange(NPW))
    put("key4", NG - np.arange(NG))
    put("key8", EPG - np.arange(EPG))
    put("by64", SLOT * np.arange(1, 9))
    put("ids", np.arange(NE))
    put("evens", 2 * np.arange(1, NPT))
    put("ovs", np.arange(OV))
    put("ovpairs", 2 * np.arange(NOVP))
    tok = np.arange(NT)[None, :] * P + i[:, None]
    put("valid", tok < T)
    put("token", tok * (tok < T))
    e = np.arange(NE)
    put("before", (e[None, :] < e[:, None]).reshape(-1)[None, :])
    c["c_route"] = route
    return {k: np.ascontiguousarray(x, dtype=f) for k, x in c.items()}


_INS = ["x_prompt", "x_sample", "mem_prompt", "state_ret", "cache_win_k", "cache_win_v", "cache_mem_k", "cache_mem_v",
        "g_mix", "w_in", "g_ret_out", "g_q_att", "g_k_att", "w_o", "g_cross", "g_mem", "w_mq", "w_mk", "w_mv",
        "g_q_mem", "g_k_mem", "w_mo", "g_moe", "w_router_group", "b_router_group", "w_router_expert",
        "b_router_expert", "w_exp_gate", "w_exp_up", "w_exp_down"]
_OUTS = [("o_yp", (1, SEQ, D)), ("o_ys", (NB, LS, D)), ("o_rp", (1, 1, H, HD, HD)), ("o_wkp", (1, 1, SEQ, H, HD)),
         ("o_wvp", (1, 1, SEQ, H, HD)), ("o_mk", (1, 1, MEM, MH, MD)), ("o_mv", (1, 1, MEM, MH, MD)),
         ("o_rs", (1, NB, H, HD, HD)), ("o_wks", (1, NB, LS, H, HD)), ("o_wvs", (1, NB, LS, H, HD))]


def kernel(**inputs):
    import concourse.bacc as bacc
    from concourse.bass_utils import run_bass_kernel_spmd

    nc = bacc.Bacc("TRN2", target_bir_lowering=False, num_devices=1)
    arrays, a = {}, {}
    for name, x in [*((n, np.ascontiguousarray(inputs[n])) for n in _INS), *constants().items()]:
        arrays[name] = x
        a[name] = nc.dram_tensor(name, x.shape, F32, kind="ExternalInput").ap()
    for name, shape in _OUTS:
        a[name] = nc.dram_tensor(name, shape, F32, kind="ExternalOutput").ap()
    trunk_step(nc, a)
    got = run_bass_kernel_spmd(nc, [arrays], core_ids=[0]).results[0]
    return tuple(got[name] for name, _ in _OUTS)
```

```python
from contextlib import ExitStack

import numpy as np

import concourse.bass as bass
from concourse import mybir

F32 = mybir.dt.float32
F32R = mybir.dt.float32r
I32 = mybir.dt.int32
U32 = mybir.dt.uint32
ALU = mybir.AluOpType
ACT = mybir.ActivationFunctionType
AX = mybir.AxisListType

P = 128
D = 1024
C8 = D // P
SEQ = 512
NB, LS = 8, 8
NS = NB * LS
T = SEQ + NS
TP = SEQ + P
NT = 5
H, HD = 8, 64
NP = H // 2
RW = H * HD
PAST, WBUF = 4096, 2048
PATTERNS = ((128, 1), (512, 4), (2048, 16))
NEAR = 512
FAR = (WBUF - NEAR) // 16 * LS
KC = (FAR + NEAR) // P
FC = FAR // P
WK = KC * P + NS
MEM, MH, MD = 256, 4, 256
NG, EPG, NE, FE = 4, 8, 32, 256
SLOT = 64
OV = 18
NPAIR, NOVP = NE // 2, OV // 2
NPT = NPAIR + NOVP
EPS = 1e-6
NEG = -1e30


def rows(t):
    return P if t < NT - 1 else NS


def tcol(t):
    return slice(t * P, t * P + rows(t))


class Chain:

    def __init__(self, eng, sem, start=0):
        self.eng, self.sem, self.n = eng, sem, start

    def __call__(self, ins):
        self.n += 1
        ins.then_inc(self.sem, 1)
        self.eng.wait_ge(self.sem, self.n)


class Plan:

    X, HT, HTH, Z, W, WH, SMALL, END = 0, 5120, 10240, 15360, 33280, 41472, 49664, 53200

    def __init__(self, nc, ctx):
        self.nc, self.ctx = nc, ctx
        self.base = 16512
        self.open = []
        self.small = self.SMALL
        self.bank = [ctx.enter_context(nc.psum_tensor(f"bank{i}", [P, 512], F32)) for i in range(8)]
        self.x = self.at("x", self.X, [NT, D])
        self.ht = self.at("ht", self.HT, [C8, TP])

    def at(self, name, word, shape, dt=F32):
        n = int(np.prod(shape))
        assert word + n <= self.END, (name, word, n)
        return self.nc.alloc_sbuf_tensor_at(name, [P, *shape], dt, offset=self.base + 4 * word)

    def keep(self, name, shape, dt=F32):
        t = self.at(name, self.small, shape, dt)
        self.small += (int(np.prod(shape)) + 7) // 8 * 8
        return t

    def sem(self, name):
        self.open.append(self.nc.alloc_semaphore(name=name))
        return self.open[-1]

    def free_sems(self):
        self.nc.clear_and_free_semaphores(self.open)
        self.nc.all_engine_barrier()
        self.open = []


def over(ap, n):
    k = len(ap.shape)
    return ap.unsqueeze(k).to_broadcast([*ap.shape, n])


def across(ap, at, n):
    s = list(ap.shape)
    return ap.unsqueeze(at).to_broadcast(s[:at] + [n] + s[at:])


class Weights:

    def __init__(self, nc, m, name, blocks, at, hi_at):
        self.blocks, self.sent = blocks, 0
        self.w = [m.at(f"{name}_w{i}", at[i], [C8, 512]) for i in range(2)]
        self.lo = [m.at(f"{name}_wl{i}", at[i], [C8, 512], F32R) for i in range(2)]
        self.hi = [m.at(f"{name}_wh{i}", hi_at[i], [C8, 512], F32R) for i in range(2)]
        self.loaded = [nc.alloc_semaphore(name=f"{name}_w_loaded{i}") for i in range(2)]

    def load(self, eng):
        i = self.sent % 2
        eng.dma_start(self.w[i][:], self.blocks[self.sent]).then_inc(self.loaded[i], 16)
        self.sent += 1


def dense(nc, m, name, src, weights, tiles, store, hooks={}, gain=None, widths=None, junk_at=None, arrived=None, later=None):
    nt, nb, BANKS = len(tiles), len(weights.blocks), 4
    PARTS = 4
    part = lambda i: slice(i * C8 // PARTS, (i + 1) * C8 // PARTS)
    hth = m.at(f"{name}_hth", m.HTH, [C8, TP], F32R)
    htl = m.at(f"{name}_htl", m.HT, [C8, TP], F32R)
    w, wl, wh, loaded = weights.w, weights.lo, weights.hi, weights.loaded
    s = lambda n: m.sem(f"{name}_{n}")
    sq_done, var_done, rstd_done, xs_done = s("sq_done"), s("var_done"), s("rstd_done"), s("xs_done")
    turned, ht_done, hth_done, htl_done = s("turned"), s("ht_done"), s("hth_done"), s("htl_done")
    low_out, summed = s("low_rows_out"), s("low_rows_summed")
    low_rows = m.ht[:NS, :, T:TP]
    sampled = lambda n: nt == NT and n == NT - 1
    eighths = lambda ap: ap.rearrange("p (c n) -> p c n", c=8)
    wh_done, wl_done, mm_done, stored = s("wh_done"), s("wl_done"), s("mm_done"), s("stored")
    normed = src is not None
    if normed:
        junk = [m.at(f"{name}_normed{i}", junk_at + 1024 * i, [D]) for i in range(2)]
    full = lambda n: slice(n * P, (n + 1) * P)

    with nc.Block() as block:
        @block.sync
        def _(sp):
            for b in range(weights.sent, nb):
                if b >= 2:
                    sp.wait_ge(mm_done, (b - 1) * nt)
                weights.load(sp)
            if later is not None:
                later(sp, mm_done)

        @block.gpsimd
        def _(pool):
            if normed:
                for n in range(nt):
                    r = widths[n]
                    pool.wait_ge(sq_done, n + 1)
                    pool.tensor_scalar(m.stat[:r, 8 + n:9 + n], m.stat[:r, n:n + 1], 1.0 / D, EPS,
                                       ALU.mult, ALU.add).then_inc(var_done, 1)
                    pool.wait_ge(var_done, n + 1)
                    pool.tensor_tensor(m.stat[:r, 16 + n:17 + n], m.stat[:r, 8 + n:9 + n],
                                       m.neghalf[:r, 0:1], ALU.pow).then_inc(rstd_done, 1)
            if "gpsimd" in hooks:
                hooks["gpsimd"](pool)

        @block.scalar
        def _(act):
            def norm(n):
                r = widths[n]
                if arrived is not None:
                    arrived(act, n)
                if n >= 2:
                    act.wait_ge(turned, 2 * (n - 1))
                act.activation(junk[n % 2][:r, :], src[:r, n, :], ACT.Square,
                               accum_out=m.stat[:r, n:n + 1]).then_inc(sq_done, 1)
                act.wait_ge(rstd_done, n + 1)
                act.activation(junk[n % 2][:r, :], src[:r, n, :], ACT.Copy,
                               scale=m.stat[:r, 16 + n:17 + n]).then_inc(xs_done, 1)

            def split_w(b):
                act.wait_ge(loaded[b % 2], 16 * (b // 2 + 1))
                if b >= 2:
                    act.wait_ge(mm_done, (b - 1) * nt)
                for i in range(PARTS):
                    act.activation(wh[b % 2][:, part(i)], w[b % 2][:, part(i)], ACT.Copy).then_inc(wh_done, 1)

            def split_rows(n):
                if normed:
                    act.wait_ge(ht_done, 2 * n + 2)
                c = slice(n * P, n * P + NS) if sampled(n) else full(n)
                act.activation(hth[:, :, c], m.ht[:, :, c], ACT.Copy).then_inc(hth_done, 1)

            def finish(k):
                b, n = divmod(k, nt)
                act.wait_ge(mm_done, k + 1)
                if sampled(n):
                    act.activation(low_rows, eighths(m.bank[k % BANKS][NS:]), ACT.Copy).then_inc(low_out, 1)
                    act.wait_ge(summed, b + 1)
                store(act, m.bank[k % BANKS], b, n).then_inc(stored, 1)
                if "scalar" in hooks:
                    hooks["scalar"](act, b, n, stored, k)

            if normed:
                norm(0)
                norm(1)
            split_rows(0)
            split_w(0)
            split_rows(1)
            if normed:
                for n in range(2, min(4, nt)):
                    norm(n)
            for n in range(2, nt):
                split_rows(n)
                if n == nt - 1:
                    split_w(1)
                finish(n - 2)
                if normed and n + 2 < nt:
                    norm(n + 2)
            if nt == 2:
                split_w(1)
            for k in range(nt - 2, nb * nt):
                if k % nt == 0 and nt <= k < (nb - 1) * nt:
                    split_w(k // nt + 1)
                finish(k)

        @block.vector
        def _(dve):
            if normed and arrived is not None:
                arrived(dve, 0)

            def scale_rows(n):
                r = widths[n]
                for j in range(2):
                    dve.wait_ge(turned, 2 * n + j + 1)
                    dve.tensor_tensor(m.ht[:, 4 * j:4 * j + 4, n * P:n * P + r],
                                      m.bank[4 + j][:].rearrange("p (c n) -> p c n", c=4)[:, :, :r],
                                      over(gain[:, 4 * j:4 * j + 4], r), ALU.mult).then_inc(ht_done, 1)

            def split_rows(n):
                dve.wait_ge(hth_done, n + 1)
                if sampled(n):
                    c = slice(SEQ, T)
                    dve.tensor_tensor(hth[:, :, T:TP], m.ht[:, :, c], hth[:, :, c].bitcast(F32), ALU.subtract).then_inc(htl_done, 1)
                    return
                dve.tensor_tensor(htl[:, :, full(n)], m.ht[:, :, full(n)], hth[:, :, full(n)].bitcast(F32),
                                  ALU.subtract).then_inc(htl_done, 1)

            def split_w(b):
                for i in range(PARTS):
                    dve.wait_ge(wh_done, PARTS * b + i + 1)
                    dve.tensor_tensor(wl[b % 2][:, part(i)], w[b % 2][:, part(i)], wh[b % 2][:, part(i)].bitcast(F32),
                                      ALU.subtract).then_inc(wl_done, 1)

            if normed:
                scale_rows(0)
                scale_rows(1)
            split_rows(0)
            split_w(0)
            for n in range(1, nt):
                if normed and n >= 2:
                    scale_rows(n)
                split_rows(n)
            for b in range(nb):
                if b + 1 < nb:
                    split_w(b + 1)
                for n in range(nt):
                    if sampled(n):
                        dve.wait_ge(low_out, b + 1)
                        o = eighths(m.bank[(b * nt + n) % BANKS][:NS])
                        dve.tensor_tensor(o, o, low_rows, ALU.add).then_inc(summed, 1)
                    if "vector" in hooks:
                        hooks["vector"](dve, b, n, stored, b * nt + n)

        @block.tensor
        def _(pe):
            if normed and arrived is not None:
                arrived(pe, 0)

            def turn(n):
                r = widths[n]
                pe.wait_ge(xs_done, n + 1)
                rows_ = junk[n % 2][:r, :].rearrange("n (p c) -> n c p", c=C8)
                for j in range(2):
                    if n:
                        pe.wait_ge(ht_done, 2 * n - 1 + j)
                    for c in range(4):
                        last = pe.transpose(m.bank[4 + j][:, c * P:c * P + r], rows_[:, 4 * j + c, :], m.ident[:r, :r])
                    last.then_inc(turned, 1)

            def product(k):
                b, n = divmod(k, nt)
                if b == 0:
                    pe.wait_ge(hth_done, n + 1)
                    pe.wait_ge(htl_done, n + 1)
                if k >= BANKS:
                    pe.wait_ge(stored, k - BANKS + 1)
                o = m.bank[k % BANKS][:]
                for c in range(C8):
                    if n == 0 and c * PARTS % C8 == 0:
                        pe.wait_ge(wh_done, PARTS * b + c * PARTS // C8 + 1)
                        pe.wait_ge(wl_done, PARTS * b + c * PARTS // C8 + 1)
                    hi, lo = hth[:, c, full(n)], htl[:, c, full(n)]
                    if sampled(n):
                        pe.matmul(o, hi, wh[b % 2][:, c, :], start=(c == 0), stop=False)
                        last = pe.matmul(o, hi, wl[b % 2][:, c, :], start=False, stop=(c == C8 - 1))
                        continue
                    pe.matmul(o, hi, wh[b % 2][:, c, :], start=(c == 0), stop=False)
                    pe.matmul(o, hi, wl[b % 2][:, c, :], start=False, stop=False)
                    last = pe.matmul(o, lo, wh[b % 2][:, c, :], start=False, stop=(c == C8 - 1))
                last.then_inc(mm_done, 1)

            if normed:
                for n in range(nt):
                    turn(n)
                    if n:
                        product(n - 1)
                product(nt - 1)
            for k in range(nt if normed else 0, nb * nt):
                product(k)


def load_constants(nc, m, a):
    with nc.Block() as block:
        zeroed = m.sem("neghalf_set")

        @block.sync
        def _(sp):
            xp = a["x_prompt"].rearrange("a (t p) d -> p (a t) d", p=P)
            for t in range(NT - 1):
                sp.dma_start(m.x[:, t, :], xp[:, t, :]).then_inc(m.rows_in[t], 16)
                if t == 1:
                    m.w_in.load(sp)
            sp.dma_start(m.x[:NS, NT - 1, :], a["x_sample"].rearrange("b i d -> (b i) d")).then_inc(m.rows_in[NT - 1], 16)
            m.w_in.load(sp)

        @block.scalar
        def _(act):
            for n, (dst, src) in enumerate(m.constant_loads):
                act.dma_start(dst, src).then_inc(m.first_in if n < 2 else m.constants_in, 16)

        @block.vector
        def _(dve):
            dve.memset(m.neghalf[:], -0.5).then_inc(zeroed, 1)


def project_in(nc, m, a):
    squared, reduced, rstd = m.sem("qk_squared"), m.sem("qk_reduced"), m.sem("qk_rstd")
    exped, gated, chain_s = m.sem("gate_exped"), m.sem("gate_gated"), m.sem("in_dve_chain")
    varied = m.sem("qk_varied")
    sq = [m.scr[:, 0:512], m.scr[:, 512:1024]]

    gate_exp = m.z[6]

    def store(act, bank, b, t):
        if b == 6 and t == 0:
            act.wait_ge(gated, NT)
        return act.activation(m.z[b][:rows(t), t, :], bank[:rows(t), :], ACT.Copy)

    def scalar(act, b, t, stored, k):
        r = rows(t)
        if b < 2:
            if k >= 2:
                act.wait_ge(reduced, k - 1)
            act.wait_ge(stored, k + 1)
            act.activation(sq[k % 2][:r, :], m.z[b][:r, t, :], ACT.Square).then_inc(squared, 1)
        elif b == 2:
            act.wait_ge(stored, k + 1)
            act.activation(gate_exp[:r, t, :], m.z[2][:r, t, :], ACT.Exp, scale=-1.0).then_inc(exped, 1)

    chain = []

    def vector(dve, b, t, stored, k):
        if not chain:
            chain.append(Chain(dve, chain_s))
            dve.wait_ge(m.constants_in, 16 * (len(m.constant_loads) - 2))
        r = rows(t)
        if b < 2:
            dve.wait_ge(squared, k + 1)
            dve.tensor_reduce(m.qms[:r, 8 * k:8 * k + 8], heads(sq[k % 2][:r, :]), AX.X, ALU.add).then_inc(reduced, 1)
            if k:
                normed_heads(dve, k - 1)
        elif b == 2 and t == 0:
            normed_heads(dve, 2 * NT - 1)
        elif b == 3 and t < 3:
            gate(dve, t)
        elif b == 4 and t < NT - 3:
            gate(dve, t + 3)

    heads = lambda ap: ap.rearrange("p (h d) -> p h d", h=H)

    def normed_heads(dve, k):
        link, (b, t) = chain[0], divmod(k, NT)
        r = rows(t)
        z = heads(m.z[b][:r, t, :])
        dve.wait_ge(rstd, k + 1)
        link(dve.tensor_tensor(z, z, over(m.qrs[:r, 8 * k:8 * k + 8], HD), ALU.mult))
        link(dve.tensor_tensor(z, z, across(m.g_qk[b][:r, :], 1, H), ALU.mult))

    def gate(dve, t):
        link, r = chain[0], rows(t)
        z, e = m.z[2][:r, t, :], gate_exp[:r, t, :]
        dve.wait_ge(exped, t + 1)
        link(dve.tensor_scalar(e, e, 1.0, None, ALU.add))
        link(dve.reciprocal(e, e))
        link(dve.tensor_tensor(e, e, m.g_ret[:r, :], ALU.mult))
        dve.tensor_tensor(z, z, e, ALU.mult).then_inc(gated, 1)

    def gpsimd(pool):
        for k in range(2 * NT):
            r = rows(k % NT)
            c = slice(8 * k, 8 * k + 8)
            pool.wait_ge(reduced, k + 1)
            pool.tensor_scalar(m.qrs[:r, c], m.qms[:r, c], 1.0 / HD, EPS, ALU.mult, ALU.add).then_inc(varied, 1)
            pool.wait_ge(varied, k + 1)
            pool.tensor_tensor(m.qrs[:r, c], m.qrs[:r, c], m.neghalf[:r, 0:8], ALU.pow).then_inc(rstd, 1)

    def arrived(eng, n):
        if eng is nc.scalar:
            eng.wait_ge(m.rows_in[n], 16)
        else:
            eng.wait_ge(m.first_in, 32)

    dense(nc, m, "in", m.x, m.w_in, range(NT), store, {"scalar": scalar, "vector": vector, "gpsimd": gpsimd},
          m.g_mix, [rows(t) for t in range(NT)], m.Z + 6 * NT * RW, arrived)


def mix_prompt(nc, m, a):
    QA, KA, GR, QR, KR, VR, VA = range(7)
    tr = [m.at(n, m.W + i * NP * T, [NP, T]) for i, n in enumerate(("qr_t", "kr_t", "qa_t", "ka_t"))]
    qr_t, kr_t, qa_t, ka_t = tr
    m.qa_t, m.ka_t = qa_t, ka_t
    w0 = m.W + 4 * NP * T
    tab = m.at("tab", w0, [H, 512])
    dm = m.at("dm", w0 + 4096, [H, P])
    qa_hi, ka_hi = m.at("qa_hi", m.Z + GR * 2560, [NP, SEQ], F32R), m.at("ka_hi", m.Z + VR * 2560, [NP, SEQ], F32R)
    qa_lo, ka_lo = (m.at(n, m.W + i * NP * T, [NP, T], F32R) for i, n in ((2, "qa_lo"), (3, "ka_lo")))
    pair_of_rows = lambda n, word: m.at(n, word, [2, 512])
    sb = [pair_of_rows("scored0", w0 + 5120), pair_of_rows("scored1", w0 + 6144)]
    pt = [pair_of_rows("probs_t0", m.HTH), pair_of_rows("probs_t1", w0 + 4096)]
    pb = [pair_of_rows(f"probs{i}", m.Z + KR * 2560 + 1024 * i) for i in range(2)]
    h0 = m.HTH
    sd = m.at("decayed", h0 + 1024, [H, P])
    qw = m.at("q_weighted", h0 + 2048, [NP, P])
    kw = m.at("k_weighted", h0 + 2560, [RW])
    cc = m.at("centred", h0 + 3072, [RW])
    sq = m.at("centred_sq", h0 + 3584, [RW])
    ot = [m.at(f"out_rows{i}", h0 + 4096 + 512 * i, [RW]) for i in range(2)]
    s0 = m.at("state_in", m.Z, [NP, NB * HD])
    vx = [m.at(f"v_spread{i}", w, [NB * HD]) for i, w in
          enumerate((m.Z + 2048, m.Z + 2560 + 2048, m.Z + QR * 2560 + 1024, m.Z + QR * 2560 + 1536))]
    s1 = m.at("state_out", m.Z + 2560, [NP, NB * HD])
    z3 = m.Z + QR * 2560
    dms = m.at("dms", z3, [H, NS])
    qws = m.at("qs_weighted", z3 + 512, [NP, NS])
    ots = m.at("os_t", z3 + 768, [NP, NS])
    wq, wqs = m.scr[:, 0:512], m.scr[:, 512:768]
    st = m.state
    z = m.z
    S = m.sem
    tabs_in, dms_in, state_in = S("tabs_in"), S("dms_in"), S("state_in")
    tr_done, tev = S("tr_done"), [S("tr_stored_even"), S("tr_stored_odd")]
    sc_done, sd_done, qw_done, kw_done = S("ret_scored"), S("ret_decayed"), S("q_weighted"), S("k_weighted")
    o_done, kv_done, st_done, gn_c = S("ret_out"), S("kv_out"), S("state_done"), S("gn_centred")
    gn_sq, gn_red, gn_var, gn_rstd = S("gn_squared"), S("gn_reduced"), S("gn_varied"), S("gn_rstd")
    out_ready, out_turned, out_stored = S("out_ready"), S("out_turned"), S("out_stored")
    vx_done, kvs_done, ots_done, os_done = S("v_spread"), S("kvs_out"), S("os_t_stored"), S("os_turned")
    osT_done = S("os_t_done")
    s1_done = S("state_out_done")
    as_done, sb_done, mx_done, ex_done = S("att_scored"), S("att_biased"), S("att_max"), S("att_exped")
    pt_done, pt_ev, pv_done = S("probs_turned"), [S("probs_t0_stored"), S("probs_t1_stored")], S("pv_done")
    hi_done, lo_done = S("qk_hi_done"), S("qk_lo_done")
    rc_done, nm_done, ao_done = S("att_recip"), S("att_normed"), S("att_stored")
    stores = S("mix_stores")
    ch = S("mix_dve_chain")
    hv = lambda ap, h=H: ap.rearrange("p (h d) -> p h d", h=h)
    UNITS = [(qb, q) for qb in range(SEQ // P) for q in range(NP)]
    NU = len(UNITS)

    with nc.Block() as block:
        @block.sync
        def _(sp):
            n = 0
            sp.dma_start(tab[:], a["c_tab"]).then_inc(tabs_in, 16)
            sp.dma_start(dm[:], a["c_dm"]).then_inc(tabs_in, 16)
            sp.dma_start(wq, a["c_wq"]).then_inc(tabs_in, 16)
            sp.dma_start(wqs, a["c_wqs"]).then_inc(tabs_in, 16)
            for src, dst_p, dst_s in ((KA, "o_wkp", "o_wks"), (VA, "o_wvp", "o_wvs")):
                sp.dma_start(a[dst_p].rearrange("a b (t p) h d -> p (a b t) (h d)", p=P),
                             z[src][:, 0:NT - 1, :]).then_inc(stores, 16)
                sp.dma_start(a[dst_s].rearrange("a b i h d -> (a b i) (h d)"), z[src][:NS, NT - 1, :]).then_inc(stores, 16)
                n += 32
            sp.wait_ge(stores, n)
            sp.wait_ge(tev[0], 10)
            sp.wait_ge(tev[1], 10)
            sp.dma_start(dms[:NS], a["c_dms"]).then_inc(dms_in, 16)
            src = a["state_ret"].rearrange("a b (q e) d f -> e q d (a b) f", e=2)
            for e in range(2):
                for q in range(NP):
                    sp.dma_start(s0[64 * e:64 * e + 64, q, :].rearrange("d (b f) -> d b f", b=NB),
                                 src[e, q]).then_inc(state_in, 16)
            sp.wait_ge(st_done, SEQ // P)
            dst = a["o_rp"].rearrange("a b (q e) d f -> e d (a b q) f", e=2)
            for e in range(2):
                sp.dma_start(dst[e], st[64 * e:64 * e + 64]).then_inc(stores, 16)
                n += 16
            sp.wait_ge(s1_done, NP)
            dst = a["o_rs"].rearrange("a b (q e) d f -> e q d (a b) f", e=2)
            for e in range(2):
                for q in range(NP):
                    sp.dma_start(dst[e, q], s1[64 * e:64 * e + 64, q, :].rearrange("d (b f) -> d b f", b=NB)
                                 ).then_inc(stores, 16)
                    n += 16
            sp.wait_ge(stores, n)
            sp.wait_ge(kvs_done, H)
            sp.wait_ge(out_ready, SEQ // P + 1)
            for is_v, i in ((0, 0), (0, 1), (1, 1)):
                m.windows.load(sp, 0, is_v, i)

        @block.tensor
        def _(pe):
            for k in range(20):
                j, t = divmod(k, NT)
                r = rows(t)
                if k >= 4:
                    pe.wait_ge(tev[k % 2], k // 2 - 1)
                for p in range(NP):
                    last = pe.transpose(m.bank[k % 4][:, p * P:p * P + r],
                                        z[(QR, KR, QA, KA)[j]][:r, t, p * P:(p + 1) * P], m.ident[:r, :r])
                last.then_inc(tr_done, 1)
            pe.wait_ge(tev[0], 10)
            pe.wait_ge(tev[1], 10)

            def turn_out(i, r):
                pe.wait_ge(out_ready, i + 1)
                if i:
                    pe.wait_ge(out_stored, i)
                for c in range(4):
                    last = pe.transpose(m.bank[6][:, c * P:c * P + r], ot[i % 2][:r, c * P:(c + 1) * P],
                                        m.ident[:r, :r])
                last.then_inc(out_turned, 1)

            def half(ap, h):
                return ap[64 * (h % 2):64 * (h % 2) + 64]

            for n in range(SEQ // P):
                tc = slice(n * P, (n + 1) * P)
                if n:
                    pe.wait_ge(sd_done, 2 * n)
                for h in range(H):
                    last = pe.matmul(m.bank[2 + h % 2][:, (h // 2) * P:(h // 2 + 1) * P],
                                     half(kr_t, h)[:, h // 2, tc], half(qr_t, h)[:, h // 2, tc],
                                     start=True, stop=True)
                    if h >= H - 2:
                        last.then_inc(sc_done, 1)
                pe.wait_ge(kw_done, n + 1)
                if n:
                    pe.wait_ge(st_done, n)
                    pe.wait_ge(gn_c, n)
                for h in range(H):
                    last = pe.matmul(half(m.bank[5], h)[:, (h // 2) * HD:(h // 2 + 1) * HD],
                                     kw[:, h * HD:(h + 1) * HD], z[VR][:, n, h * HD:(h + 1) * HD],
                                     start=True, stop=True)
                last.then_inc(kv_done, 1)
                pe.wait_ge(sd_done, 2 * n + 2)
                if n:
                    pe.wait_ge(qw_done, n)
                o = lambda h: m.bank[(4, 7)[h % 2]][:, (h // 2) * HD:(h // 2 + 1) * HD]
                for h in range(H):
                    last = pe.matmul(o(h), sd[:, h, :], z[VR][:, n, h * HD:(h + 1) * HD], start=True, stop=(n == 0),
                                     skip_group_check=True)
                    if n:
                        last = pe.matmul(o(h), half(qw, h)[:, h // 2, :], half(st, h)[:, h // 2, :], start=False,
                                         stop=True, skip_group_check=True)
                last.then_inc(o_done, 1)
                if n:
                    turn_out(n - 1, P)
            turn_out(3, P)

            sc = slice(SEQ, T)
            for h in range(H):
                last = pe.matmul(m.bank[2 + h % 2][:NS, (h // 2) * NS:(h // 2 + 1) * NS], half(kr_t, h)[:, h // 2, sc],
                                 half(qr_t, h)[:, h // 2, sc], start=True, stop=True)
            last.then_inc(sc_done, 1)
            pe.wait_ge(sd_done, 2 * 4 + 2)
            pe.wait_ge(qw_done, 4)
            pe.wait_ge(state_in, 16 * H)
            pe.wait_ge(gn_c, 4)
            for h in range(H):
                o = half(m.bank[4], h)[:, (h // 2) * NS:(h // 2 + 1) * NS]
                pe.matmul(o, z[VR][:NS, NT - 1, h * HD:(h + 1) * HD], sd[:NS, h, :NS], start=True, stop=True)
                o = half(m.bank[h % 2], h)[:, (h // 2) * NS:(h // 2 + 1) * NS]
                for b in range(NB):
                    last = pe.matmul(o[:, LS * b:LS * b + LS], half(s0, h)[:, h // 2, b * HD:(b + 1) * HD],
                                     half(qws, h)[:, h // 2, LS * b:LS * b + LS], start=True, stop=True)
            last.then_inc(osT_done, 1)
            pe.wait_ge(kw_done, 5)
            for h in range(H):
                q = h // 2
                if q >= 2 and h % 2 == 0:
                    pe.wait_ge(s1_done, q - 1)
                pe.wait_ge(vx_done, h + 1)
                last = pe.matmul(half(m.bank[(5, 7)[q % 2]], h)[:, :], kw[:NS, h * HD:(h + 1) * HD], vx[h % 4][:NS, :],
                                 start=True, stop=True)
                last.then_inc(kvs_done, 1)
            pe.wait_ge(ots_done, 3)
            for q in range(NP):
                last = pe.transpose(m.bank[3][:NS, q * P:(q + 1) * P], ots[:, q, :], m.ident[:, :])
            last.then_inc(os_done, 1)

            def scores(u):
                qb, q = UNITS[u]
                n = (qb + 1) * P
                if u >= 2:
                    pe.wait_ge(sb_done, 2 * (u - 1))
                for i, (qx, kx) in enumerate(((qa_hi, ka_hi), (qa_hi, ka_lo), (qa_lo, ka_hi))):
                    for e in range(2):
                        last = pe.matmul(m.bank[2 * (u % 2) + e][:, :n], half(qx, e)[:, q, qb * P:(qb + 1) * P],
                                         half(kx, e)[:, q, :n], start=(i == 0), stop=(i == 2))
                last.then_inc(as_done, 1)

            def turn(u):
                n = UNITS[u][0] + 1
                pe.wait_ge(nm_done, 2 * u + 2)
                for e in range(2):
                    if u:
                        pe.wait_ge(pt_ev[e], u)
                    for j in range(n):
                        last = pe.transpose(m.bank[4 + e][:, j * P:(j + 1) * P], pb[u % 2][:, e, j * P:(j + 1) * P], m.ident[:, :])
                    last.then_inc(pt_done, 1)

            def probs_v(u):
                qb, q = UNITS[u]
                for e in range(2):
                    pe.wait_ge(pt_ev[e], u + 1)
                if u >= 2:
                    pe.wait_ge(ao_done, u - 1)
                for j in range(qb + 1):
                    for e in range(2):
                        h = 2 * q + e
                        last = pe.matmul(half(m.bank[6 + u % 2], e)[:, :P], z[VA][:, j, h * HD:(h + 1) * HD],
                                         pt[u % 2][:, e, j * P:(j + 1) * P], start=(j == 0), stop=(j == qb),
                                         skip_group_check=True)
                last.then_inc(pv_done, 1)

            pe.wait_ge(hi_done, 2)
            pe.wait_ge(lo_done, 2)
            scores(0)
            pe.wait_ge(sd_done, 10)
            pe.wait_ge(gn_c, 5)
            scores(1)
            pe.wait_ge(s1_done, NP)
            for u in range(NU):
                turn(u)
                if u + 2 < NU:
                    scores(u + 2)
                if u == 0:
                    turn_out(4, NS)
                    pe.wait_ge(out_stored, 5)
                probs_v(u)

        @block.scalar
        def _(act):
            def store_turned(k):
                t = k % NT
                act.wait_ge(tr_done, k + 1)
                act.activation(tr[k // NT][:, :, tcol(t)],
                               m.bank[k % 4][:].rearrange("p (c n) -> p c n", c=4)[:, :, :rows(t)], ACT.Copy).then_inc(tev[1], 1)

            def store_out(i, t, off):
                act.wait_ge(out_turned, i + 1)
                act.activation(m.ht[:, off:off + 4, tcol(t)],
                               m.bank[6][:].rearrange("p (c n) -> p c n", c=4)[:, :, :rows(t)], ACT.Copy).then_inc(out_stored, 1)

            def square(i, r):
                act.wait_ge(gn_c, i + 1)
                if i:
                    act.wait_ge(gn_red, i)
                act.activation(sq[:r, :], cc[:r, :], ACT.Square).then_inc(gn_sq, 1)

            for k in range(1, 20, 2):
                store_turned(k)
            for n in range(4):
                square(n, P)
                store_out(n, n, 0)
            act.wait_ge(out_ready, SEQ // P)
            act.wait_ge(o_done, SEQ // P)
            for x, hi in ((qa_t, qa_hi), (ka_t, ka_hi)):
                act.activation(hi[:], x[:, :, :SEQ], ACT.Copy).then_inc(hi_done, 1)
            act.wait_ge(osT_done, 1)
            act.activation(ots[:], m.bank[4][:, :NP * NS].rearrange("p (q n) -> p q n", q=NP), ACT.Copy).then_inc(ots_done, 1)

            def exps(u):
                n = (UNITS[u][0] + 1) * P
                act.wait_ge(mx_done, u + 1)
                if u == 0:
                    act.wait_ge(kw_done, 5)
                if u >= 2:
                    act.wait_ge(pt_done, 2 * (u - 1))
                for e in range(2):
                    c = slice(2 * u + e, 2 * u + e + 1)
                    act.activation(pb[u % 2][:, e, :n], sb[u % 2][:, e, :n], ACT.Exp, bias=m.amx[:, c],
                                   accum_out=m.asum[:, c]).then_inc(ex_done, 1)

            def norms(u):
                n = (UNITS[u][0] + 1) * P
                act.wait_ge(rc_done, u + 1)
                for e in range(2):
                    act.activation(pb[u % 2][:, e, :n], pb[u % 2][:, e, :n], ACT.Copy,
                                   scale=m.asum[:, 2 * u + e:2 * u + e + 1]).then_inc(nm_done, 1)

            square(4, NS)
            exps(0)
            norms(0)
            exps(1)
            for u in range(NU):
                n = (UNITS[u][0] + 1) * P
                act.wait_ge(pt_done, 2 * u + 1)
                if u >= 2:
                    act.wait_ge(pv_done, u - 1)
                act.activation(pt[u % 2][:, 0, :n], m.bank[4][:, :n], ACT.Copy).then_inc(pt_ev[0], 1)
                if u + 1 < NU:
                    norms(u + 1)
                if u + 2 < NU:
                    exps(u + 2)
                if u == 0:
                    store_out(4, 4, 0)

        @block.gpsimd
        def _(pool):
            pool.wait_ge(tabs_in, 64)
            pool.wait_ge(tev[0], 10)
            pool.wait_ge(tev[1], 10)

            def norm(i, r):
                pool.wait_ge(gn_red, i + 1)
                pool.tensor_scalar(m.gnr[:r, :], m.gnv[:r, :], 1.0 / HD, EPS, ALU.mult, ALU.add).then_inc(gn_var, 1)
                pool.wait_ge(gn_var, i + 1)
                pool.tensor_tensor(m.gnr[:r, :], m.gnr[:r, :], m.neghalf[:r, 0:8], ALU.pow).then_inc(gn_rstd, 1)

            def weight_k(n):
                if n:
                    pool.wait_ge(kv_done, n)
                pool.tensor_tensor(hv(kw[:]), hv(z[KR][:, n, :]), over(m.wk[:, :], HD), ALU.mult).then_inc(kw_done, 1)

            weight_k(0)
            for n in range(4):
                if n:
                    pool.wait_ge(o_done, n)
                    pool.tensor_tensor(qw[:], qr_t[:, :, n * P:(n + 1) * P], hv(wq, NP), ALU.mult).then_inc(qw_done, 1)
                if n < 3:
                    weight_k(n + 1)
                norm(n, P)
            pool.wait_ge(kv_done, 4)
            pool.wait_ge(dms_in, 16)
            pool.tensor_tensor(qws[:], qr_t[:, :, SEQ:T], hv(wqs, NP), ALU.mult).then_inc(qw_done, 1)
            pool.tensor_tensor(hv(kw[:NS]), hv(z[KR][:NS, NT - 1, :]), over(m.wks[:NS, :], HD), ALU.mult).then_inc(kw_done, 1)
            for h in range(H):
                if h >= 4:
                    pool.wait_ge(kvs_done, h - 3)
                pool.tensor_tensor(hv(vx[h % 4][:NS]), across(z[VR][:NS, NT - 1, h * HD:(h + 1) * HD], 1, NB),
                                   over(m.bmask[:NS, :], HD), ALU.mult).then_inc(vx_done, 1)
            norm(4, NS)

        @block.vector
        def _(dve):
            link = Chain(dve, ch)
            for k in range(0, 20, 2):
                t = k % NT
                dve.wait_ge(tr_done, k + 1)
                dve.tensor_copy(tr[k // NT][:, :, tcol(t)],
                                m.bank[k % 4][:].rearrange("p (c n) -> p c n", c=4)[:, :, :rows(t)]).then_inc(tev[0], 1)
            dve.wait_ge(tabs_in, 64)

            def group_norm(i, t, o, meanwhile=None):
                r = rows(t)
                for e in range(2):
                    link(dve.tensor_reduce(m.gnm[:r, e::2], o[e], AX.X, ALU.add))
                link(dve.tensor_scalar(m.gnm[:r, :], m.gnm[:r, :], -1.0 / HD, None, ALU.mult))
                link(dve.tensor_tensor(hv(cc[:r])[:, 0::2], o[0], over(m.gnm[:r, 0::2], HD), ALU.add))
                dve.tensor_tensor(hv(cc[:r])[:, 1::2], o[1], over(m.gnm[:r, 1::2], HD), ALU.add).then_inc(gn_c, 1)
                dve.wait_ge(gn_sq, i + 1)
                dve.tensor_reduce(m.gnv[:r, :], hv(sq[:r]), AX.X, ALU.add).then_inc(gn_red, 1)
                if meanwhile is not None:
                    meanwhile()
                dve.wait_ge(gn_rstd, i + 1)
                link(dve.tensor_tensor(hv(cc[:r]), hv(cc[:r]), over(m.gnr[:r, :], HD), ALU.mult))
                if i >= 2:
                    dve.wait_ge(out_turned, i - 1)
                dve.tensor_tensor(ot[i % 2][:r], cc[:r], z[GR][:r, t, :], ALU.mult).then_inc(out_ready, 1)

            def decayed(n):
                for j in range(2):
                    dve.wait_ge(sc_done, 2 * n + j + 1)
                    if n:
                        dve.wait_ge(o_done, n)
                    dve.tensor_tensor(sd[:, j::2, :], hv(m.bank[2 + j][:], 4), dm[:, j::2, :],
                                      ALU.mult).then_inc(sd_done, 1)

            decayed(0)
            for n in range(4):
                dve.wait_ge(kv_done, n + 1)
                dve.wait_ge(o_done, n + 1)
                kv = hv(m.bank[5][:, :NP * HD], NP)
                if n == 0:
                    dve.tensor_copy(st[:], kv).then_inc(st_done, 1)
                else:
                    link(dve.tensor_tensor(st[:], st[:], over(m.decay_chunk[:, :], HD), ALU.mult))
                    dve.tensor_tensor(st[:], st[:], kv, ALU.add).then_inc(st_done, 1)
                group_norm(n, n, [hv(m.bank[k][:, :NP * HD], NP) for k in (4, 7)],
                           (lambda: decayed(n + 1)) if n < 3 else None)
            dve.wait_ge(dms_in, 16)
            dve.wait_ge(sc_done, 9)
            dve.wait_ge(o_done, 4)
            for j in range(2):
                dve.tensor_tensor(sd[:NS, j::2, :NS], hv(m.bank[2 + j][:NS, :NP * NS], NP), dms[:NS, j::2, :],
                                  ALU.mult).then_inc(sd_done, 1)
            for i, (x, hi, lo) in enumerate(((qa_t, qa_hi, qa_lo), (ka_t, ka_hi, ka_lo))):
                dve.wait_ge(hi_done, i + 1)
                dve.tensor_tensor(lo[:, :, :SEQ], x[:, :, :SEQ], hi[:].bitcast(F32), ALU.subtract).then_inc(lo_done, 1)
            dve.wait_ge(ots_done, 1)
            for e in range(2):
                dve.tensor_tensor(ots[64 * e:64 * e + 64], ots[64 * e:64 * e + 64],
                                  m.bank[e][64 * e:64 * e + 64, :NP * NS].rearrange("p (q n) -> p q n", q=NP),
                                  ALU.add).then_inc(ots_done, 1)
            dve.wait_ge(state_in, 16 * H)
            for q in range(NP):
                dve.wait_ge(kvs_done, 2 * q + 2)
                link(dve.tensor_scalar(s1[:, q, :], s0[:, q, :], m.decay_steps[:, q:q + 1], None, ALU.mult))
                dve.tensor_tensor(s1[:, q, :], s1[:, q, :], m.bank[(5, 7)[q % 2]][:], ALU.add).then_inc(s1_done, 1)
            dve.wait_ge(os_done, 1)
            os_ = m.bank[3][:NS].rearrange("p (q e d) -> p e q d", e=2, d=HD)
            group_norm(4, 4, [os_[:, 0], os_[:, 1]])

            def maxima(u):
                qb, q = UNITS[u]
                n = (qb + 1) * P
                dve.wait_ge(as_done, u + 1)
                if u >= 2:
                    dve.wait_ge(ex_done, 2 * (u - 1))
                for e in range(2):
                    dve.scalar_tensor_tensor(sb[u % 2][:, e, :n], m.bank[2 * (u % 2) + e][:, :n], HD ** -0.5,
                                             tab[:, 2 * q + e, 512 - n:], ALU.mult, ALU.add).then_inc(sb_done, 1)
                dve.wait_ge(sb_done, 2 * u + 2)
                dve.tensor_reduce(m.amx[:, 2 * u:2 * u + 2], sb[u % 2][:, :, :n], AX.X, ALU.max, negate=True
                                  ).then_inc(mx_done, 1)

            def recip(u):
                dve.wait_ge(ex_done, 2 * u + 2)
                dve.reciprocal(m.asum[:, 2 * u:2 * u + 2], m.asum[:, 2 * u:2 * u + 2]).then_inc(rc_done, 1)

            maxima(0)
            recip(0)
            maxima(1)
            for u, (qb, q) in enumerate(UNITS):
                n = (qb + 1) * P
                dve.wait_ge(pt_done, 2 * u + 2)
                if u >= 2:
                    dve.wait_ge(pv_done, u - 1)
                dve.tensor_copy(pt[u % 2][:, 1, :n], m.bank[5][:, :n]).then_inc(pt_ev[1], 1)
                if u + 1 < NU:
                    recip(u + 1)
                if u + 2 < NU:
                    maxima(u + 2)
                dve.wait_ge(pv_done, u + 1)
                dve.tensor_copy(m.ht[:, NP + q, qb * P:(qb + 1) * P], m.bank[6 + u % 2][:, :P]).then_inc(ao_done, 1)


class Windows:
    HALF = KC // 2

    def __init__(self, m, a):
        at = lambda n, j: [m.at(f"{n}_half{i}", m.Z + 2560 * (j + i), [self.HALF, RW]) for i in range(2)]
        self.k, self.v = at("k", 0), at("v", 2)
        self.k_in, self.v_in = ([m.sem(f"{n}_half{i}_in") for i in range(2)] for n in "kv")
        ck, cv = a["cache_win_k"], a["cache_win_v"]
        self.far = [c.rearrange("a b (c g r) h d -> (a b) g r c (h d)", g=16, r=16) for c in (ck, cv)]
        self.near = [c[:, :, WBUF - NEAR:].rearrange("a b (p c) h d -> (a b) p c (h d)", p=P) for c in (ck, cv)]

    def load(self, sp, b, is_v, half):
        dst, sem = (self.v if is_v else self.k)[half], (self.v_in if is_v else self.k_in)[half]
        i = bass.ds(b, 1)
        for c in range(self.HALF if half == 0 else FC - self.HALF):
            src = self.far[is_v][i, :, 0:LS, half * self.HALF + c, :]
            sp.dma_start(dst[:, c, :], src.rearrange("a g r n -> (a g) r n")).then_inc(sem, 16)
        if half:
            sp.dma_start(dst[:, FC - self.HALF:, :], self.near[is_v][i].rearrange("a p c n -> (a p) c n")).then_inc(sem, 16)

    COUNT = (HALF, FC - HALF + 1)


def mix_windows(nc, m, a):
    qa_t, ka_t = m.qa_t, m.ka_t
    win = m.windows
    k_half, v_half, kin, vin, HC = win.k, win.v, win.k_in, win.v_in, win.HALF
    kt = m.at("window_k_t", m.Z + 4 * 2560, [NP, KC * P])
    btab = m.at("window_tab", m.W, [KC * P + 2 * NS - LS])
    pb = m.at("window_probs", m.W + 1408, [WK])
    pt = m.at("window_probs_t", m.W + 2752, [KC + 1, P])
    sb = m.at("window_scored", m.HTH, [WK])
    qb_all = m.at("q_blocks", m.HTH + 1344, [NB, NP, 32])
    qb = m.at("q_block", m.HTH + 2368, [NP, 32])
    va = m.z[6]
    ow = m.at("window_out", m.HTH + 3600, [P])
    ow_done, ot_done = m.sem("window_out_normed"), m.sem("window_out_turned")
    S = m.sem
    tab_in, qz, qb_done = S("window_tab_in"), S("q_blocks_zeroed"), S("q_block_done")
    kt_done, kt_ev = S("window_k_turned"), [S("k_t_stored_even"), S("k_t_stored_odd")]
    ws_done, sb_done, mx_done, ex_done = (S("window_scored"), S("window_biased"), S("window_max"), S("window_exped"))
    rl = S("window_recip")
    pt_done, pt_ev, pv_done, o_ev = S("window_p_turned"), S("window_p_stored"), S("window_pv"), S("window_out")
    out4 = lambda e: m.ht[64 * e:64 * e + 64, 4:8, :]

    with nc.Block() as block:
        @block.sync
        def _(sp):
            sp.dma_start(btab[:], a["c_btab"]).then_inc(tab_in, 16)

            def keys(n):
                sp.wait_ge(kt_done, n * KC - KC + HC + 1)
                win.load(sp, n, 0, 0)
                sp.wait_ge(kt_done, n * KC + 1)
                win.load(sp, n, 0, 1)

            def values(n):
                sp.wait_ge(pv_done, n + 1)
                for half in range(2):
                    win.load(sp, n, 1, half)

            win.load(sp, 0, 1, 0)
            keys(1)
            with sp.Fori(0, NB - 2) as i:
                keys(i + 2)
                values(i + 1)
            values(NB - 1)
            m.w_o.load(sp)

        @block.vector
        def _(dve):
            for sem in (sb_done, kt_ev[0], o_ev):
                dve.sem_inc(sem, 1)
            dve.memset(qb_all[:], 0.0).then_inc(qz, 1)
            dve.wait_ge(qz, 1)
            for e in range(2):
                for q in range(NP):
                    dve.tensor_copy(qb_all[64 * e:64 * e + 64, :, q, 8 * e:8 * e + 8],
                                    qa_t[64 * e:64 * e + 64, q, SEQ:T].rearrange("p (b i) -> p b i", b=NB)).then_inc(qz, 1)
            dve.wait_ge(qz, 1 + 2 * NP)
            dve.wait_ge(tab_in, 16)

            def keys(n):
                for c in range(0, KC, 2):
                    dve.wait_ge(kt_done, n * KC + c + 2)
                    if c == 0:
                        dve.wait_ge(ws_done, n * 3 + 1)
                    dve.tensor_copy(kt[:, :, c * P:(c + 1) * P], m.bank[0][:].rearrange("p (q n) -> p q n", q=NP)
                                    ).then_inc(kt_ev[0], 1)
                dve.tensor_copy(qb[:], qb_all[:, bass.ds(n, 1)].rearrange("p a q n -> p (a q) n")).then_inc(qb_done, 1)

            def biased(n):
                dve.wait_ge(ex_done, n + 1)
                for j, lo in enumerate((0, 512)):
                    dve.wait_ge(ws_done, n * 3 + j + 2)
                    dve.scalar_tensor_tensor(sb[:, lo:lo + 512], m.bank[2 + j][:], HD ** -0.5, btab[:, lo:lo + 512],
                                             ALU.mult, ALU.add).then_inc(sb_done, 1)
                k = KC * P - 1024
                dve.wait_ge(ws_done, n * 3 + 4)
                dve.scalar_tensor_tensor(sb[:, 1024:KC * P], m.bank[4][:, :k], HD ** -0.5, btab[:, 1024:KC * P],
                                         ALU.mult, ALU.add).then_inc(sb_done, 1)
                dve.scalar_tensor_tensor(sb[:, KC * P:], m.bank[4][:, k:k + NS], HD ** -0.5,
                                         btab[:, bass.ds((n * -1 + (NB - 1)) * LS + KC * P, NS)],
                                         ALU.mult, ALU.add).then_inc(sb_done, 1)
                dve.wait_ge(sb_done, n * 4 + 5)
                dve.tensor_reduce(m.wmx[:, 0:1], sb[:], AX.X, ALU.max, negate=True).then_inc(mx_done, 1)

            def turned(n):
                dve.wait_ge(pt_done, n * 3 + 3)
                dve.wait_ge(pv_done, n + 1)
                dve.tensor_copy(pt[:, 4:8, :], m.bank[6][:].rearrange("p (c n) -> p c n", c=4)).then_inc(pt_ev, 1)
                dve.wait_ge(ex_done, n + 2)
                dve.reciprocal(m.wmx[:, 2:3], m.wmx[:, 1:2]).then_inc(rl, 1)

            def outputs(n):
                dve.wait_ge(rl, n + 1)
                dve.wait_ge(pv_done, n + 2)
                dve.tensor_scalar(ow[:], m.bank[1][:, 0:P], m.wmx[:, 2:3], None, ALU.mult).then_inc(ow_done, 1)
                dve.wait_ge(ot_done, n + 1)
                for e in range(2):
                    dve.tensor_copy(out4(e)[:, :, bass.ds(n * LS + SEQ, LS)],
                                    m.bank[1][64 * e:64 * e + 64, P:2 * P].rearrange("p (q n) -> p q n", q=NP)[:, :, 8 * e:8 * e + 8]
                                    ).then_inc(o_ev, 1)

            keys(0)
            biased(0)
            with dve.Fori(0, NB - 1) as i:
                keys(i + 1)
                turned(i)
                biased(i + 1)
                outputs(i)
            turned(NB - 1)
            outputs(NB - 1)

        @block.scalar
        def _(act):
            for sem in (kt_ev[1], pt_ev, ex_done):
                act.sem_inc(sem, 1)

            def keys(n):
                for c in range(1, KC, 2):
                    act.wait_ge(kt_done, n * KC + c + 2)
                    if c == 1:
                        act.wait_ge(ws_done, n * 3 + 1)
                    act.activation(kt[:, :, c * P:(c + 1) * P], m.bank[7][:].rearrange("p (q n) -> p q n", q=NP),
                                   ACT.Copy).then_inc(kt_ev[1], 1)

            def exps(n):
                act.wait_ge(mx_done, n + 1)
                act.wait_ge(pt_done, n * 3 + 1)
                act.activation(pb[:], sb[:], ACT.Exp, bias=m.wmx[:, 0:1], accum_out=m.wmx[:, 1:2]).then_inc(ex_done, 1)

            def turned(n):
                act.wait_ge(pt_done, n * 3 + 2)
                act.wait_ge(pv_done, n + 1)
                act.activation(pt[:, 0:4, :], m.bank[5][:].rearrange("p (c n) -> p c n", c=4), ACT.Copy).then_inc(pt_ev, 1)
                act.wait_ge(pt_done, n * 3 + 4)
                act.activation(pt[:, 8:10, :], m.bank[1][:, 256:512].rearrange("p (c n) -> p c n", c=2), ACT.Copy).then_inc(pt_ev, 1)
                act.activation(pt[:NS, KC, :], m.bank[1][:NS, P:2 * P], ACT.Copy).then_inc(pt_ev, 1)

            keys(0)
            with act.Fori(0, NB - 1) as i:
                exps(i)
                keys(i + 1)
                turned(i)
            exps(NB - 1)
            turned(NB - 1)

        @block.tensor
        def _(pe):
            for sem in (ws_done, pt_done, pv_done, kt_done):
                pe.sem_inc(sem, 1)

            def keys(n):
                for c in range(KC):
                    if c == 0:
                        pe.wait_ge(kin[0], (n + 1) * (16 * win.COUNT[0]))
                    if c == HC:
                        pe.wait_ge(kin[1], (n + 1) * (16 * win.COUNT[1]))
                    pe.wait_ge(kt_ev[c % 2], n * HC + c // 2 + 1)
                    for q in range(NP):
                        last = pe.transpose(m.bank[(0, 7)[c % 2]][:, q * P:(q + 1) * P],
                                            k_half[c // HC][:, c % HC, q * P:(q + 1) * P], m.ident[:, :])
                    last.then_inc(kt_done, 1)

            def scores(n):
                pe.wait_ge(qb_done, n + 1)
                pe.wait_ge(sb_done, n * 4 + 1)
                for j, (lo, k) in enumerate(((0, 512), (512, 512), (1024, KC * P - 1024))):
                    for par in range(2):
                        pe.wait_ge(kt_ev[par], n * HC + ((lo + k) // P + 1 - par) // 2 + 1)
                    for q in range(NP):
                        last = pe.matmul(m.bank[2 + j][32 * q:32 * q + 32, :k], qb[:, q, :], kt[:, q, lo:lo + k],
                                         start=True, stop=True)
                    if j == 2:
                        for q in range(NP):
                            last = pe.matmul(m.bank[4][32 * q:32 * q + 32, k:k + NS], qb[:, q, :], ka_t[:, q, SEQ:T],
                                             start=True, stop=True)
                    last.then_inc(ws_done, 1)

            def turn_probs(n):
                pe.wait_ge(ex_done, n + 2)
                pe.wait_ge(pt_ev, n * 4 + 1)
                pe.wait_ge(o_ev, n * 2 + 1)
                places = [m.bank[b][:, lo * P:(lo + 1) * P] for b, first, c in ((5, 0, 4), (6, 0, 4), (1, 2, 2))
                          for lo in range(first, first + c)]
                for c in range(KC):
                    last = pe.transpose(places[c], pb[:, c * P:(c + 1) * P], m.ident[:, :])
                    if c in (3, 7):
                        last.then_inc(pt_done, 1)
                pe.transpose(m.bank[1][:NS, P:2 * P], pb[:, KC * P:], m.ident[:, :]).then_inc(pt_done, 1)

            def products(n):
                pe.wait_ge(pt_ev, n * 4 + 5)
                pe.wait_ge(vin[0], (n + 1) * (16 * win.COUNT[0]))
                pe.wait_ge(vin[1], (n + 1) * (16 * win.COUNT[1]))
                for c in range(KC + 1):
                    for q in range(NP):
                        v = v_half[c // HC][:, c % HC, q * P:(q + 1) * P] if c < KC else va[:NS, NT - 1, q * P:(q + 1) * P]
                        p = pt[:, c, 32 * q:32 * q + 32] if c < KC else pt[:NS, KC, 32 * q:32 * q + 32]
                        last = pe.matmul(m.bank[1][32 * q:32 * q + 32, 0:P], p, v, start=(c == 0), stop=(c == KC),
                                         skip_group_check=True)
                last.then_inc(pv_done, 1)

            def turn_out(n):
                pe.wait_ge(ow_done, n + 1)
                pe.transpose(m.bank[1][:, P:2 * P], ow[:], m.ident[:, :]).then_inc(ot_done, 1)

            keys(0)
            scores(0)
            with pe.Fori(0, NB - 1) as i:
                keys(i + 1)
                turn_probs(i)
                scores(i + 1)
                products(i)
                turn_out(i)
            turn_probs(NB - 1)
            products(NB - 1)
            turn_out(NB - 1)


def project_out(nc, m, a):
    m.mem_in = m.sem("mem_in")
    zero = m.at("zero_rows", m.Z + 1024, [D])
    zero_done, zero_out = m.sem("zero_rows_done"), m.sem("zero_rows_out")

    def later(sp, mm_done):
        sp.wait_ge(zero_done, 1)
        for n in range(NPAIR, NPT):
            sp.dma_start(m.slots_dram[n * P:(n + 1) * P, :], zero[:]).then_inc(zero_out, 16)
        sp.dma_start(m.mem_rows[:], a["mem_prompt"].rearrange("a (t p) d -> p (a t) d", p=P)).then_inc(m.mem_in, 16)
        sp.wait_ge(mm_done, NT)
        m.w_mem.load(sp)
        sp.wait_ge(zero_out, 16 * NOVP)

    def gpsimd(pool):
        pool.memset(zero[:], 0.0).then_inc(zero_done, 1)

    residual(nc, m, "wo", m.w_o, m.Z, later, {"gpsimd": gpsimd})


def residual(nc, m, name, weights, rows_at, later, hooks={}):
    res = m.sem(f"{name}_added")
    st = [m.at(f"{name}_rows{i}", rows_at + 512 * i, [512]) for i in range(2)]

    def store(act, bank, b, t):
        k = b * NT + t
        if k >= 2:
            act.wait_ge(res, k - 1)
        return act.activation(st[k % 2][:rows(t), :], bank[:rows(t), :], ACT.Copy)

    def vector(dve, b, t, stored, k):
        dve.wait_ge(stored, k + 1)
        x = m.x[:rows(t), t, 512 * b:512 * b + 512]
        dve.tensor_tensor(x, x, st[k % 2][:rows(t), :], ALU.add).then_inc(res, 1)

    dense(nc, m, name, None, weights, range(NT), store, {"vector": vector, **hooks}, later=later)


def project_memory(nc, m, a):
    mk = m.at("mem_k", m.Z + 5120, [2, D])
    mv = m.at("mem_v", m.Z + 7168, [2, D])
    m.mem_k, m.mem_v = mk, mv
    dsts = [mk, mk, mv, mv]
    store = lambda act, bank, b, t: act.activation(dsts[b][:, t, 512 * (b % 2):512 * (b % 2) + 512], bank[:], ACT.Copy)
    hooks = wide_norm(nc, m, "mem", [(0, 2), (1, 2)], mk, m.g_k_mem, 2, [P, P])
    arrived = lambda eng, n: eng.wait_ge(m.mem_in, 16)

    def later(sp, mm_done):
        for b in range(2):
            sp.wait_ge(mm_done, 2 * (b + 3))
            m.w_mq.load(sp)

    dense(nc, m, "mem", m.mem_rows, m.w_mem, range(2), store, hooks, m.g_mem, [P, P], m.Z + 10240, arrived, later)


def wide_norm(nc, m, name, blocks, dst, gain, nt, widths):
    squared, reduced, rstd, varied, ch = (m.sem(f"{name}_hsq"), m.sem(f"{name}_hred"), m.sem(f"{name}_hrstd"),
                                          m.sem(f"{name}_hvar"), m.sem(f"{name}_hchain"))
    sq = [m.scr[:, 0:512], m.scr[:, 512:1024]]
    hv = lambda ap: ap.rearrange("p (h d) -> p h d", h=2)
    chain = []

    def scalar(act, b, t, stored, k):
        if b < 2:
            if k >= 2:
                act.wait_ge(reduced, k - 1)
            act.wait_ge(stored, k + 1)
            r = widths[t]
            act.activation(sq[k % 2][:r, :], dst[:r, t, 512 * b:512 * b + 512], ACT.Square).then_inc(squared, 1)

    def vector(dve, b, t, stored, k):
        if b < 2:
            if not chain:
                chain.append(Chain(dve, ch))
            r = widths[t]
            dve.wait_ge(squared, k + 1)
            dve.tensor_reduce(m.qms[:r, 2 * k:2 * k + 2], hv(sq[k % 2][:r, :]), AX.X, ALU.add).then_inc(reduced, 1)
            if k:
                normed_heads(dve, k - 1)
            if k == 2 * nt - 1:
                normed_heads(dve, k)

    def normed_heads(dve, k):
        b, t = divmod(k, nt)
        r = widths[t]
        z = hv(dst[:r, t, 512 * b:512 * b + 512])
        dve.wait_ge(rstd, k + 1)
        chain[0](dve.tensor_tensor(z, z, over(m.qrs[:r, 2 * k:2 * k + 2], MD), ALU.mult))
        chain[0](dve.tensor_tensor(z, z, across(gain[:r, :], 1, 2), ALU.mult))

    def gpsimd(pool):
        for k in range(2 * nt):
            r = widths[k % nt]
            c = slice(2 * k, 2 * k + 2)
            pool.wait_ge(reduced, k + 1)
            pool.tensor_scalar(m.qrs[:r, c], m.qms[:r, c], 1.0 / MD, EPS, ALU.mult, ALU.add).then_inc(varied, 1)
            pool.wait_ge(varied, k + 1)
            pool.tensor_tensor(m.qrs[:r, c], m.qrs[:r, c], m.neghalf[:r, 0:2], ALU.pow).then_inc(rstd, 1)

    return {"scalar": scalar, "vector": vector, "gpsimd": gpsimd}


def project_cross(nc, m, a):
    qm = m.at("cross_q", m.Z, [NT, D])
    m.cross_q = qm
    store = lambda act, bank, b, t: act.activation(qm[:rows(t), t, 512 * b:512 * b + 512], bank[:rows(t), :], ACT.Copy)
    widths = [rows(t) for t in range(NT)]
    hooks = wide_norm(nc, m, "cross", None, qm, m.g_q_mem, NT, widths)
    dense(nc, m, "cross", m.x, m.w_mq, range(NT), store, hooks, m.g_cross, widths, m.Z + 10240)


def cross_attend(nc, m, a):
    qm, mk, mv = m.cross_q, m.mem_k, m.mem_v
    qt = m.at("cross_q_t", m.Z + 9216, [C8, T])
    sk = [m.at(f"cache_k{i}", m.W + 2048 * i, [2, D]) for i in range(2)]
    sv = [m.at(f"cache_v{i}", m.W + 4096 + 2048 * i, [2, D]) for i in range(2)]
    skt = m.at("cache_k_t", m.WH, [C8, MEM])
    pb = [m.at(f"cross_probs{i}", m.WH + 2048 + 1024 * i, [MH, MEM]) for i in range(2)]
    qt_hi, qt_lo = m.at("cross_q_hi", m.HTH, [C8, SEQ], F32R), m.at("cross_q_lo", m.Z + 9216, [C8, T], F32R)
    kt_hi, kt_lo = m.at("mem_k_hi", m.Z + 15872, [C8, MEM], F32R), m.at("mem_k_lo", m.Z + 9216 + C8 * T, [C8, MEM], F32R)
    mv_hi, mv_lo = m.at("mem_v_hi", m.Z + 5120, [2, D], F32R), m.at("mem_v_lo", m.Z + 7168, [2, D], F32R)
    pt_hi, pt_lo = (m.at(f"cross_probs_t_{n}", m.Z + 2048 * i, [2 * MH, 2 * P], F32R) for i, n in enumerate(("hi", "lo")))
    spb = [m.at(f"cache_probs{i}", m.WH + 5120 + 256 * i, [MEM]) for i in range(2)]
    S = m.sem
    tr_done, tr_hi, tev = S("cr_turned"), S("cr_turned_hi"), S("cr_turns_out")
    mv_split, pt_h = S("mem_v_split"), S("cr_p_hi")
    sc_done, mx_done, ex_done, pn_done = S("cr_scored"), S("cr_max"), S("cr_exped"), S("cr_normed")
    pt_done, pt_ev, o_done, o_ev = S("cr_p_turned"), S("cr_p_stored"), S("cr_out"), S("cr_out_stored")
    kin, vin = [S("cache_k0_in"), S("cache_k1_in")], [S("cache_v0_in"), S("cache_v1_in")]
    qs = m.at("cache_q", m.WH + 5888, [C8, 32])
    ps = m.at("cache_probs_turned", m.WH + 6144, [2, P])
    so = m.at("cache_out", m.WH + 6400, [MD])
    so_done, st_done = m.sem("cs_out_normed"), m.sem("cs_out_turned")
    cq_done = S("cache_q_done")
    ch, stores = S("cr_chain"), S("cr_stores")
    kt_done, kt_ev = S("ck_turned"), [S("ck_stored_even"), S("ck_stored_odd")]
    s_sc, s_mx, s_ex, s_rl = S("cs_scored"), S("cs_max"), S("cs_exped"), S("cs_recip")
    s_pt, s_pev, s_o, s_oev = S("cs_p_turned"), S("cs_p_stored"), S("cs_out"), S("cs_out_stored")
    ckv = [a[n].rearrange("a b (t p) h d -> p (a b) t (h d)", p=P) for n in ("cache_mem_k", "cache_mem_v")]
    turns = [(qm, qt_hi, qt_lo, t, j) for t in range(NT - 1) for j in range(2)] + \
        [(mk, kt_hi, kt_lo, t, j) for t in range(2) for j in range(2)] + [(qm, None, qt, NT - 1, j) for j in range(2)]
    TURN_BANKS = (0, 1, 6, 7)
    OUT_BANKS = (6, 7, 0, 1)
    four = lambda ap: ap.rearrange("p (c n) -> p c n", c=4)
    NQ = NT - 1
    SC = MD ** -0.5

    with nc.Block() as block:
        @block.sync
        def _(sp):
            for src, dst in ((mk, "o_mk"), (mv, "o_mv")):
                sp.dma_start(a[dst].rearrange("a b (t p) h d -> p (a b t) (h d)", p=P), src[:]).then_inc(stores, 16)
            for b in range(2):
                sp.dma_start(sk[b][:], ckv[0][:, b]).then_inc(kin[b], 16)
                sp.dma_start(sv[b][:], ckv[1][:, b]).then_inc(vin[b], 16)
            with sp.Fori(0, NB // 2 - 1) as i:
                for b in range(2):
                    nxt = bass.ds(i * 2 + 2 + b, 1)
                    sp.wait_ge(kt_done, i * 8 + 4 * b + 4)
                    sp.dma_start(sk[b][:], ckv[0][:, nxt].rearrange("p a t n -> p (a t) n")).then_inc(kin[b], 16)
                    sp.wait_ge(s_o, i * 2 + b + 2)
                    sp.dma_start(sv[b][:], ckv[1][:, nxt].rearrange("p a t n -> p (a t) n")).then_inc(vin[b], 16)
            sp.wait_ge(o_done, 4 * (NQ // 2))
            m.w_mo.load(sp)
            sp.wait_ge(stores, 32)

        @block.tensor
        def _(pe):
            for k, (src, _, _, t, j) in enumerate(turns):
                r = rows(t) if src is qm else P
                if k >= 4:
                    pe.wait_ge(tev, k - 3)
                for c in range(4):
                    last = pe.transpose(m.bank[TURN_BANKS[k % 4]][:, c * P:c * P + r],
                                        src[:r, t, (4 * j + c) * P:(4 * j + c + 1) * P], m.ident[:r, :r])
                last.then_inc(tr_done, 1)
            pe.wait_ge(tev, len(turns))

            def scores(t):
                if t:
                    pe.wait_ge(ex_done, 4 * t)
                for h in range(MH):
                    o = m.bank[2 + h // 2][:, (h % 2) * MEM:(h % 2 + 1) * MEM]
                    for k in range(2):
                        for i, (qx, kx) in enumerate(((qt_hi, kt_hi), (qt_hi, kt_lo), (qt_lo, kt_hi))):
                            last = pe.matmul(o, qx[:, 2 * h + k, tcol(t)], kx[:, 2 * h + k, :],
                                             start=(k == 0 and i == 0), stop=(k == 1 and i == 2))
                last.then_inc(sc_done, 1)

            scores(0)
            for t in range(NQ):
                if t + 1 < NQ:
                    scores(t + 1)
                pe.wait_ge(pn_done, t + 1)
                if t:
                    pe.wait_ge(pt_ev, 2 * t)
                for j in range(2):
                    for c in range(4):
                        h, k = divmod(4 * j + c, 2)
                        last = pe.transpose(m.bank[4 + j][:, c * P:(c + 1) * P], pb[t % 2][:, h, k * P:(k + 1) * P], m.ident[:, :])
                    last.then_inc(pt_done, 1)
                if t % 2 == 0:
                    continue
                pe.wait_ge(pt_ev, 2 * t + 2)
                pe.wait_ge(mv_split, 2)
                if t > 1:
                    pe.wait_ge(o_ev, 4 * (t // 2))
                for c in range(C8):
                    o = m.bank[OUT_BANKS[c // 2]][:, (c % 2) * 2 * P:(c % 2 + 1) * 2 * P]
                    for k in range(2):
                        for i, (vx, px) in enumerate(((mv_hi, pt_hi), (mv_hi, pt_lo), (mv_lo, pt_hi))):
                            last = pe.matmul(o, vx[:, k, c * P:(c + 1) * P], px[:, c // 2 * 2 + k, :],
                                             start=(k == 0 and i == 0), stop=(k == 1 and i == 2))
                    if c % 2:
                        last.then_inc(o_done, 1)
            pe.wait_ge(o_ev, 4 * (NQ // 2))
            pe.wait_ge(ex_done, 4 * NQ)
            for sem in (s_sc, s_pt, s_o):
                pe.sem_inc(sem, 1)

            def keys(n, b, use):
                pe.wait_ge(kin[b], use * 16 + 16)
                for k in range(4):
                    t, j = divmod(k, 2)
                    pe.wait_ge(kt_ev[k % 2], n * 2 + k // 2 + 1)
                    for c in range(4):
                        last = pe.transpose(m.bank[k % 2][:, c * P:(c + 1) * P], sk[b][:, t, (4 * j + c) * P:(4 * j + c + 1) * P], m.ident[:, :])
                    last.then_inc(kt_done, 1)

            def cache_scores(n):
                pe.wait_ge(kt_ev[0], n * 2 + 3)
                pe.wait_ge(kt_ev[1], n * 2 + 3)
                pe.wait_ge(s_ex, n + 1)
                pe.wait_ge(cq_done, n + 2)
                for k in range(2):
                    for h in range(MH):
                        last = pe.matmul(m.bank[2][32 * h:32 * h + 32, :MEM], qs[:, 2 * h + k, :],
                                         skt[:, 2 * h + k, :], start=(k == 0), stop=(k == 1), skip_group_check=True)
                last.then_inc(s_sc, 1)

            def products(n, b, use):
                pe.wait_ge(s_ex, n + 2)
                pe.wait_ge(s_pev, n + 1)
                for k in range(2):
                    last = pe.transpose(m.bank[4][:, k * P:(k + 1) * P], spb[0][:, k * P:(k + 1) * P], m.ident[:, :])
                last.then_inc(s_pt, 1)
                pe.wait_ge(s_pev, n + 2)
                pe.wait_ge(vin[b], use * 16 + 16)
                pe.wait_ge(s_oev, n * 2 + 1)
                for k in range(2):
                    for h in range(MH):
                        last = pe.matmul(m.bank[6][32 * h:32 * h + 32, :MD], ps[:, k, 32 * h:32 * h + 32],
                                         sv[b][:, k, h * MD:(h + 1) * MD], start=(k == 0), stop=(k == 1),
                                         skip_group_check=True)
                last.then_inc(s_o, 1)

            def turn_out(n):
                pe.wait_ge(so_done, n + 1)
                for k in range(2):
                    last = pe.transpose(m.bank[7][:, k * P:(k + 1) * P], so[:, k * P:(k + 1) * P], m.ident[:, :])
                last.then_inc(st_done, 1)

            keys(0, 0, 0)
            cache_scores(0)
            with pe.Fori(0, NB // 2 - 1) as i:
                for b in range(2):
                    keys(i * 2 + b + 1, 1 - b, i + b)
                    products(i * 2 + b, b, i)
                    cache_scores(i * 2 + b + 1)
                    turn_out(i * 2 + b)
            keys(NB - 1, 1, NB // 2 - 1)
            products(NB - 2, 0, NB // 2 - 1)
            cache_scores(NB - 1)
            turn_out(NB - 2)
            products(NB - 1, 1, NB // 2 - 1)
            turn_out(NB - 1)

        def turned_part(k, dst):
            src, _, _, t, j = turns[k]
            r = rows(t) if src is qm else P
            return four(m.bank[TURN_BANKS[k % 4]][:])[:, :, :r], dst[:, 4 * j:4 * j + 4, t * P:t * P + r]

        @block.scalar
        def _(act):
            copy = lambda dst, src: act.activation(dst, src, ACT.Copy)
            for k, turn in enumerate(turns):
                if turn[1] is not None:
                    act.wait_ge(tr_done, k + 1)
                    got, dst = turned_part(k, turn[1])
                    copy(dst, got).then_inc(tr_hi, 1)
            act.wait_ge(stores, 32)
            copy(mv_hi[:], mv[:]).then_inc(mv_split, 1)

            def exps(t):
                act.wait_ge(mx_done, t + 1)
                if t >= 2:
                    act.wait_ge(pt_done, 2 * (t - 1))
                for h in range(MH):
                    act.activation(pb[t % 2][:, h, :], m.bank[2 + h // 2][:, (h % 2) * MEM:(h % 2 + 1) * MEM], ACT.Exp,
                                   bias=m.amx[:, 4 * t + h:4 * t + h + 1], scale=SC,
                                   accum_out=m.asum[:, 4 * t + h:4 * t + h + 1]).then_inc(ex_done, 1)

            exps(0)
            for t in range(NQ):
                tc = slice(t % 2 * P, (t % 2 + 1) * P)
                for j in range(2):
                    act.wait_ge(pt_done, 2 * t + j + 1)
                    if t == 2:
                        act.wait_ge(o_done, 4)
                    copy(pt_hi[:, 4 * j:4 * j + 4, tc], four(m.bank[4 + j][:])).then_inc(pt_h, 1)
                if t + 1 < NQ:
                    exps(t + 1)
                if t % 2:
                    for j in range(4):
                        act.wait_ge(o_done, 4 * (t // 2) + j + 1)
                        copy(m.ht[:, 2 * j:2 * j + 2, (t - 1) * P:(t + 1) * P],
                             m.bank[OUT_BANKS[j]][:].rearrange("p (c n) -> p c n", c=2)).then_inc(o_ev, 1)
            for sem in (kt_ev[1], s_ex):
                act.sem_inc(sem, 1)

            def keys(n):
                act.wait_ge(s_sc, n + 1)
                for k in range(1, 4, 2):
                    t, j = divmod(k, 2)
                    act.wait_ge(kt_done, n * 4 + k + 1)
                    copy(skt[:, 4 * j:4 * j + 4, t * P:(t + 1) * P], four(m.bank[1][:])).then_inc(kt_ev[1], 1)

            def exps(n):
                act.wait_ge(s_mx, n + 1)
                act.wait_ge(s_pt, n + 1)
                act.activation(spb[0][:], m.bank[2][:, :MEM], ACT.Exp, bias=m.wmx[:, 0:1], scale=SC,
                               accum_out=m.wmx[:, 1:2]).then_inc(s_ex, 1)

            keys(0)
            with act.Fori(0, NB - 1) as i:
                exps(i)
                keys(i + 1)
            exps(NB - 1)

        @block.vector
        def _(dve):
            link = Chain(dve, ch)
            dve.memset(qs[:], 0.0).then_inc(cq_done, 1)
            dve.wait_ge(cq_done, 1)
            for k, (_, hi, lo, _, _) in enumerate(turns):
                dve.wait_ge(tr_done, k + 1)
                got, dst = turned_part(k, lo)
                if hi is None:
                    dve.tensor_copy(dst, got).then_inc(tev, 1)
                else:
                    dve.wait_ge(tr_hi, k + 1)
                    dve.tensor_tensor(dst, got, turned_part(k, hi)[1].bitcast(F32), ALU.subtract).then_inc(tev, 1)

            def maxima(t):
                dve.wait_ge(sc_done, t + 1)
                c = slice(4 * t, 4 * t + 4)
                for j in range(2):
                    link(dve.tensor_reduce(m.amx[:, 4 * t + 2 * j:4 * t + 2 * j + 2],
                                           m.bank[2 + j][:].rearrange("p (h n) -> p h n", h=2), AX.X, ALU.max))
                dve.tensor_scalar(m.amx[:, c], m.amx[:, c], -SC, None, ALU.mult).then_inc(mx_done, 1)

            maxima(0)
            dve.wait_ge(mv_split, 1)
            dve.tensor_tensor(mv_lo[:], mv[:], mv_hi[:].bitcast(F32), ALU.subtract).then_inc(mv_split, 1)
            for t in range(NQ):
                c = slice(4 * t, 4 * t + 4)
                dve.wait_ge(ex_done, 4 * t + 4)
                link(dve.reciprocal(m.asum[:, c], m.asum[:, c]))
                dve.tensor_tensor(pb[t % 2][:], pb[t % 2][:], over(m.asum[:, c], MEM), ALU.mult).then_inc(pn_done, 1)
                if t + 1 < NQ:
                    maxima(t + 1)
                for j in range(2):
                    dve.wait_ge(pt_h, 2 * t + j + 1)
                    dve.tensor_tensor(pt_lo[:, 4 * j:4 * j + 4, t % 2 * P:(t % 2 + 1) * P], four(m.bank[4 + j][:]),
                                      pt_hi[:, 4 * j:4 * j + 4, t % 2 * P:(t % 2 + 1) * P].bitcast(F32), ALU.subtract).then_inc(pt_ev, 1)
            for sem in (kt_ev[0], s_pev, s_oev):
                dve.sem_inc(sem, 1)

            def keys(n):
                dve.wait_ge(s_sc, n + 1)
                dve.tensor_copy(qs[:, :, 0:LS], qt[:, :, bass.ds(n * LS + SEQ, LS)]).then_inc(cq_done, 1)
                for k in range(0, 4, 2):
                    t, j = divmod(k, 2)
                    dve.wait_ge(kt_done, n * 4 + k + 1)
                    dve.tensor_copy(skt[:, 4 * j:4 * j + 4, t * P:(t + 1) * P], four(m.bank[0][:])).then_inc(kt_ev[0], 1)

            def maxima(n):
                dve.wait_ge(s_sc, n + 2)
                dve.tensor_reduce(m.wmx[:, 3:4], m.bank[2][:, :MEM], AX.X, ALU.max).then_inc(s_rl, 1)
                dve.wait_ge(s_rl, n * 2 + 1)
                dve.tensor_scalar(m.wmx[:, 0:1], m.wmx[:, 3:4], -SC, None, ALU.mult).then_inc(s_mx, 1)

            def outputs(n):
                dve.wait_ge(s_pt, n + 2)
                dve.wait_ge(s_o, n + 1)
                dve.tensor_copy(ps[:], m.bank[4][:, :2 * P].rearrange("p (k n) -> p k n", k=2)).then_inc(s_pev, 1)
                dve.wait_ge(s_ex, n + 2)
                dve.reciprocal(m.wmx[:, 2:3], m.wmx[:, 1:2]).then_inc(s_rl, 1)
                dve.wait_ge(s_rl, n * 2 + 2)
                dve.wait_ge(s_o, n + 2)
                dve.tensor_scalar(so[:], m.bank[6][:, :MD], m.wmx[:, 2:3], None, ALU.mult).then_inc(so_done, 1)
                dve.wait_ge(st_done, n + 1)
                for k in range(2):
                    dve.tensor_copy(m.ht[:, k::2, bass.ds(n * LS + SEQ, LS)],
                                    m.bank[7][:, k * P:(k + 1) * P].rearrange("p (h n) -> p h n", h=MH)[:, :, 0:LS]).then_inc(s_oev, 1)

            keys(0)
            with dve.Fori(0, NB - 1) as i:
                maxima(i)
                keys(i + 1)
                outputs(i)
            maxima(NB - 1)
            outputs(NB - 1)


def project_back(nc, m, a):
    residual(nc, m, "back", m.w_mo, m.Z + 8192, lambda sp, mm_done: m.experts.load(sp, 1, 1))


NPW = NPT + NPT % 2

CONST = {}
_at = 0
for _n, _w in (("iota", P), ("pairs", NPW), ("key4", NG), ("key8", EPG), ("by64", 8), ("ids", NE), ("evens", NPT - 1),
               ("ovs", OV), ("ovpairs", NOVP), ("valid", NT), ("token", NT), ("before", NE * NE)):
    CONST[_n] = slice(_at, _at + _w)
    _at += _w
NCONST = _at


def route(nc, m, a):
    xs = m.at("moe_rows", m.HTH, [NT, D])
    cst = m.at("route_const", m.experts.END, [NCONST])
    wr = m.at("router_w", m.WH, [C8, NG + NE])
    tri = m.at("earlier", m.WH + 512, [P])
    ones = m.at("ones", m.WH + 640, [P])
    big = m.at("route_big", m.WH + 768, [1024])
    sa = m.at("slot_onehot", m.WH + 1792, [2, NT, P], F32R)
    ph = m.at("pair_onehot", m.WH + 5872, [2, NT, NPW])
    pbt = m.at("pair_token", m.WH + 6144, [2, NT, NPW], F32R)
    mk = m.at("expert_mask", m.WH + 3328, [2, NT, NE])
    both = m.at("expert_chosen", m.WH + 5680, [NT + 1, NE])
    rk = m.at("ranks", m.WH + 3808, [NT, NE])
    tmp = m.at("route_tmp", m.WH + 5360, [2, NT, NE])
    lgt = m.at("logits", m.WH + 4128, [NT, NG + NE])
    bias = m.at("router_bias", m.WH + 4312, [NG + NE])
    f = m.at("route_small", m.WH + 4352, [40, 8])
    e4 = [m.at(f"route_e{k}", m.WH + 4672 + 40 * k, [NT, 8]) for k in range(6)]
    cv = [m.at(f"route_v{k}", m.WH + 4912 + 32 * k, [NE]) for k in range(4)]
    S = m.sem
    consts, sq_done, var_done, rstd_done, xs_done = S("ro_consts"), S("ro_sq"), S("ro_var"), S("ro_rstd"), S("ro_rows")
    turned, ht_done, lg_done = S("ro_turned"), S("ro_ht"), S("ro_logits")
    exp_in, exp_out, mask_done, rank_done, oh_done, ix_done = (S("ro_exp_in"), S("ro_exp_out"), S("ro_masks"),
                                                              S("ro_ranks"), S("ro_onehots"), S("ro_index"))
    ch, stores, ones_done = S("ro_chain"), S("ro_stores"), S("ro_ones")
    C = lambda n: cst[:, CONST[n]]
    v = lambda k: f[:, k, 0:NT]
    v2 = lambda k: f[:, 16 + 2 * k:18 + 2 * k, 0:NT]
    widths = [rows(t) for t in range(NT)]

    with nc.Block() as block:
        @block.sync
        def _(sp):
            sp.dma_start(cst[:], a["c_route"]).then_inc(consts, 16)
            sp.dma_start(tri[:], a["c_tri"]).then_inc(consts, 16)
            sp.dma_start(wr[:, :, 0:NG], a["w_router_group"].rearrange("a (p c) g -> p (a c) g", p=P)).then_inc(consts, 16)
            for g in range(NG):
                sp.dma_start(wr[:, :, NG + EPG * g:NG + EPG * (g + 1)],
                             a["w_router_expert"][0, g].rearrange("(p c) e -> p c e", p=P)).then_inc(consts, 16)
            sp.dma_start(bias[:, 0:NG], a["b_router_group"].partition_broadcast(P).rearrange("p a g -> p (a g)")).then_inc(consts, 16)
            sp.dma_start(bias[:, NG:], a["b_router_expert"].partition_broadcast(P).rearrange("p a g e -> p (a g e)")).then_inc(consts, 16)
            m.experts.load(sp, 0, 0)
            for t in range(NT):
                sp.wait_ge(xs_done, t + 1)
                sp.dma_start(m.rows_dram[t * P:t * P + rows(t), :], xs[:rows(t), t, :]).then_inc(stores, 16)
            sp.wait_ge(stores, 16 * NT)

        @block.gpsimd
        def _(pool):
            pool.memset(ones[:], 1.0).then_inc(ones_done, 1)
            pool.memset(both[:, NT, :], 0.0).then_inc(ones_done, 1)
            for t, r in enumerate(widths):
                pool.wait_ge(sq_done, t + 1)
                pool.tensor_scalar(m.stat[:r, 8 + t:9 + t], m.stat[:r, t:t + 1], 1.0 / D, EPS, ALU.mult, ALU.add).then_inc(var_done, 1)
                pool.wait_ge(var_done, t + 1)
                pool.tensor_tensor(m.stat[:r, 16 + t:17 + t], m.stat[:r, 8 + t:9 + t], m.neghalf[:r, 0:1], ALU.pow).then_inc(rstd_done, 1)

        @block.scalar
        def _(act):
            for t, r in enumerate(widths):
                act.activation(xs[:r, t, :], m.x[:r, t, :], ACT.Square, accum_out=m.stat[:r, t:t + 1]).then_inc(sq_done, 1)
                act.wait_ge(rstd_done, t + 1)
                act.activation(xs[:r, t, :], m.x[:r, t, :], ACT.Copy, scale=m.stat[:r, 16 + t:17 + t]).then_inc(xs_done, 1)
            act.wait_ge(exp_in, 1)
            act.activation(e4[0][:, :, 0:NG], e4[0][:, :, 0:NG], ACT.Exp).then_inc(exp_out, 1)
            act.wait_ge(exp_in, 2)
            act.activation(v(2), v(2), ACT.Exp).then_inc(exp_out, 1)

        @block.tensor
        def _(pe):
            def logits(t):
                if t == 0:
                    pe.wait_ge(consts, 16 * 9)
                pe.wait_ge(ht_done, 2 * t + 2)
                for c in range(C8):
                    for g in range(rows(t) // 64):
                        last = pe.matmul(m.bank[0][64 * g:64 * g + 64, 64 * t:64 * t + NG + NE],
                                         m.ht[:, c, t * P + 64 * g:t * P + 64 * g + 64], wr[:, c, :],
                                         start=(c == 0), stop=(c == C8 - 1), skip_group_check=True)
                return last

            for t, r in enumerate(widths):
                pe.wait_ge(xs_done, t + 1)
                for j in range(2):
                    if t:
                        pe.wait_ge(ht_done, 2 * t - 1 + j)
                    for c in range(4):
                        last = pe.transpose(m.bank[4 + j][:, c * P:c * P + r], xs[:r, t, :].rearrange("n (p c) -> n c p", c=C8)[:, 4 * j + c, :], m.ident[:r, :r])
                    last.then_inc(turned, 1)
                if t:
                    logits(t - 1)
            logits(NT - 1).then_inc(lg_done, 1)
            pe.wait_ge(mask_done, 1)
            pe.wait_ge(ones_done, 2)
            counts = m.bank[1][:, 0:NE * (NT + 1)].rearrange("p (t e) -> p t e", t=NT + 1)
            pe.matmul(counts, ones[:], across(both[:, NT, :], 1, NT + 1), start=True, stop=False)
            for u in range(NT):
                pe.matmul(counts[:, u + 1:, :], ones[:], across(both[:, u, :], 1, NT - u), start=False, stop=False,
                          skip_group_check=True)
            pe.matmul(counts, tri[:], both[:], start=False, stop=True).then_inc(rank_done, 1)
            pe.wait_ge(oh_done, 2)
            for k in range(2):
                for t in range(NT):
                    last = pe.matmul(m.bank[2][:, 0:NPW], sa[:, k, t, :], pbt[:, k, t, :],
                                     start=(k == 0 and t == 0), stop=(k == 1 and t == NT - 1))
            last.then_inc(ix_done, 1)

        @block.vector
        def _(dve):
            link = Chain(dve, ch)
            for t, r in enumerate(widths):
                for j in range(2):
                    dve.wait_ge(turned, 2 * t + j + 1)
                    dve.tensor_tensor(m.ht[:, 4 * j:4 * j + 4, t * P:t * P + r],
                                      m.bank[4 + j][:].rearrange("p (c n) -> p c n", c=4)[:, :, :r],
                                      over(m.g_moe[:, 4 * j:4 * j + 4], r), ALU.mult).then_inc(ht_done, 1)
            link(dve.memset(lgt[:], 0.0))
            dve.wait_ge(lg_done, 1)
            dve.wait_ge(consts, 16 * 9)
            lp = m.bank[0][:, 0:64 * NT].rearrange("p (t n) -> p t n", t=NT)[:, :, 0:NG + NE]
            link(dve.tensor_tensor(lgt[:, 0:NT - 1, :], lp[:, 0:NT - 1, :], across(bias[:], 1, NT - 1), ALU.add))
            link(dve.tensor_tensor(lgt[:NS, NT - 1, :], lp[:NS, NT - 1, :], bias[:NS], ALU.add))

            def first_best(best, x, keys, n, d, onehot):
                link(dve.tensor_reduce(v(best), x, AX.X, ALU.max))
                link(dve.tensor_tensor(d, x, over(v(best), n), ALU.subtract))
                link(dve.scalar_tensor_tensor(onehot, d, 0.0, across(keys, 1, NT), ALU.is_ge, ALU.mult))
                link(dve.tensor_reduce(v(9), onehot, AX.X, ALU.max))
                link(dve.tensor_tensor(onehot, onehot, over(v(9), n), ALU.is_equal))

            d4, og = e4[0][:, :, 0:NG], e4[1][:, :, 0:NG]
            first_best(0, lgt[:, :, 0:NG], C("key4"), NG, d4, og)
            dve.tensor_copy(v(8), v(0)).then_inc(exp_in, 1)
            dve.wait_ge(exp_out, 1)
            link(dve.tensor_reduce(v(1), d4, AX.X, ALU.add))
            link(dve.reciprocal(v(1), v(1)))
            link(dve.tensor_tensor(tmp[:, 0].rearrange("p t (g e) -> p t g e", g=NG),
                                   lgt[:, :, NG:].rearrange("p t (g e) -> p t g e", g=NG), over(og, EPG), ALU.mult))
            sel, d8, o1, o2 = e4[2][:], e4[3][:], e4[4][:], e4[5][:]
            link(dve.tensor_reduce(sel, tmp[:, 0].rearrange("p t (g e) -> p t e g", g=NG), AX.X, ALU.add))
            first_best(3, sel, C("key8"), EPG, d8, o1)
            link(dve.scalar_tensor_tensor(sel, o1, NEG, sel, ALU.mult, ALU.add))
            first_best(4, sel, C("key8"), EPG, d8, o2)
            dve.tensor_tensor(v(2), v(4), v(3), ALU.subtract).then_inc(exp_in, 1)
            dve.wait_ge(exp_out, 2)
            link(dve.tensor_scalar(v(5), v(2), 1.0, None, ALU.add))
            link(dve.reciprocal(v(5), v(5)))
            link(dve.tensor_tensor(m.wt[:, 0, :], v(5), v(1), ALU.mult))
            link(dve.tensor_tensor(m.wt[:, 1, :], m.wt[:, 0, :], v(2), ALU.mult))
            link(dve.tensor_tensor(og, og, over(C("valid"), NG), ALU.mult))
            for k, o in enumerate((o1, o2)):
                link(dve.tensor_tensor(mk[:, k].rearrange("p t (g e) -> p t g e", g=NG), over(og, EPG), across(o, 2, NG), ALU.mult))
            dve.tensor_tensor(both[:, 0:NT], mk[:, 0], mk[:, 1], ALU.add).then_inc(mask_done, 1)
            dve.wait_ge(rank_done, 1)
            link(dve.tensor_copy(rk[:], m.bank[1][:, 0:NE * NT].rearrange("p (t e) -> p t e", t=NT)))
            cnt, ov, ovb, ove = cv[0][:], cv[1][:], cv[2][:], cv[3][:]
            link(dve.tensor_copy(cnt, m.bank[1][:, NE * NT:NE * (NT + 1)]))
            b8 = big[:, 0:NE * 8].rearrange("p (e j) -> p e j", e=NE)
            link(dve.tensor_tensor(b8, over(cnt, 8), across(C("by64"), 1, NE), ALU.is_gt))
            link(dve.tensor_reduce(ov, b8, AX.X, ALU.add))
            be = big[:].rearrange("p (e j) -> p e j", e=NE)
            link(dve.tensor_tensor(be, across(ov, 1, NE), C("before").rearrange("p (e j) -> p e j", e=NE), ALU.mult))
            link(dve.tensor_reduce(ovb, be, AX.X, ALU.add))
            link(dve.tensor_tensor(ove, ovb, ov, ALU.add))
            r, e, ob, q, tau, pair = (v2(k) for k in range(6))
            each = lambda ap: across(across(ap, 1, NT), 1, 2)
            for dst, other in ((r, across(rk[:], 1, 2)), (e, each(C("ids"))), (ob, each(ovb))):
                link(dve.tensor_tensor(tmp[:], mk[:, 0:2], other, ALU.mult))
                link(dve.tensor_reduce(dst, tmp[:], AX.X, ALU.add))
            t8 = tmp[:, :, :, 0:8]
            link(dve.tensor_tensor(t8, over(r, 8), each(C("by64")), ALU.is_ge))
            link(dve.tensor_reduce(q, t8, AX.X, ALU.add))
            link(dve.scalar_tensor_tensor(r, q, -float(SLOT), r, ALU.mult, ALU.add))
            link(dve.tensor_tensor(ob, ob, q, ALU.add))
            link(dve.scalar_tensor_tensor(ob, ob, NE - 1.0, e, ALU.add, ALU.subtract))
            link(dve.tensor_scalar(q, q, 1.0, None, ALU.min))
            link(dve.tensor_tensor(ob, ob, q, ALU.mult))
            link(dve.tensor_tensor(tau, e, ob, ALU.add))
            t24 = tmp[:, :, :, 0:NPT - 1]
            link(dve.tensor_tensor(t24, over(tau, NPT - 1), each(C("evens")), ALU.is_ge))
            link(dve.tensor_reduce(pair, t24, AX.X, ALU.add))
            link(dve.scalar_tensor_tensor(q, tau, float(SLOT), r, ALU.mult, ALU.add))
            link(dve.tensor_copy(m.place[:], q))
            link(dve.scalar_tensor_tensor(tau, pair, -2.0, tau, ALU.mult, ALU.add))
            link(dve.scalar_tensor_tensor(tau, tau, float(SLOT), r, ALU.mult, ALU.add))
            dve.tensor_tensor(sa[:], each(C("iota")), over(tau, P), ALU.is_equal).then_inc(oh_done, 1)
            link(dve.tensor_tensor(ph[:], each(C("pairs")), over(pair, NPW), ALU.is_equal))
            dve.tensor_tensor(pbt[:], ph[:], across(over(C("token"), NPW), 1, 2), ALU.mult).then_inc(oh_done, 1)
            bo = big[0:1, 0:OV * NE].rearrange("p (j e) -> p j e", j=OV)
            link(dve.tensor_tensor(bo, across(ove[0:1], 1, OV), over(C("ovs")[0:1], NE), ALU.is_le))
            eo = big[0:1, 600:600 + OV]
            link(dve.tensor_reduce(eo, bo, AX.X, ALU.add))
            link(dve.tensor_scalar(eo, eo, NE - 1.0, None, ALU.min))
            link(dve.tensor_copy(m.ovexp[0:1, 0:OV], eo))
            np_ = big[0:1, 640:640 + NOVP]
            link(dve.tensor_tensor(np_, ove[0:1, NE - 1:NE].to_broadcast([1, NOVP]), C("ovpairs")[0:1], ALU.is_gt))
            link(dve.tensor_reduce(big[0:1, 660:661], np_, AX.X, ALU.add))
            link(dve.tensor_copy(m.novp[0:1, 0:1], big[0:1, 660:661]))
            dve.wait_ge(ix_done, 1)
            link(dve.tensor_copy(m.idx[:], m.bank[2][:, 0:NPT]))


class Experts:

    def __init__(self, nc, m, a):
        z = m.Z
        e = self.END = z + 2 * 12288
        self.gu = [[m.at(f"gate_up{s}{h}", z + 12288 * s + 4096 * h, [2, C8, FE]) for h in range(2)] for s in range(2)]
        self.dn = [[m.at(f"down{s}{h}", z + 12288 * s + 8192 + 2048 * h, [2, D]) for h in range(2)] for s in range(2)]
        self.rows = [m.at(f"slot_rows{s}", e + 1024 * s, [D]) for s in range(2)]
        self.xt = [m.at(f"slot_rows_t{s}", e + 2048 + 1024 * s, [C8, P]) for s in range(2)]
        self.hid = [m.at(f"hidden{s}", e + 4096 + 256 * s, [FE]) for s in range(2)]
        self.sig = [m.at(f"swish{s}", e + 4608 + 256 * s, [FE]) for s in range(2)]
        self.hidt = [m.at(f"hidden_t{s}", e + 5120 + 256 * s, [2, P]) for s in range(2)]
        self.y = [m.at(f"slot_out{s}", e + 5632 + 1024 * s, [D]) for s in range(2)]
        self.gate_up_src = [a[n].rearrange("a e (p c) f -> (a e) p c f", p=P) for n in ("w_exp_gate", "w_exp_up")]
        self.down_src = a["w_exp_down"].rearrange("a e (p k) d -> (a e) p k d", p=P)
        sems = lambda n: [nc.alloc_semaphore(name=f"expert_{n}{i}_in") for i in range(2)]
        self.gate_up_in, self.down_in = sems("gate_up"), sems("down")

    def load_gate_up(self, sp, s, ids, sem):
        for h in range(2):
            for j in range(2):
                sp.dma_start(self.gu[s][h][:, j], self.gate_up_src[j][ids[h]].rearrange("a p c f -> p (a c) f")).then_inc(sem, 16)

    def load_down(self, sp, s, ids, sem):
        for h in range(2):
            sp.dma_start(self.dn[s][h][:], self.down_src[ids[h]].rearrange("a p k d -> p (a k) d")).then_inc(sem, 16)

    def load(self, sp, s, pair, gate_up_free=None, down_free=None):
        ids = [bass.ds(pair * 2 + h, 1) for h in range(2)]
        if gate_up_free is not None:
            gate_up_free()
        self.load_gate_up(sp, s, ids, self.gate_up_in[s])
        if down_free is not None:
            down_free()
        self.load_down(sp, s, ids, self.down_in[s])


def experts(nc, m, a):
    B = m.experts
    y_out = m.slots_dram

    for over_tiles in (False, True):
        n_ = "ov_" if over_tiles else "ex_"
        S = lambda n: m.sem(n_ + n)
        gate_up_in, down_in = ([S("gate_up_in")], [S("down_in")]) if over_tiles else (B.gate_up_in, B.down_in)
        r_in = [S("rows0_in"), S("rows1_in")]
        xt_done, xt_ev, gu_done, ex_done, hid_done = S("rows_turned"), S("rows_t_stored"), S("gate_up"), S("exped"), S("hidden")
        ht_done, ht_ev, y_done, y_ev, y_out_s = S("hidden_turned"), S("hidden_t_stored"), S("down"), S("out_copied"), S("out_written")
        ch, y_ev2 = S("swish_chain"), S("out_copied2")
        four = lambda ap: ap.rearrange("p (c n) -> p c n", c=4)

        def turn_rows(pe, n, s, use):
            pe.wait_ge(r_in[s], use * 16 + 16)
            pe.wait_ge(xt_ev, n * 2 + 1)
            xr = B.rows[s][:].rearrange("p (d c) -> p d c", c=C8)
            for j in range(2):
                for c in range(4):
                    last = pe.transpose(m.bank[j][:, c * P:(c + 1) * P], xr[:, :, 4 * j + c], m.ident[:, :])
                last.then_inc(xt_done, 1)

        def gate_up(pe, n, s, use):
            pe.wait_ge(gate_up_in[s], use * 64 + 64)
            pe.wait_ge(xt_ev, n * 2 + 2 + 1)
            pe.wait_ge(hid_done, n + 1)
            for c in range(C8):
                for h in range(2):
                    last = pe.matmul(m.bank[2][64 * h:64 * h + 64, :], B.xt[s][:, c, 64 * h:64 * h + 64],
                                     B.gu[s][h][:, :, c, :], start=(c == 0), stop=(c == C8 - 1), skip_group_check=True)
            last.then_inc(gu_done, 1)

        def down(pe, n, s, use):
            pe.wait_ge(hid_done, n + 2)
            for k in range(2):
                last = pe.transpose(m.bank[3][:, k * P:(k + 1) * P],
                                    B.hid[s][:].rearrange("p (f k) -> p f k", k=2)[:, :, k], m.ident[:, :])
            last.then_inc(ht_done, 1)
            pe.wait_ge(down_in[s], use * 32 + 32)
            pe.wait_ge(ht_ev, n + 1)
            pe.wait_ge(y_ev, n + 1)
            pe.wait_ge(y_ev2, n + 1)
            for j in range(2):
                for k in range(2):
                    for h in range(2):
                        last = pe.matmul(m.bank[4 + j][64 * h:64 * h + 64, :], B.hidt[s][:, k, 64 * h:64 * h + 64],
                                         B.dn[s][h][:, k, 512 * j:512 * j + 512], start=(k == 0), stop=(k == 1),
                                         skip_group_check=True)
            last.then_inc(y_done, 1)

        def act_pair(act, n, s, dst):
            act.wait_ge(gu_done, n + 2)
            act.wait_ge(hid_done, n + 1)
            act.activation(B.sig[s][:], m.bank[2][:, 0:FE], ACT.Exp, scale=-1.0).then_inc(ex_done, 1)
            act.wait_ge(ht_done, n + 1)
            act.wait_ge(y_done, n + 1)
            act.activation(B.hidt[s][:], m.bank[3][:, 0:2 * P].rearrange("p (k n) -> p k n", k=2), ACT.Copy).then_inc(ht_ev, 1)
            act.wait_ge(y_done, n + 2)
            act.wait_ge(y_out_s, n * 16 + 16)
            act.activation(B.y[s][:, 0:512], m.bank[4][:], ACT.Copy).then_inc(y_ev, 1)
            act.wait_ge(y_ev, n + 2)
            act.wait_ge(y_ev2, n + 2)
            act.dma_start(dst, B.y[s][:]).then_inc(y_out_s, 16)

        def store_rows(dve, n, s):
            for j in range(2):
                dve.wait_ge(xt_done, n * 2 + 1 + j)
                dve.wait_ge(gu_done, n + 1)
                dve.tensor_tensor(B.xt[s][:, 4 * j:4 * j + 4, :], four(m.bank[j][:]),
                                  over(m.g_moe[:, 4 * j:4 * j + 4], P), ALU.mult).then_inc(xt_ev, 1)

        def swish(dve, n, s):
            dve.wait_ge(ex_done, n + 1)
            g = B.sig[s][:]
            dve.tensor_scalar(g, g, 1.0, None, ALU.add).then_inc(ch, 1)
            dve.wait_ge(ch, n * 3 + 1)
            dve.reciprocal(g, g).then_inc(ch, 1)
            dve.wait_ge(ch, n * 3 + 2)
            dve.tensor_tensor(g, g, m.bank[2][:, 0:FE], ALU.mult).then_inc(ch, 1)
            dve.wait_ge(ch, n * 3 + 3)
            dve.tensor_tensor(B.hid[s][:], g, m.bank[2][:, FE:2 * FE], ALU.mult).then_inc(hid_done, 1)

        def store_out(dve, n, s):
            dve.wait_ge(y_done, n + 2)
            dve.wait_ge(y_out_s, n * 16 + 16)
            dve.tensor_copy(B.y[s][:, 512:], m.bank[5][:]).then_inc(y_ev2, 1)

        def credit(eng, **of):
            for sem in {"pe": (gu_done, y_done), "dve": (xt_ev, hid_done, y_ev2), "act": (y_ev,)}[of["on"]]:
                eng.sem_inc(sem, 1)
            if of["on"] == "act":
                eng.sem_inc(y_out_s, 16)

        if not over_tiles:
            with nc.Block() as block:
                @block.sync
                def _(sp):
                    with sp.Fori(0, NPAIR // 2 - 1) as i:
                        for s in range(2):
                            B.load(sp, s, i * 2 + (2 + s), lambda: sp.wait_ge(gu_done, i * 2 + s + 2),
                                   lambda: sp.wait_ge(y_done, i * 2 + s + 2))

                @block.gpsimd
                def _(pool):
                    for n in range(NPAIR):
                        if n >= 2:
                            pool.wait_ge(xt_done, 2 * n - 2)
                        pool.indirect_dma_start(B.rows[n % 2][:], None, m.rows_dram,
                                                bass.IndirectOffsetOnAxis(m.idx[:, n:n + 1], 0)).then_inc(r_in[n % 2], 16)

                @block.tensor
                def _(pe):
                    credit(pe, on="pe")
                    turn_rows(pe, 0, 0, 0)
                    with pe.Fori(0, NPAIR // 2 - 1) as i:
                        for s in range(2):
                            gate_up(pe, i * 2 + s, s, i)
                            turn_rows(pe, i * 2 + (s + 1), 1 - s, i + s)
                            down(pe, i * 2 + s, s, i)
                    use = NPAIR // 2 - 1
                    gate_up(pe, NPAIR - 2, 0, use)
                    turn_rows(pe, NPAIR - 1, 1, use)
                    down(pe, NPAIR - 2, 0, use)
                    gate_up(pe, NPAIR - 1, 1, use)
                    down(pe, NPAIR - 1, 1, use)

                @block.scalar
                def _(act):
                    credit(act, on="act")
                    with act.Fori(0, NPAIR // 2) as i:
                        for s in range(2):
                            act_pair(act, i * 2 + s, s, y_out[bass.ds((i * 2 + s) * P, P), :])
                    act.wait_ge(y_out_s, 16 * NPAIR + 16)

                @block.vector
                def _(dve):
                    credit(dve, on="dve")
                    store_rows(dve, 0, 0)
                    with dve.Fori(0, NPAIR // 2 - 1) as i:
                        for s in range(2):
                            swish(dve, i * 2 + s, s)
                            store_rows(dve, i * 2 + (s + 1), 1 - s)
                            store_out(dve, i * 2 + s, s)
                    swish(dve, NPAIR - 2, 0)
                    store_rows(dve, NPAIR - 1, 1)
                    store_out(dve, NPAIR - 2, 0)
                    swish(dve, NPAIR - 1, 1)
                    store_out(dve, NPAIR - 1, 1)
        else:
            with nc.Block() as block:
                @block.sync
                def _(sp):
                    n = sp.value_load(m.novp[0:1, 0:1], min_val=0, max_val=NOVP)
                    with sp.If(n > 0):
                        for j in range(NOVP):
                            with sp.If(n > j):
                                if j:
                                    sp.wait_ge(y_done, j + 1)
                                ids = [bass.ds(sp.value_load(m.ovexp[0:1, 2 * j + h:2 * j + h + 1], min_val=0, max_val=NE - 1), 1)
                                       for h in range(2)]
                                B.load_gate_up(sp, 0, ids, gate_up_in[0])
                                B.load_down(sp, 0, ids, down_in[0])
                            with sp.Else():
                                pass
                    with sp.Else():
                        pass

                @block.gpsimd
                def _(pool):
                    n = pool.value_load(m.novp[0:1, 0:1], min_val=0, max_val=NOVP)
                    with pool.If(n > 0):
                        for j in range(NOVP):
                            with pool.If(n > j):
                                if j:
                                    pool.wait_ge(xt_done, 2 * j)
                                pool.indirect_dma_start(B.rows[0][:], None, m.rows_dram,
                                                        bass.IndirectOffsetOnAxis(m.idx[:, NPAIR + j:NPAIR + j + 1], 0)
                                                        ).then_inc(r_in[0], 16)
                            with pool.Else():
                                pass
                    with pool.Else():
                        pass

                @block.tensor
                def _(pe):
                    credit(pe, on="pe")
                    n = pe.value_load(m.novp[0:1, 0:1], min_val=0, max_val=NOVP)
                    with pe.If(n > 0):
                        for j in range(NOVP):
                            with pe.If(n > j):
                                turn_rows(pe, j, 0, j)
                                gate_up(pe, j, 0, j)
                                down(pe, j, 0, j)
                            with pe.Else():
                                pass
                    with pe.Else():
                        pass

                @block.scalar
                def _(act):
                    credit(act, on="act")
                    n = act.value_load(m.novp[0:1, 0:1], min_val=0, max_val=NOVP)
                    with act.If(n > 0):
                        for j in range(NOVP):
                            with act.If(n > j):
                                act_pair(act, j, 0, y_out[(NPAIR + j) * P:(NPAIR + j + 1) * P, :])
                                act.wait_ge(y_out_s, 16 * (j + 2))
                            with act.Else():
                                pass
                    with act.Else():
                        pass

                @block.vector
                def _(dve):
                    credit(dve, on="dve")
                    n = dve.value_load(m.novp[0:1, 0:1], min_val=0, max_val=NOVP)
                    with dve.If(n > 0):
                        for j in range(NOVP):
                            with dve.If(n > j):
                                store_rows(dve, j, 0)
                                swish(dve, j, 0)
                                store_out(dve, j, 0)
                            with dve.Else():
                                pass
                    with dve.Else():
                        pass


def combine(nc, m, a):
    got = [[m.at(f"expert_rows{t}{k}", m.Z + 2048 * t + 1024 * k, [D]) for k in range(2)] for t in range(NT)]
    arrived, added, stores = [m.sem(f"co_rows{t}") for t in range(NT)], m.sem("co_added"), m.sem("co_stores")
    with nc.Block() as block:
        @block.gpsimd
        def _(pool):
            for t in range(NT):
                r = rows(t)
                for k in range(2):
                    pool.indirect_dma_start(got[t][k][:r], None, m.slots_dram,
                                            bass.IndirectOffsetOnAxis(m.place[:r, k, t:t + 1], 0)).then_inc(arrived[t], 16)

        @block.vector
        def _(dve):
            for t in range(NT):
                r = rows(t)
                dve.wait_ge(arrived[t], 32)
                for k in range(2):
                    dve.scalar_tensor_tensor(m.x[:r, t, :], got[t][k][:r], m.wt[:r, k, t:t + 1], m.x[:r, t, :],
                                             ALU.mult, ALU.add).then_inc(added, 1)
                    dve.wait_ge(added, 2 * t + k + 1)

        @block.sync
        def _(sp):
            yp = a["o_yp"].rearrange("a (t p) d -> p (a t) d", p=P)
            for t in range(NT):
                sp.wait_ge(added, 2 * t + 2)
                if t < NT - 1:
                    sp.dma_start(yp[:, t, :], m.x[:, t, :]).then_inc(stores, 16)
                else:
                    sp.dma_start(a["o_ys"].rearrange("b i d -> (b i) d"), m.x[:NS, t, :]).then_inc(stores, 16)
            sp.wait_ge(stores, 16 * NT)


def trunk_step(nc, a):
    with ExitStack() as ctx:
        m = Plan(nc, ctx)
        m.z = [m.at(f"z{i}", m.Z + 2560 * i, [NT, RW]) for i in range(7)]
        m.ident = m.keep("ident", [P])
        m.scr = m.keep("scr", [1024])
        m.g_mix, m.g_cross, m.g_moe, m.g_mem = (m.keep(n, [C8]) for n in ("g_mix", "g_cross", "g_moe", "g_mem"))
        m.g_qk = [m.keep("g_q", [HD]), m.keep("g_k", [HD])]
        m.g_ret = m.keep("g_ret", [RW])
        m.g_q_mem, m.g_k_mem = m.keep("g_q_mem", [MD]), m.keep("g_k_mem", [MD])
        m.wk, m.wks, m.decay_chunk, m.decay_steps, m.bmask = (m.keep(n, [w]) for n, w in (("wk", H), ("wks", H), ("gc", NP), ("gcs", NP), ("bmask", NB)))
        m.neghalf = m.keep("neghalf", [8])
        m.stat = m.keep("stat", [32])
        m.qms, m.qrs = m.keep("head_sums", [80]), m.keep("head_rstd", [80])
        m.gnm, m.gnv, m.gnr = m.keep("gn_mean", [H]), m.keep("gn_var", [H]), m.keep("gn_rstd", [H])
        m.amx, m.asum, m.wmx = m.keep("att_max", [32]), m.keep("att_sum", [32]), m.keep("win_stat", [4])
        m.state = m.keep("state", [NP, HD])
        m.wt = m.keep("route_w", [2, NT])
        m.place, m.idx = m.keep("place", [2, NT], U32), m.keep("slot_token", [NPT], U32)
        m.ovexp, m.novp = m.keep("overflow_expert", [OV], I32), m.keep("overflow_pairs", [1], I32)
        m.rows_dram = nc.dram_tensor("moe_rows_dram", (T, D), F32).ap()
        m.slots_dram = nc.dram_tensor("slot_out_dram", (NPT * P, D), F32).ap()
        chunks = lambda n: a[n].rearrange("a (p c) -> p (a c)", p=P)
        wide = lambda n: a[n].partition_broadcast(P).rearrange("p a n -> p (a n)")
        m.constant_loads = [
            (m.ident[:], a["c_ident"]), (m.g_mix[:], chunks("g_mix")), (m.g_cross[:], chunks("g_cross")),
            (m.g_moe[:], chunks("g_moe")), (m.g_mem[:], chunks("g_mem")), (m.g_qk[0][:], wide("g_q_att")),
            (m.g_qk[1][:], wide("g_k_att")), (m.g_ret[:], wide("g_ret_out")), (m.g_q_mem[:], wide("g_q_mem")),
            (m.g_k_mem[:], wide("g_k_mem")), (m.wk[:], a["c_wk"]), (m.wks[:], a["c_wks"]), (m.decay_chunk[:], a["c_gc"]),
            (m.decay_steps[:], a["c_gcs"]), (m.bmask[:], a["c_bmask"])]
        m.rows_in = [nc.alloc_semaphore(name=f"token_rows{t}_in") for t in range(NT)]
        m.first_in = nc.alloc_semaphore(name="first_constants_in")
        m.constants_in = nc.alloc_semaphore(name="constants_in")
        halves = lambda n, r: [a[n].rearrange(r, p=P)[:, :, 512 * j:512 * j + 512] for j in range(2)]
        by_p, by_c = "a (p c) n -> p (a c) n", "a (c p) n -> p (a c) n"
        w_in = a["w_in"].rearrange(by_p, p=P)
        w_in = [w_in[:, :, 512 * j:512 * j + 512] for j in (4, 5, 3, 0, 1, 2, 6)]
        low, high = (m.W, m.W + 4096), (m.WH + 4096, m.WH)
        m.w_in = Weights(nc, m, "in", w_in, low, (m.WH, m.WH + 4096))
        m.w_o = Weights(nc, m, "wo", halves("w_o", by_c), high, low)
        m.w_mem = Weights(nc, m, "mem", halves("w_mk", by_p) + halves("w_mv", by_p), high, low)
        m.w_mq = Weights(nc, m, "cross", halves("w_mq", by_p), high, low)
        m.w_mo = Weights(nc, m, "back", halves("w_mo", by_c), (m.Z, m.Z + 4096), (m.WH, m.WH + 4096))
        m.mem_rows = m.at("mem_rows", m.Z + 15872, [2, D])
        m.windows = Windows(m, a)
        m.experts = Experts(nc, m, a)
        stages = (load_constants, project_in, mix_prompt, mix_windows, project_out, project_memory, project_cross,
                  cross_attend, project_back, route, experts, combine)
        for stage in stages:
            stage(nc, m, a)
            if stage in (mix_windows, project_back):
                m.free_sems()


def constants():
    f = np.float32
    i, j = np.arange(P), np.arange(P)
    gamma = 1.0 - 2.0 ** (-5.0 - np.arange(H))
    slope = 2.0 ** (-8.0 * np.arange(1, H + 1) / H)

    def bias(d, window_ok):
        n = sum(((d >= 0) & (d % dil == 0) & (d <= win)).astype(int) for win, dil in PATTERNS)
        n = n * window_ok
        return np.where(n > 0, np.log(np.maximum(n, 1)), 0.0), n > 0

    c = {}
    c["c_ident"] = np.eye(P)
    c["c_tri"] = (i[:, None] < j[None, :])
    d = i[:, None] + (512 - P) - np.arange(512)[None, :]
    logn, ok = bias(d, 1)
    c["c_tab"] = np.stack([np.where(ok, logn - s * d, NEG) for s in slope], axis=1)
    rel = i[None, :] - j[:, None]
    c["c_dm"] = np.stack([np.where(rel >= 0, HD ** -0.5 * g ** np.maximum(rel, 0), 0) for g in gamma], axis=1)
    t = np.arange(NS)
    rel = (t[None, :] - t[:, None])
    same = (t[None, :] // LS == t[:, None] // LS) & (rel >= 0)
    dms = np.zeros((P, H, NS))
    dms[:NS] = np.stack([np.where(same, HD ** -0.5 * g ** np.maximum(rel, 0), 0) for g in gamma], axis=1)
    c["c_dms"] = dms[:NS]
    by_pair = np.stack([np.repeat(gamma[2 * q:2 * q + 2], HD) for q in range(NP)], axis=1)
    c["c_wq"] = (by_pair[:, :, None] ** (i[None, None, :] + 1)).reshape(P, -1)
    c["c_wqs"] = (by_pair[:, :, None] ** (t[None, None, :] % LS + 1)).reshape(P, -1)
    c["c_gc"], c["c_gcs"] = by_pair ** P, by_pair ** LS
    c["c_wk"] = HD ** -0.5 * gamma[None, :] ** (P - 1 - j[:, None])
    c["c_wks"] = HD ** -0.5 * gamma[None, :] ** (LS - 1 - j[:, None] % LS)
    c["c_bmask"] = (j[:, None] // LS == np.arange(NB)[None, :])
    r = np.arange(FAR)
    far = 16 * (r // LS) + r % LS
    near = WBUF - NEAR + 4 * np.arange(P)[None, :] + np.arange(NEAR // P)[:, None]
    key = np.concatenate([far, near.reshape(-1), WBUF + np.arange(2 * NS - LS) - (NS - LS)])
    own = np.concatenate([np.ones(KC * P), (key[KC * P:] >= WBUF) & (key[KC * P:] < WBUF + LS)])
    tab = np.zeros((P, len(key)))
    for h in range(H):
        for s in range(LS):
            d = WBUF + s - key
            logn, ok = bias(d, own)
            tab[32 * (h // 2) + 8 * (h % 2) + s] = np.where(ok, logn - slope[h] * d, NEG)
    c["c_btab"] = tab
    route = np.zeros((P, NCONST))
    put = lambda n, x: route.__setitem__((slice(None), CONST[n]), x)
    put("iota", np.arange(P))
    put("pairs", np.arange(NPW))
    put("key4", NG - np.arange(NG))
    put("key8", EPG - np.arange(EPG))
    put("by64", SLOT * np.arange(1, 9))
    put("ids", np.arange(NE))
    put("evens", 2 * np.arange(1, NPT))
    put("ovs", np.arange(OV))
    put("ovpairs", 2 * np.arange(NOVP))
    tok = np.arange(NT)[None, :] * P + i[:, None]
    put("valid", tok < T)
    put("token", tok * (tok < T))
    e = np.arange(NE)
    put("before", (e[None, :] < e[:, None]).reshape(-1)[None, :])
    c["c_route"] = route
    return {k: np.ascontiguousarray(x, dtype=f) for k, x in c.items()}


_INS = ["x_prompt", "x_sample", "mem_prompt", "state_ret", "cache_win_k", "cache_win_v", "cache_mem_k", "cache_mem_v",
        "g_mix", "w_in", "g_ret_out", "g_q_att", "g_k_att", "w_o", "g_cross", "g_mem", "w_mq", "w_mk", "w_mv",
        "g_q_mem", "g_k_mem", "w_mo", "g_moe", "w_router_group", "b_router_group", "w_router_expert",
        "b_router_expert", "w_exp_gate", "w_exp_up", "w_exp_down"]
_OUTS = [("o_yp", (1, SEQ, D)), ("o_ys", (NB, LS, D)), ("o_rp", (1, 1, H, HD, HD)), ("o_wkp", (1, 1, SEQ, H, HD)),
         ("o_wvp", (1, 1, SEQ, H, HD)), ("o_mk", (1, 1, MEM, MH, MD)), ("o_mv", (1, 1, MEM, MH, MD)),
         ("o_rs", (1, NB, H, HD, HD)), ("o_wks", (1, NB, LS, H, HD)), ("o_wvs", (1, NB, LS, H, HD))]


def kernel(**inputs):
    import concourse.bacc as bacc
    from concourse.bass_utils import run_bass_kernel_spmd

    nc = bacc.Bacc("TRN2", target_bir_lowering=False, num_devices=1)
    arrays, a = {}, {}
    for name, x in [*((n, np.ascontiguousarray(inputs[n])) for n in _INS), *constants().items()]:
        arrays[name] = x
        a[name] = nc.dram_tensor(name, x.shape, F32, kind="ExternalInput").ap()
    for name, shape in _OUTS:
        a[name] = nc.dram_tensor(name, shape, F32, kind="ExternalOutput").ap()
    trunk_step(nc, a)
    got = run_bass_kernel_spmd(nc, [arrays], core_ids=[0]).results[0]
    return tuple(got[name] for name, _ in _OUTS)
```
